# Optimizing a Trainium2 kernel written in Bass

```python
import jax
import jax.numpy as jnp
from jax import lax
import numpy as np
import math

D_MODEL = 1024
BATCH = 1
SEQ = 256
DEPTH = 2

CTX_LEN = 256
GRID_W = 64
CONV_DIM = 512
CONV_K = 31
NA_HEADS = 8
HEAD_DIM = 64
NA_DIM = NA_HEADS * HEAD_DIM
NA_KH_MAX = 8
NA_KW = 16
ROPE_THETA = 10000.0
FFN_DIM = 2816
FFN_CONV_K = 3
N_BRANCH = 2
EPS = 1e-6
GLU_END = 2 * CONV_DIM
QKV_END = GLU_END + 3 * NA_DIM
IN_DIM = QKV_END + N_BRANCH * D_MODEL


def rmsnorm(x, g):
    xf = x.astype(jnp.float32)
    y = xf * lax.rsqrt(jnp.mean(xf * xf, axis=-1, keepdims=True) + EPS)
    return (y * g.astype(jnp.float32)).astype(x.dtype)

def layernorm(x, g, b):
    xf = x.astype(jnp.float32)
    mu = jnp.mean(xf, axis=-1, keepdims=True)
    var = jnp.mean(jnp.square(xf - mu), axis=-1, keepdims=True)
    y = (xf - mu) * lax.rsqrt(var + EPS)
    return (y * g.astype(jnp.float32) + b.astype(jnp.float32)).astype(x.dtype)

def modulate(h, shift, scale):
    return h * (1 + scale) + shift

def dwconv1d(x, w, b):
    k, ch = w.shape
    y = lax.conv_general_dilated(
        x, w.astype(x.dtype)[:, None, :], window_strides=(1,),
        padding=[(k // 2, k // 2)],
        dimension_numbers=("NWC", "WIO", "NWC"),
        feature_group_count=ch)
    return y + b

def split_heads(t):
    b, l, _ = t.shape
    return t.reshape(b, l, NA_HEADS, HEAD_DIM).transpose(0, 2, 1, 3)

def merge_heads(t):
    b, h, l, d = t.shape
    return t.transpose(0, 2, 1, 3).reshape(b, l, h * d)

def rope_2d(x, pos_row, pos_col):
    half = HEAD_DIM // 2
    inv_freq = ROPE_THETA ** (-jnp.arange(0, half, 2, dtype=jnp.float32) / half)

    def rot(xa, pos):
        ang = pos[:, None] * inv_freq[None, :]
        cos, sin = jnp.cos(ang), jnp.sin(ang)
        x1, x2 = jnp.split(xa.astype(jnp.float32), 2, axis=-1)
        return jnp.concatenate([x1 * cos - x2 * sin, x1 * sin + x2 * cos], axis=-1)

    out = jnp.concatenate([rot(x[..., :half], pos_row), rot(x[..., half:], pos_col)], axis=-1)
    return out.astype(x.dtype)

def conv_branch(p_glu, dw, dw_b, ln_g, ln_b, w_o):
    a, g = jnp.split(p_glu, 2, axis=-1)
    u = a * jax.nn.sigmoid(g)
    u = dwconv1d(u, dw, dw_b)
    u = jax.nn.silu(layernorm(u, ln_g, ln_b))
    return u @ w_o

def neighbourhood_attention(q, k, v, k_ctx, v_ctx, rpb):
    b, h, l, dh = q.shape
    rows = l // GRID_W
    kh = min(NA_KH_MAX, rows)
    n_win = kh * NA_KW
    qg = q.reshape(b, h, rows, GRID_W, dh)
    kg = k.reshape(b, h, rows, GRID_W, dh)
    vg = v.reshape(b, h, rows, GRID_W, dh)
    cols = jnp.arange(GRID_W)
    col_start = jnp.clip(cols - NA_KW // 2, 0, GRID_W - NA_KW)
    col_idx = col_start[:, None] + jnp.arange(NA_KW)[None, :]
    dc_idx = col_idx - cols[:, None] + (NA_KW - 1)
    scale = HEAD_DIM ** -0.5

    def row_block(r):
        row_start = jnp.clip(r - kh // 2, 0, rows - kh)
        q_r = lax.dynamic_index_in_dim(qg, r, axis=2, keepdims=False)
        k_band = lax.dynamic_slice_in_dim(kg, row_start, kh, axis=2)
        v_band = lax.dynamic_slice_in_dim(vg, row_start, kh, axis=2)
        k_win = k_band[:, :, :, col_idx]
        v_win = v_band[:, :, :, col_idx]
        s_win = jnp.einsum("bhqd,bhiqjd->bhqij", q_r, k_win,
                           preferred_element_type=jnp.float32) * scale
        dr_idx = row_start + jnp.arange(kh) - r + (NA_KH_MAX - 1)
        bias = rpb[:, dr_idx[None, :, None], dc_idx[:, None, :]]
        s_win = s_win + bias[None].astype(jnp.float32)
        s_ctx = jnp.einsum("bhqd,bhcd->bhqc", q_r, k_ctx,
                           preferred_element_type=jnp.float32) * scale
        s = jnp.concatenate([s_win.reshape(b, h, GRID_W, n_win), s_ctx], axis=-1)
        p = jax.nn.softmax(s, axis=-1).astype(v.dtype)
        p_win = p[..., :n_win].reshape(b, h, GRID_W, kh, NA_KW)
        p_ctx = p[..., n_win:]
        return (jnp.einsum("bhqij,bhiqjd->bhqd", p_win, v_win)
                + jnp.einsum("bhqc,bhcd->bhqd", p_ctx, v_ctx))

    out = lax.map(row_block, jnp.arange(rows))
    return out.transpose(1, 2, 0, 3, 4).reshape(b, h, l, dh)

def context_attention(q, k, v):
    s = jnp.einsum("bhqd,bhkd->bhqk", q, k, preferred_element_type=jnp.float32) * (HEAD_DIM ** -0.5)
    p = jax.nn.softmax(s, axis=-1).astype(v.dtype)
    return jnp.einsum("bhqk,bhkd->bhqd", p, v)

def gated_merge(p_gate, y_conv, y_attn, w_o):
    g_conv, g_attn = jnp.split(jax.nn.sigmoid(p_gate), 2, axis=-1)
    return (g_conv * y_conv + g_attn * y_attn) @ w_o

def conv_ffn(h, w_up, dw, dw_b, w_down):
    u = dwconv1d(h @ w_up, dw, dw_b)
    a, g = jnp.split(u, 2, axis=-1)
    return (jax.nn.silu(g) * a) @ w_down

def first_inputs(seed: int = 0) -> dict:
    key = jax.random.key(seed)
    ks = jax.random.split(key, 24)
    n = jax.random.normal
    f32 = jnp.float32
    D = D_MODEL
    return {
        "x": n(ks[0], (BATCH, SEQ, D), f32),
        "c": n(ks[1], (BATCH, D), f32),
        "ctx": n(ks[2], (BATCH, CTX_LEN, D), f32),
        "c_ctx": n(ks[3], (D,), f32),
        "w_ada": n(ks[4], (DEPTH, D, 6 * D), f32) * (0.5 * D ** -0.5),
        "b_ada": n(ks[5], (DEPTH, 6 * D), f32) * 0.02,
        "norm1_g": 1.0 + 0.02 * n(ks[6], (DEPTH, D), f32),
        "w_in": n(ks[7], (DEPTH, D, IN_DIM), f32) * D ** -0.5,
        "conv_dw": n(ks[8], (DEPTH, CONV_K, CONV_DIM), f32) * CONV_K ** -0.5,
        "conv_dw_b": n(ks[9], (DEPTH, CONV_DIM), f32) * 0.02,
        "conv_ln_g": 1.0 + 0.02 * n(ks[10], (DEPTH, CONV_DIM), f32),
        "conv_ln_b": n(ks[11], (DEPTH, CONV_DIM), f32) * 0.02,
        "w_conv_out": n(ks[12], (DEPTH, CONV_DIM, D), f32) * CONV_DIM ** -0.5,
        "na_rpb": n(ks[13], (DEPTH, NA_HEADS, 2 * NA_KH_MAX - 1, 2 * NA_KW - 1), f32) * 0.1,
        "w_na_out": n(ks[14], (DEPTH, NA_DIM, D), f32) * NA_DIM ** -0.5,
        "w_out": n(ks[15], (DEPTH, D, D), f32) * D ** -0.5,
        "norm2_g": 1.0 + 0.02 * n(ks[16], (DEPTH, D), f32),
        "w_up": n(ks[17], (DEPTH, D, 2 * FFN_DIM), f32) * D ** -0.5,
        "ffn_dw": n(ks[18], (DEPTH, FFN_CONV_K, 2 * FFN_DIM), f32) * FFN_CONV_K ** -0.5,
        "ffn_dw_b": n(ks[19], (DEPTH, 2 * FFN_DIM), f32) * 0.02,
        "w_down": n(ks[20], (DEPTH, FFN_DIM, D), f32) * FFN_DIM ** -0.5,
        "final_norm_g": 1.0 + 0.02 * n(ks[21], (D,), f32),
    }

def first_block(x, c, ctx, c_ctx, w_ada, b_ada, norm1_g, w_in, conv_dw, conv_dw_b, conv_ln_g,
              conv_ln_b, w_conv_out, na_rpb, w_na_out, w_out, norm2_g, w_up, ffn_dw, ffn_dw_b,
              w_down, final_norm_g):
    L = x.shape[1]
    t = jnp.arange(L)
    pos_row = (t // GRID_W).astype(jnp.float32)
    pos_col = (t % GRID_W).astype(jnp.float32)
    xc = ctx
    s_lat = jax.nn.silu(c)
    s_ctx = jax.nn.silu(c_ctx)
    for l in range(DEPTH):
        last = l == DEPTH - 1
        mod = (s_lat @ w_ada[l] + b_ada[l])[:, None, :]
        sh1, sc1, g1, sh2, sc2, g2 = jnp.split(mod, 6, axis=-1)
        mod_c = s_ctx @ w_ada[l] + b_ada[l]
        csh1, csc1, cg1, csh2, csc2, cg2 = jnp.split(mod_c, 6, axis=-1)

        h = modulate(rmsnorm(x, norm1_g[l]), sh1, sc1)
        hc = modulate(rmsnorm(xc, norm1_g[l]), csh1, csc1)
        p = h @ w_in[l]
        if last:
            kv_c = hc @ w_in[l][:, GLU_END + NA_DIM:QKV_END]
            k_c, v_c = (split_heads(u) for u in jnp.split(kv_c, 2, axis=-1))
        else:
            pc = hc @ w_in[l]
            q_c, k_c, v_c = (split_heads(u) for u in jnp.split(pc[..., GLU_END:QKV_END], 3, axis=-1))

        q, k, v = (split_heads(u) for u in jnp.split(p[..., GLU_END:QKV_END], 3, axis=-1))
        q = rope_2d(q, pos_row, pos_col)
        k = rope_2d(k, pos_row, pos_col)
        y_conv = conv_branch(p[..., :GLU_END], conv_dw[l], conv_dw_b[l], conv_ln_g[l],
                             conv_ln_b[l], w_conv_out[l])
        y_attn = merge_heads(neighbourhood_attention(q, k, v, k_c, v_c, na_rpb[l])) @ w_na_out[l]
        x = x + g1 * gated_merge(p[..., QKV_END:], y_conv, y_attn, w_out[l])

        h2 = modulate(rmsnorm(x, norm2_g[l]), sh2, sc2)
        x = x + g2 * conv_ffn(h2, w_up[l], ffn_dw[l], ffn_dw_b[l], w_down[l])

        if not last:
            yc_conv = conv_branch(pc[..., :GLU_END], conv_dw[l], conv_dw_b[l], conv_ln_g[l],
                                  conv_ln_b[l], w_conv_out[l])
            yc_attn = merge_heads(context_attention(q_c, k_c, v_c)) @ w_na_out[l]
            xc = xc + cg1 * gated_merge(pc[..., QKV_END:], yc_conv, yc_attn, w_out[l])
            hc2 = modulate(rmsnorm(xc, norm2_g[l]), csh2, csc2)
            xc = xc + cg2 * conv_ffn(hc2, w_up[l], ffn_dw[l], ffn_dw_b[l], w_down[l])
    return rmsnorm(x, final_norm_g)


N_META = 16
A_HEAD_DIM = 64
A_W = D_MODEL // 2
A_HEADS = A_W // A_HEAD_DIM
IDX_HEADS = 8
IDX_DIM = 64
TOPK_MAX = 256
B_HEAD_DIM = 64
B_HALF = B_HEAD_DIM // 2
B_W = D_MODEL // 4
B_HEADS = B_W // B_HEAD_DIM
C_HEAD_DIM = 64
C_W = D_MODEL // 4
C_HEADS = C_W // C_HEAD_DIM
RET_CHUNK = 128
ROPE_BASE = 10000.0
REL_BUCKETS = 32
REL_MAX_DIST = 128
D_FF = 4 * D_MODEL
Q_BLOCK = 128
IN_SIZES = (A_W, A_W, A_W, IDX_HEADS * IDX_DIM, IDX_DIM, IDX_HEADS, B_W, B_W, B_W, C_W, C_W, C_W, C_W)
IN_COLS = sum(IN_SIZES)


def _split_points():
    pts, acc = [], 0
    for s in IN_SIZES[:-1]:
        acc += s
        pts.append(acc)
    return pts

def rmsnorm_2(x, g):
    xf = x.astype(jnp.float32)
    y = xf * lax.rsqrt(jnp.mean(xf * xf, axis=-1, keepdims=True) + EPS)
    return (y * g.astype(jnp.float32)).astype(x.dtype)

def rel_bucket(dist):
    n = jnp.maximum(dist, 0)
    max_exact = REL_BUCKETS // 2
    nf = jnp.maximum(n, 1).astype(jnp.float32)
    large = max_exact + (jnp.log(nf / max_exact) / math.log(REL_MAX_DIST / max_exact)
                         * (REL_BUCKETS - max_exact)).astype(jnp.int32)
    large = jnp.minimum(large, REL_BUCKETS - 1)
    return jnp.where(n < max_exact, n, large)

def rotary(x, pos):
    d = x.shape[-1]
    inv = ROPE_BASE ** (-jnp.arange(0, d, 2, dtype=jnp.float32) / d)
    ang = pos.astype(jnp.float32)[:, None] * inv[None, :]
    cos = jnp.cos(ang)[None, :, None, :]
    sin = jnp.sin(ang)[None, :, None, :]
    xf = x.astype(jnp.float32)
    x1, x2 = xf[..., : d // 2], xf[..., d // 2:]
    return jnp.concatenate([x1 * cos - x2 * sin, x1 * sin + x2 * cos], axis=-1).astype(x.dtype)

def to_blocks(a, nblk):
    pad = nblk * Q_BLOCK - a.shape[1]
    a = jnp.pad(a, [(0, 0), (0, pad)] + [(0, 0)] * (a.ndim - 2))
    a = a.reshape((a.shape[0], nblk, Q_BLOCK) + a.shape[2:])
    return jnp.moveaxis(a, 1, 0)

def from_blocks(a, t_len):
    a = jnp.moveaxis(a, 0, 1)
    a = a.reshape((a.shape[0], -1) + a.shape[3:])
    return a[:, :t_len]

def sparse_indexer_attention(q, k, v, qi, ki, wi, bias_table, topk):
    bsz, t_len = q.shape[0], q.shape[1]
    nblk = -(-t_len // Q_BLOCK)
    key_pos = jnp.arange(t_len)
    scale = A_HEAD_DIM ** -0.5
    wi = wi.astype(jnp.float32) * (IDX_HEADS ** -0.5 * IDX_DIM ** -0.5)
    bidx = jnp.arange(bsz)[:, None]

    def body(xs):
        qb, qib, wib, start = xs
        qpos = start + jnp.arange(Q_BLOCK)
        causal = key_pos[None, :] <= qpos[:, None]
        dots = jax.nn.relu(jnp.einsum('bqhd,bsd->bqhs', qib, ki)).astype(jnp.float32)
        score = jnp.einsum('bqh,bqhs->bqs', wib, dots)
        score = jnp.where(causal[None], score, -jnp.inf)
        _, idx = lax.top_k(score, topk)
        flat = idx.reshape(bsz, Q_BLOCK * topk)
        kg = k[bidx, flat].reshape(bsz, Q_BLOCK, topk, A_HEADS, A_HEAD_DIM)
        vg = v[bidx, flat].reshape(bsz, Q_BLOCK, topk, A_HEADS, A_HEAD_DIM)
        dist = qpos[None, :, None] - idx
        bias = jnp.moveaxis(bias_table[rel_bucket(dist)], -1, 1).astype(jnp.float32)
        logits = jnp.einsum('bqhd,bqkhd->bhqk', qb, kg).astype(jnp.float32) * scale + bias
        logits = jnp.where((dist >= 0)[:, None], logits, -jnp.inf)
        p = jax.nn.softmax(logits, axis=-1).astype(v.dtype)
        return jnp.einsum('bhqk,bqkhd->bqhd', p, vg)

    starts = jnp.arange(nblk) * Q_BLOCK
    out = lax.map(body, (to_blocks(q, nblk), to_blocks(qi, nblk), to_blocks(wi, nblk), starts))
    return from_blocks(out, t_len)

def diff_attention(q, k, v, bias_table, lam):
    t_len = q.shape[1]
    nblk = -(-t_len // Q_BLOCK)
    key_pos = jnp.arange(t_len)
    scale = B_HALF ** -0.5

    def body(xs):
        qb, start = xs
        qpos = start + jnp.arange(Q_BLOCK)
        dist = qpos[:, None] - key_pos[None, :]
        bias = jnp.moveaxis(bias_table[rel_bucket(dist)], -1, 0).astype(jnp.float32)
        logits = jnp.einsum('bqhcd,bshcd->bchqs', qb, k).astype(jnp.float32) * scale + bias[None, None]
        logits = jnp.where(dist >= 0, logits, -jnp.inf)
        p = jax.nn.softmax(logits, axis=-1)
        w = (p[:, 0] - lam * p[:, 1]).astype(v.dtype)
        return jnp.einsum('bhqs,bshd->bqhd', w, v)

    starts = jnp.arange(nblk) * Q_BLOCK
    out = lax.map(body, (to_blocks(q, nblk), starts))
    return from_blocks(out, t_len)

def _retention_chunk(qc, kc, vc, state, log_gamma):
    L = qc.shape[1]
    i = jnp.arange(L, dtype=jnp.float32)
    diff = i[:, None] - i[None, :]
    dmat = jnp.where(diff >= 0, jnp.exp(log_gamma[:, None, None] * jnp.maximum(diff, 0.0)), 0.0)
    inner = jnp.einsum('bihd,bjhd->bhij', qc, kc) * dmat
    out = jnp.einsum('bhij,bjhe->bihe', inner, vc)
    q_decay = jnp.exp(log_gamma[None, :] * (i[:, None] + 1.0))
    out = out + jnp.einsum('bihd,bhde->bihe', qc, state) * q_decay[None, :, :, None]
    k_decay = jnp.exp(log_gamma[None, :] * (L - 1.0 - i[:, None]))
    state = state * jnp.exp(log_gamma * L)[None, :, None, None] + jnp.einsum('bjhd,jh,bjhe->bhde', kc, k_decay, vc)
    return out, state

def retention(q, k, v):
    bsz, t_len, nh, dk = q.shape
    dv = v.shape[-1]
    log_gamma = jnp.log1p(-jnp.exp2(-5.0 - jnp.arange(nh, dtype=jnp.float32)))
    qf = q.astype(jnp.float32)
    kf = k.astype(jnp.float32) * (dk ** -0.5)
    vf = v.astype(jnp.float32)
    state0 = jnp.zeros((bsz, nh, dk, dv), jnp.float32)
    out_meta, state = _retention_chunk(qf[:, :N_META], kf[:, :N_META], vf[:, :N_META], state0, log_gamma)
    nc = (t_len - N_META) // RET_CHUNK

    def to_chunks(a):
        return jnp.moveaxis(a[:, N_META:].reshape(bsz, nc, RET_CHUNK, nh, a.shape[-1]), 1, 0)

    def step(s, xs):
        qc, kc, vc = xs
        o, s = _retention_chunk(qc, kc, vc, s, log_gamma)
        return s, o

    _, outs = lax.scan(step, state, (to_chunks(qf), to_chunks(kf), to_chunks(vf)))
    out_real = jnp.moveaxis(outs, 0, 1).reshape(bsz, nc * RET_CHUNK, nh, dv)
    return jnp.concatenate([out_meta, out_real], axis=1)

def second_inputs(seed: int = 0) -> dict:
    key = jax.random.key(seed)
    ks = jax.random.split(key, 16)

    def nrm(k, shape, scale):
        return jax.random.normal(k, shape, jnp.float32) * scale

    return {
        'x': nrm(ks[0], (BATCH, SEQ, D_MODEL), 1.0),
        'meta': nrm(ks[1], (N_META, D_MODEL), 1.0),
        'rel_bias': nrm(ks[2], (REL_BUCKETS, A_HEADS + B_HEADS), 0.5),
        'w_in': nrm(ks[3], (DEPTH, D_MODEL, IN_COLS), D_MODEL ** -0.5),
        'norm_mix': 1.0 + nrm(ks[4], (DEPTH, D_MODEL), 0.01),
        'diff_lambda': nrm(ks[5], (DEPTH, 4, B_HALF), 0.1),
        'diff_norm': 1.0 + nrm(ks[6], (DEPTH, B_HEAD_DIM), 0.01),
        'ret_norm': 1.0 + nrm(ks[7], (DEPTH, C_W), 0.01),
        'w_out': nrm(ks[8], (DEPTH, D_MODEL, D_MODEL), 0.5 * D_MODEL ** -0.5),
        'norm_ff': 1.0 + nrm(ks[9], (DEPTH, D_MODEL), 0.01),
        'w_ff1': nrm(ks[10], (DEPTH, D_MODEL, D_FF), D_MODEL ** -0.5),
        'w_ff2': nrm(ks[11], (DEPTH, D_FF, D_MODEL), 0.5 * D_FF ** -0.5),
        'final_norm': 1.0 + nrm(ks[12], (D_MODEL,), 0.01),
    }

def second_block(x, meta, rel_bias, w_in, norm_mix, diff_lambda, diff_norm, ret_norm, w_out, norm_ff, w_ff1, w_ff2, final_norm):
    bsz, s_len, _ = x.shape
    t_len = s_len + N_META
    topk = min(TOPK_MAX, s_len // 4)
    h = jnp.concatenate([jnp.broadcast_to(meta.astype(x.dtype)[None], (bsz, N_META, D_MODEL)), x], axis=1)
    pos = jnp.arange(t_len)
    split_pts = _split_points()
    bias_a = rel_bias[:, :A_HEADS]
    bias_b = rel_bias[:, A_HEADS:]
    for l in range(DEPTH):
        u = rmsnorm_2(h, norm_mix[l])
        proj = u @ w_in[l]
        (qa, ka, va, qi, ki, wi, qb, kb, vb, qc, kc, vc, gc) = jnp.split(proj, split_pts, axis=-1)

        a_out = sparse_indexer_attention(
            qa.reshape(bsz, t_len, A_HEADS, A_HEAD_DIM),
            ka.reshape(bsz, t_len, A_HEADS, A_HEAD_DIM),
            va.reshape(bsz, t_len, A_HEADS, A_HEAD_DIM),
            qi.reshape(bsz, t_len, IDX_HEADS, IDX_DIM), ki, wi, bias_a, topk,
        ).reshape(bsz, t_len, A_W)

        lambda_init = 0.8 - 0.6 * math.exp(-0.3 * l)
        lp = diff_lambda[l].astype(jnp.float32)
        lam = jnp.exp(jnp.sum(lp[0] * lp[1])) - jnp.exp(jnp.sum(lp[2] * lp[3])) + lambda_init
        b_heads = diff_attention(
            qb.reshape(bsz, t_len, B_HEADS, 2, B_HALF),
            kb.reshape(bsz, t_len, B_HEADS, 2, B_HALF),
            vb.reshape(bsz, t_len, B_HEADS, B_HEAD_DIM), bias_b, lam,
        )
        b_out = (rmsnorm_2(b_heads, diff_norm[l]) * (1.0 - lambda_init)).reshape(bsz, t_len, B_W)

        qcr = rotary(qc.reshape(bsz, t_len, C_HEADS, C_HEAD_DIM), pos)
        kcr = rotary(kc.reshape(bsz, t_len, C_HEADS, C_HEAD_DIM), pos)
        ret = retention(qcr, kcr, vc.reshape(bsz, t_len, C_HEADS, C_HEAD_DIM)).astype(h.dtype)
        ret = rmsnorm_2(ret, ret_norm[l].reshape(C_HEADS, C_HEAD_DIM)).reshape(bsz, t_len, C_W)
        c_out = jax.nn.silu(gc) * ret

        h = h + jnp.concatenate([a_out, b_out, c_out], axis=-1) @ w_out[l]
        u = rmsnorm_2(h, norm_ff[l])
        h = h + jnp.square(jax.nn.relu(u @ w_ff1[l])) @ w_ff2[l]
    return rmsnorm_2(h, final_norm)[:, N_META:]


_first_inputs = second_inputs


def second_inputs(seed=0):
    import zlib

    import numpy as np

    out = dict(_first_inputs(seed))
    spreads = {}
    factors = {'norm_mix': 4.444,
     'diff_norm': 8.0,
     'ret_norm': 8.0,
     'norm_ff': 6.019,
     'final_norm': 5.776}
    for name, (base, spread) in spreads.items():
        noise = np.random.default_rng([zlib.crc32(name.encode()), seed]).standard_normal(out[name].shape)
        drawn = base * np.exp(spread * noise) if base else spread * noise
        out[name] = jnp.asarray(drawn.astype(out[name].dtype))
    for name, factor in factors.items():
        out[name] = (out[name] * factor).astype(out[name].dtype)
    return out


_narrow_inputs = second_inputs


def second_inputs(seed=0):

    out = dict(_narrow_inputs(seed))
    wider = {'diff_norm': 11.67, 'ret_norm': 4.11, 'norm_ff': 3.48, 'final_norm': 6.5}
    for name, times in wider.items():
        mean = out[name].mean()
        out[name] = (mean + times * (out[name] - mean)).astype(out[name].dtype)
    return out


def setup_inputs(seed=0):
    out = dict(first_inputs(seed))
    for name, value in second_inputs(seed + 1).items():
        if name != "x":
            out[name + "_2"] = value
    return out


def reference(
    x, c, ctx, c_ctx, w_ada, b_ada, norm1_g, w_in, conv_dw, conv_dw_b, conv_ln_g, conv_ln_b,
    w_conv_out, na_rpb, w_na_out, w_out, norm2_g, w_up, ffn_dw, ffn_dw_b, w_down, final_norm_g,
    meta_2, rel_bias_2, w_in_2, norm_mix_2, diff_lambda_2, diff_norm_2, ret_norm_2, w_out_2,
    norm_ff_2, w_ff1_2, w_ff2_2, final_norm_2,
):
    x = first_block(
        x, c, ctx, c_ctx, w_ada, b_ada, norm1_g, w_in, conv_dw, conv_dw_b, conv_ln_g, conv_ln_b,
        w_conv_out, na_rpb, w_na_out, w_out, norm2_g, w_up, ffn_dw, ffn_dw_b, w_down,
        final_norm_g,
    )
    return second_block(
        x, meta_2, rel_bias_2, w_in_2, norm_mix_2, diff_lambda_2, diff_norm_2, ret_norm_2,
        w_out_2, norm_ff_2, w_ff1_2, w_ff2_2, final_norm_2,
    )


_drawn_inputs = setup_inputs


def setup_inputs(seed=0):
    import zlib

    import numpy as np

    out = dict(_drawn_inputs(seed))
    spreads = {}
    factors = {'na_rpb': 4.416, 'diff_lambda_2': 3.727}
    for name, (base, spread) in spreads.items():
        noise = np.random.default_rng([zlib.crc32(name.encode()), seed]).standard_normal(out[name].shape)
        drawn = base * np.exp(spread * noise) if base else spread * noise
        out[name] = jnp.asarray(drawn.astype(out[name].dtype))
    for name, factor in factors.items():
        out[name] = (out[name] * factor).astype(out[name].dtype)
    return out
```

```python
import math
from contextlib import ExitStack

import concourse.bass as bass
import numpy as np
from concourse import mybir

F32 = mybir.dt.float32
F32R = mybir.dt.float32r
ALU = mybir.AluOpType
ACT = mybir.ActivationFunctionType
AXX = mybir.AxisListType.X

P = 128
D = 1024
DC = D // P
SEQ = 256
CTX = 256
DEPTH = 2
EPS = 1e-6
NEG = -1e30
TAKEN = -3e38

GRID_W = 64
CONV_C = 512 // P
TAPS = 31
HALO = TAPS // 2
HEADS = 8
HD = 64
QC = HEADS * HD // P
FF_C = 2816 // P
RPB_PAD = 128
T_BOTH = SEQ + CTX

META = 16
T2 = SEQ + META
TOPK = 64
A_HEADS = 8
IDX_HEADS = 8
B_HEADS = 4
C_HEADS = 4
FF2_C = 4 * D // P
N1, N2, N0 = META + P, T2, META
S1, S2, S0 = 0, N1, N1 + N2
S_ALL = N1 + N2 + N0
VLEN = 544

TILE = P * P
SLAB = 8 * P
RING = 4
ADA_SLABS = 6 * DC
GLU_SLABS = 2 * CONV_C
QKV_V_SLABS = 4
L1_SLABS = GLU_SLABS + 2 * QC + QKV_V_SLABS + 2 * DC + DC + DC + 2 * FF_C + FF_C
L2_FRONT = 23
L2_SLABS = L2_FRONT + 8 + DC + FF2_C + FF2_C
N_SLABS = DEPTH * (ADA_SLABS + L1_SLABS + L2_SLABS)

PRM1 = {}
_n = 0
for _name, _w in (("n1g", DC), ("dw", CONV_C * TAPS), ("dwb", CONV_C), ("lng", CONV_C), ("lnb", CONV_C),
                  ("n2g", DC), ("fdw", 3 * 2 * FF_C), ("fdwb", 2 * FF_C), ("bada", 6 * DC)):
    PRM1[_name] = (_n, _n + _w)
    _n += _w
PRM1_N = _n
PRM2 = {}
_n = 0
for _name, _w in (("nmix", DC), ("dnorm", 1), ("rnorm", 2), ("nff", DC)):
    PRM2[_name] = (_n, _n + _w)
    _n += _w
PRM2_N = _n
TAB = {}
_n = 0
for _name, _w in (("ident", P), ("ones_d", P), ("ones_c", P), ("ones_h", P), ("perm1", P), ("perm2", P),
                  ("sel", 2), ("cos1", SEQ), ("sin1", SEQ), ("win", GRID_W),
                  ("cos2", T2), ("sin2", T2), ("causal", N1 + N2), ("decay1", 4 * 384), ("decay0", 4 * T2),
                  ("onehot", VLEN), ("vmask", VLEN)):
    TAB[_name] = (_n, _n + _w)
    _n += _w
TAB_N = _n


def lambda_init(layer):
    return 0.8 - 0.6 * math.exp(-0.3 * layer)


def build(nc, A, out, marks):
    SAME = {"chunk": "slab_used", "up_all": "up_out", "down_done": "down_out", "ff1_all": "ff1_out"}
    seen = {}
    sems = {}
    counts = {}
    ctx = ExitStack()

    def sem(name):
        if name not in sems:
            sems[name] = ctx.enter_context(nc.semaphore(name))
            counts[name] = 0
        return sems[name]

    def done(name, key, by=1):
        s = sem(name)
        counts[name] += by
        assert (name, key) not in seen, (name, key)
        seen[name, key] = counts[name]
        return s, by

    def again(name, n):
        counts[name] += n

    def after(name, key, plus=0):
        return sem(SAME.get(name, name)), marks.get((name, key), 1) + plus

    with ctx:
        top = [16512]

        def at(name, shape, dt, offset):
            t = nc.alloc_sbuf_tensor_at(name, [P, *shape], dt, offset=offset)
            return t[(slice(None),) * (len(shape) + 1)]

        def sb(name, shape, dt=F32):
            n = int(np.prod(shape)) * 4
            t = at(name, shape, dt, top[0])
            top[0] += -(-n // 32) * 32
            assert top[0] <= nc.sbuf_usable_end, name
            return t

        bank = [ctx.enter_context(nc.psum_tensor(f"bank{i}", [P, 512], F32)) for i in range(8)]
        lin, aux = bank[0:4], bank[4:8]

        raw = sb("raw", [RING, SLAB])
        w_hi = sb("w_hi", [RING, SLAB], F32R)
        w_lo = sb("w_lo", [RING, SLAB], F32R)
        cst = sb("cst", [6 * P + 2])
        prm = sb("prm", [DEPTH, PRM1_N])
        prm2 = sb("prm2", [DEPTH, PRM2_N])
        fin_g = sb("fin_g", [2, DC])
        cvec = sb("cvec", [DC, 2])
        cth = sb("cth", [DC, 2])
        mod = sb("mod", [DEPTH, 6 * DC, 2])
        a1 = sb("a1", [DEPTH, DC, 2])
        a2 = sb("a2", [DEPTH, DC, 2])
        gh = sb("gh", [DEPTH, 2, DC, 2])
        small = sb("small", [96])
        eps = sb("eps", [8])
        sq = sb("sq", [2, 512])
        nt = sb("nt", [2, 512])
        nr = sb("nr", [2, 512])
        work = top[0]
        top[0] += 12288
        rinv = at("rinv", [512], F32, work + 10240)
        p_x = at("p_x", [2, 512], F32, work)
        p_c = at("p_c", [2, 256], F32, work + 4096)
        pt_x = at("pt_x", [4, 256], F32, work + 6144)
        pt_c = at("pt_c", [2, 256], F32, work + 10240)
        up_a = at("up_a", [2, 512], F32, work)
        up_g = at("up_g", [2, 512], F32, work + 4096)
        up_t = at("up_t", [2, 512], F32, work + 8192)
        glu_t = at("glu_t", [2, 512], F32, work)
        dn_hi = at("dn_hi", [2, 512], F32R, work)
        dn_lo = at("dn_lo", [2, 512], F32R, work + 4096)
        ada_part = at("ada_part", [2, 512], F32, work)
        p2 = at("p2", [2, S_ALL], F32, work)
        pt0 = at("pt0", [2, T2], F32, work + 3456)
        pt1 = at("pt1", [2, 384], F32, work + 5632)
        relu2 = at("relu2", [2, N1 + N2], F32, work + 8704)

        x_at = top[0]
        X = sb("X", [DC, T_BOTH])
        h_at = top[0]
        h_hi = sb("h_hi", [DC, T_BOTH], F32R)
        h_lo = sb("h_lo", [DC, T_BOTH], F32R)
        y_hi = at("y_hi", [DC, T_BOTH], F32R, h_at)
        y_lo = at("y_lo", [DC, T_BOTH], F32R, h_at + DC * T_BOTH * 4)
        g_at = top[0]
        gates = sb("gates", [2 * DC, T_BOTH])
        cs = at("cs", [DC, 32], F32, g_at)
        ffa = at("ffa", [FF_C, T_BOTH], F32, g_at)
        q_at = top[0]
        qT = sb("qT", [QC, T_BOTH])
        kT = sb("kT", [QC, T_BOTH])
        at_hi = at("at_hi", [QC, T_BOTH], F32R, q_at)
        at_lo = at("at_lo", [QC, T_BOTH], F32R, q_at + QC * T_BOTH * 4)
        V = sb("V", [4, 512])
        up_at = top[0]
        upad = sb("upad", [CONV_C, 2, SEQ + 2 * HALO])
        cv_at = top[0]
        cv = sb("cv", [CONV_C, T_BOTH])
        cv_hi = at("cv_hi", [CONV_C, T_BOTH], F32R, up_at)
        cv_lo = at("cv_lo", [CONV_C, T_BOTH], F32R, cv_at)
        biash = sb("biash", [2, 2, 256])
        tab1 = sb("tab1", [2 * SEQ + GRID_W])
        end1 = top[0]
        cos1, sin1, win = tab1[:, 0:SEQ], tab1[:, SEQ:2 * SEQ], tab1[:, 2 * SEQ:2 * SEQ + GRID_W]

        o = h_at
        u_hi = at("u_hi", [DC, T2], F32R, o)
        u_lo = at("u_lo", [DC, T2], F32R, o + DC * T2 * 4)
        H = at("H", [DC, T2], F32, o + 2 * DC * T2 * 4)
        decay0 = at("decay0", [4, T2], F32, o + 3 * DC * T2 * 4)
        assert 3 * DC * T2 * 4 + 4 * T2 * 4 <= 2 * DC * T_BOTH * 4
        tab2 = at("tab2", [2 * T2 + N1 + N2 + 4 * 384], F32, x_at)
        cos2, sin2, causal = tab2[:, 0:T2], tab2[:, T2:2 * T2], tab2[:, 2 * T2:2 * T2 + N1 + N2]
        decay1 = tab2[:, 2 * T2 + N1 + N2:].rearrange("p (h n) -> p h n", h=4)
        n_tab2 = 2 * T2 + N1 + N2 + 4 * 384
        score = at("score", [N1 + N2], F32, x_at + n_tab2 * 4)
        nsel = at("nsel", [N1 + N2], F32, x_at + (n_tab2 + N1 + N2) * 4)
        wi_w = at("wi_w", [2, DC, 8], F32R, x_at + (n_tab2 + 2 * (N1 + N2)) * 4)
        wi_r = at("wi_r", [DC, 8], F32, x_at + (n_tab2 + 2 * (N1 + N2) + 128) * 4)
        lamp = at("lamp", [4 * 32], F32, x_at + (n_tab2 + 2 * (N1 + N2) + 192) * 4)
        assert n_tab2 + 2 * (N1 + N2) + 192 + P <= DC * T_BOTH
        o = g_at
        pj = at("pj", [L2_FRONT, T2], F32, o)
        V2 = at("V2", [3, 1024], F32, o + L2_FRONT * T2 * 4)
        ff2a = at("ff2a", [FF2_C, T2], F32, o)
        o += (L2_FRONT * T2 + 3 * 1024) * 4
        assert FF2_C * T2 <= L2_FRONT * T2 + 3 * 1024
        o_hi = at("o_hi", [DC, T2], F32R, o)
        o_lo = at("o_lo", [DC, T2], F32R, o + DC * T2 * 4)
        o += 2 * DC * T2 * 4
        bias2 = at("bias2", [A_HEADS + B_HEADS, S_ALL], F32, o)
        o += (A_HEADS + B_HEADS) * S_ALL * 4
        assert o <= end1, (o, end1)
        KI, QI, QCR, KCR, QB, KB, QA, KA, GC = 0, 1, 5, 7, 9, 11, 13, 17, 21
        bc_raw = pj[:, QI:QI + 4, :]
        bc_r = pj[:, QCR:QCR + 4, :]
        vec = at("vec", [VLEN], F32, g_at)
        oneh = at("oneh", [2, VLEN], F32, g_at + VLEN * 4)
        relb = at("relb", [A_HEADS + B_HEADS], F32, g_at + 3 * VLEN * 4)

        ident = cst[:, 0:P]
        ones_d, ones_c, ones_h = (cst[:, i * P:(i + 1) * P] for i in (1, 2, 3))
        perm1, perm2, sel = cst[:, 4 * P:5 * P], cst[:, 5 * P:6 * P], cst[:, 6 * P:6 * P + 2]
        by_distance = nc.dram_tensor("bias_by_distance", (A_HEADS + B_HEADS, P, VLEN), F32).ap()
        by_offset = nc.dram_tensor("rpb_by_offset", (DEPTH, HEADS, 7, GRID_W, RPB_PAD), F32).ap()

        def par(layer, name, c=None, plus=0):
            a, b = PRM1[name]
            if c is None:
                return prm[:, layer, a:b]
            return prm[:, layer, a + c:a + c + 1] if type(plus) is int else prm[:, layer, bass.ds(a + c + plus, 1)]

        def par2(layer, name, c):
            return prm2[:, layer, PRM2[name][0] + c:PRM2[name][0] + c + 1]

        kinds = []
        first = {}
        for layer in range(DEPTH):
            first["ada", layer] = len(kinds)
            kinds += ["ada"] * ADA_SLABS
        for layer in range(DEPTH):
            first["l1", layer] = len(kinds)
            kinds += ["split"] * L1_SLABS
        for layer in range(DEPTH):
            first["l2", layer] = len(kinds)
            kinds += ["split"] * L2_SLABS
        assert len(kinds) == N_SLABS
        N_ADA = DEPTH * ADA_SLABS
        split_no = {}
        for i, k in enumerate(kinds):
            if k == "split":
                split_no[i] = len(split_no)
                assert i % RING == split_no[i] % RING
        slab_of = {q: i for i, q in split_no.items()}
        N_SPLIT = len(split_no)

        def streams(ap, layer, lo=0, hi=SEQ):
            n = 2 if layer == 0 else 1
            return ap[:, 0:n * SEQ].rearrange("p (s t) -> p s t", s=n)[:, :, lo:hi]

        def n_tok(layer):
            return T_BOTH if layer == 0 else SEQ

        def parts(layer):
            return [(s, slice(s * SEQ, (s + 1) * SEQ)) for s in range(2 if layer == 0 else 1)]

        L2_STEPS = [("slab", c) for c in range(0, QCR)] + [("wi", 0), ("index", 0)]
        L2_STEPS += [("slab", c) for c in range(QCR, QB)] + [("vals", 1)]
        L2_STEPS += [("slab", c) for c in range(QB, QA)]
        heads = [("c", h) for h in range(C_HEADS)] + [("b", h) for h in range(B_HEADS)]
        L2_STEPS += [s for c, u in zip(range(QA, QA + 8), heads) for s in (("slab", c), u)]
        L2_STEPS += [("slab", GC), ("slab", GC + 1), ("vals", 0), ("bcnorm", 0)]
        L2_STEPS += [("a", h) for h in range(A_HEADS)]
        L2_ORDER = [s for s in L2_STEPS if s[0] in ("slab", "vals")]
        L2_AT = {}
        _at = 0
        for s in L2_ORDER:
            L2_AT[s] = _at
            _at += 4 if s[0] == "vals" else 1
        assert _at == L2_FRONT + 8

        def prev_unit(kind, k):
            if k:
                return kind, k - 1
            return {"b": ("c", C_HEADS - 1), "a": ("b", B_HEADS - 1)}[kind]

        def l2_bank(step):
            return L2_AT[step] % 4

        def l2_vbank(step, tt):
            return (L2_AT[step] + tt) % 4

        block = ctx.enter_context(nc.Block())

        @block.sync
        def _(sp):
            def load(i, it=None):
                old, plus = i - RING, 0 if it is None else it * 8
                if old >= N_ADA:
                    sp.wait_ge(sem("w_lo_ready"), old - N_ADA + 1 + plus)
                elif old >= 0:
                    sp.wait_ge(sem("ada_slab_read"), old + 1 + plus)
                src = A["wstream"][i] if it is None else A["wstream"][bass.ds(i + plus, 1)].rearrange("a p n -> (a p) n")
                sp.dma_start(raw[:, i % RING, :], src).then_inc(sem(f"slab_landed{i % RING}"), 16)

            def loads(i, end):
                reps = (end - i) // 8
                with sp.Fori(0, reps) as it:
                    for b in range(8):
                        load(i + b, it)
                for j in range(i + reps * 8, end):
                    load(j)

            for i in range(RING):
                load(i)
            loads(RING, N_ADA + RING)
            loads(N_ADA + RING, N_SLABS)
            for c in range(DC):
                sp.wait_ge(*after("out_ready", c))
                sp.dma_start(out[c * P:(c + 1) * P, :], nr[:, c % 2, 0:SEQ]).then_inc(*done(f"stored{c % 2}", c, 16))
            sp.wait_ge(*after("stored0", DC - 2))
            sp.wait_ge(*after("stored1", DC - 1))

        def landed(i):
            return sem(f"slab_landed{i % RING}"), 16 * (i // RING + 1)

        @block.gpsimd
        def _(pool):
            def rest(q, it=None):
                plus = 0 if it is None else it * 8
                pool.wait_ge(sem("w_hi_ready"), q + 1 + plus)
                s = q % RING
                pool.tensor_tensor(w_lo[:, s, :], raw[:, s, :], w_hi[:, s, :].bitcast(F32), ALU.subtract)\
                    .then_inc(sem("w_lo_ready"), 1)

            reps = N_SPLIT // 8
            with pool.Fori(0, reps) as it:
                for b in range(8):
                    rest(b, it)
            for q in range(reps * 8, N_SPLIT):
                rest(q)

        @block.scalar
        def _(act):
            nxt = [0]

            def round_weights(q, it=None):
                i, s = slab_of[q], q % RING
                a, n = landed(i)
                act.wait_ge(a, n + (0 if it is None else it * (8 // RING) * 16))
                if q >= RING:
                    act.wait_ge(sem("slab_used"), q - RING + 1 + (0 if it is None else it * 8))
                act.activation(w_hi[:, s, :], raw[:, s, :], ACT.Copy).then_inc(sem("w_hi_ready"), 1)

            def ahead(i):
                while nxt[0] <= min(split_no[i] + RING - 1, N_SPLIT - 1):
                    round_weights(nxt[0])
                    nxt[0] += 1

            def copy(dst, src, **kw):
                return act.activation(dst, src, ACT.Copy, **kw)

            tb = A["tables"]
            act.dma_start(cst[:, :], tb[:, TAB["ident"][0]:TAB["sel"][1]]).then_inc(*done("const_in", 0, 16))
            act.dma_start(cvec[:, :, :], A["cvec"]).then_inc(*done("const_in", 1, 16))
            act.dma_start(X[:, :, :], A["x_in"]).then_inc(*done("x_in", 0, 16))
            act.dma_start(tab1[:, :], tb[:, TAB["cos1"][0]:TAB["win"][1]]).then_inc(*done("const_in", 2, 16))
            act.dma_start(prm[:, :, :], A["prm1"]).then_inc(*done("prm_in", 0, 16))
            act.dma_start(prm2[:, :, :], A["prm2"]).then_inc(*done("const_in", 3, 16))
            act.dma_start(fin_g[:, :, :], A["fin_g"]).then_inc(*done("const_in", 4, 16))

            for layer in range(DEPTH):
                for h in range(HEADS):
                    off = ((layer * HEADS + h) * 15 + 4) * RPB_PAD
                    src = bass.AP(A["rpb"].tensor, off, [[RPB_PAD, 7], [0, GRID_W], [1, RPB_PAD]])
                    act.dma_start(by_offset[layer, h], src).then_inc(*done("rpb_rows", (layer, h), 16))
            act.wait_ge(*after("const_in", 4))
            act.activation(cth[:, :, :], cvec[:, :, :], ACT.Tanh, scale=0.5).then_inc(*done("c_tanh", 0))

            def load_bias(layer, h):
                for t in range(2):
                    for r in range(2):
                        off = ((layer * HEADS + h) * 7 + 3 - (2 * t + r)) * GRID_W * RPB_PAD + GRID_W - 1
                        src = bass.AP(by_offset.tensor, off, [[RPB_PAD - 1, GRID_W], [GRID_W * RPB_PAD, 4], [1, GRID_W]])
                        act.dma_start(biash[r * GRID_W:(r + 1) * GRID_W, h % 2, t, :]
                                      .rearrange("p (a b) -> p a b", a=4), src)\
                            .then_inc(*done(f"bias_in{h % 2}", (layer, h, t, r), 16))

            def root(dst, mean, name, key):
                act.activation(dst, mean, ACT.Sqrt, bias=eps[:, 0:1]).then_inc(*done(name, key))

            def norm(tag, X_, T, k_ready):
                for c in range(DC):
                    if k_ready:
                        act.wait_ge(*after(*k_ready(c)))
                    if c >= 2:
                        act.wait_ge(*after("norm_summed", (tag, c - 2)))
                    act.activation(sq[:, c % 2, 0:T], X_[:, c, 0:T], ACT.Square).then_inc(*done("norm_sq", (tag, c)))
                act.wait_ge(*after("norm_summed", (tag, DC - 1)))
                root(rinv[:, 0:T], aux[0][:, 0:T], "norm_root", tag)

            def norm_round(tag, hi, T):
                for c in range(DC):
                    act.wait_ge(*after("normed", (tag, c)))
                    copy(hi[:, c, 0:T], nr[:, c % 2, 0:T]).then_inc(*done("norm_hi", (tag, c)))

            def ada():
                with act.Fori(0, DEPTH * 6) as it:
                    for b in range(2):
                        act.wait_ge(sem("ada_slab_read"), 4 * (b + 1) + it * 8)
                        copy(ada_part[:, b, :], lin[b][:, :]).then_inc(*done("ada_part_out", b))
                again("ada_part_out", 12 * DEPTH - 2)

            def network1(layer):
                T = n_tok(layer)
                first_slab = first["l1", layer]
                norm((layer, 1), X, T_BOTH, None if layer == 0 else lambda c: ("down_out", (layer - 1, c)))
                ahead(first_slab)
                norm_round((layer, 1), h_hi, T_BOTH)
                s = first_slab
                for c in range(CONV_C):
                    ahead(s)
                    act.wait_ge(*after("chunk", (layer, "glu_g", c)))
                    if c >= 2:
                        act.wait_ge(*after("glu_out", (layer, c - 2)))
                    act.activation(glu_t[:, c % 2, 0:T], lin[(2 * c) % 4][:, 0:T], ACT.Tanh, scale=0.5)\
                        .then_inc(*done("glu_tanh", (layer, c)))
                    s += 2
                for c in range(2 * QC):
                    ahead(s)
                    act.wait_ge(*after("chunk", (layer, "qk", c)))
                    Tq = T if c < QC else T_BOTH
                    dst = (qT[:, c, 0:Tq] if c < QC else kT[:, c - QC, 0:Tq])
                    copy(dst, lin[c % 4][:, 0:Tq], scale=HD ** -0.5 if c < QC else 1.0)\
                        .then_inc(*done("qk_out", (layer, c)))
                    s += 1
                ahead(s)
                ahead(s + 3)
                for tt in range(4):
                    act.wait_ge(*after("chunk", (layer, "v", tt)))
                    copy(V[:, tt, :], lin[tt][:, :]).then_inc(*done("v_out", (layer, tt)))
                s += QKV_V_SLABS
                act.wait_ge(*after("glu_out", (layer, CONV_C - 1)))
                if layer > 0:
                    act.wait_ge(*after("attn_added", (layer - 1, HEADS - 1, 1)))
                if layer == 0:
                    act.wait_ge(*after("rpb_rows", (1, HEADS - 1)))
                load_bias(layer, 0)
                load_bias(layer, 1)
                for h in range(HEADS):
                    def gate(g):
                        ahead(s + g)
                        act.wait_ge(*after("chunk", (layer, "gate", g)))
                        act.activation(gates[:, g, 0:T], lin[g % 4][:, 0:T], ACT.Tanh, scale=0.5)\
                            .then_inc(*done("gate_out", (layer, g)))
                    for t in range(2):
                        act.wait_ge(*after("attn_max", (layer, h, t)))
                        act.activation(p_x[:, t, :], aux[t][:, :], ACT.Exp, bias=small[:, t:t + 1],
                                       accum_out=small[:, 8 + t:9 + t]).then_inc(*done("attn_exp", (layer, h, t)))
                    if layer == 0:
                        for t in range(2):
                            act.wait_ge(*after("attn_max", (layer, h, 3)))
                            act.activation(p_c[:, t, :], aux[2][:, t * 256:(t + 1) * 256], ACT.Exp,
                                           bias=small[:, 2 + t:3 + t], accum_out=small[:, 10 + t:11 + t])\
                                .then_inc(*done("attn_exp", (layer, h, 2 + t)))
                    if h + 2 < HEADS:
                        load_bias(layer, h + 2)
                    gate(2 * h)
                    if h:
                        act.wait_ge(*after("attn_pv", (layer, h - 1)))
                    for t in range(2):
                        act.wait_ge(*after("attn_turned", (layer, h, t)))
                        copy(pt_x[:, :, t * P:(t + 1) * P], aux[t][:, :].rearrange("p (k q) -> p k q", k=4))\
                            .then_inc(*done("attn_pt", (layer, h, t)))
                    if layer == 0:
                        act.wait_ge(*after("attn_turned", (layer, h, 2)))
                        copy(pt_c.rearrange("p k (t q) -> p t k q", t=2),
                             aux[2][:, :].rearrange("p (t k q) -> p t k q", t=2, k=2))\
                            .then_inc(*done("attn_pt", (layer, h, 2)))
                    gate(2 * h + 1)
                    act.wait_ge(*after("attn_pv", (layer, h)))
                    r = slice((h % 2) * HD, (h % 2) * HD + HD)
                    copy(at_hi[r, h // 2, 0:T], aux[3][r, 0:T]).then_inc(*done("attn_hi", (layer, h)))
                s += 2 * DC
                for c in range(CONV_C):
                    act.wait_ge(*after("conv_centred", (layer, c)))
                    if c >= 2:
                        act.wait_ge(*after("ln_var", (layer, c - 2)))
                    act.activation(sq[:, c % 2, 0:T], cv[:, c, 0:T], ACT.Square).then_inc(*done("ln_sq", (layer, c)))
                act.wait_ge(*after("ln_var", (layer, CONV_C - 1)))
                root(rinv[:, 0:T], aux[1][:, 0:T], "ln_root", layer)
                ahead(s)
                for c in range(CONV_C):
                    act.wait_ge(*after("conv_affine", (layer, c)))
                    act.activation(nt[:, c % 2, 0:T], nr[:, c % 2, 0:T], ACT.Tanh).then_inc(*done("conv_tanh", (layer, c)))
                    act.wait_ge(*after("conv_silu", (layer, c)))
                    copy(cv_hi[:, c, 0:T], sq[:, c % 2, 0:T]).then_inc(*done("conv_hi", (layer, c)))
                for m in range(DC):
                    ahead(s)
                    act.wait_ge(*after("merged", (layer, m)))
                    copy(y_hi[:, m, 0:T], nr[:, m % 2, 0:T]).then_inc(*done("merge_hi", (layer, m)))
                    s += 1
                for m in range(DC):
                    ahead(s)
                    s += 1
                norm((layer, 2), X, T, lambda c: ("mix_out", (layer, c)))
                ahead(s)
                norm_round((layer, 2), h_hi, T)

                def up(j, b, it=None):
                    plus = 0 if it is None else it * 4
                    for w, buf in enumerate((up_a, up_g)):
                        if it is None:
                            ahead(s + 2 * j + w)
                        else:
                            round_weights(nxt[0] + 2 * b + w, it)
                        act.wait_ge(sem("slab_used"), split_no[s] + 2 * j + w + 1 + plus * 2)
                        if j >= 2 or it is not None:
                            act.wait_ge(sem("up_out"), base_up + j - 1 + plus)
                        cc = w * FF_C + j
                        wcol, bcol = par(layer, "fdw", 2 * FF_C + cc, plus), par(layer, "fdwb", cc, plus)
                        ps = lin[(2 * b + w) % 4]
                        act.activation(buf[:, b % 2, 0:T], ps[:, 0:T], ACT.Identity, bias=bcol, scale=wcol)\
                            .then_inc(*done("up_mid", (layer, j, w)))
                    act.wait_ge(sem("up_conv"), 2 * (base_up + j + 1) + plus * 2)
                    act.activation(up_t[:, b % 2, 0:T], up_g[:, b % 2, 0:T], ACT.Tanh)\
                        .then_inc(*done("up_tanh", (layer, j)))

                base_up = FF_C * layer
                for j in range(2):
                    up(j, j)
                up_first = nxt[0]
                with act.Fori(0, 5) as it:
                    for b in range(4):
                        up(2 + b, b, it)
                nxt[0] = up_first + 40
                again("up_mid", 4 * 2 * 4)
                again("up_tanh", 4 * 4)
                s += 2 * FF_C

                def down(j, b, it=None):
                    plus = 0 if it is None else it * 8
                    if it is not None or j >= 2:
                        act.wait_ge(sem("slab_used"), split_no[s] + j - 1 + plus)
                    src = ffa[:, j, 0:T] if it is None else ffa[:, bass.ds(j + plus, 1), 0:T].rearrange("p a t -> p (a t)")
                    if j == 0:
                        act.wait_ge(*after("up_all", layer))
                    copy(dn_hi[:, j % 2, 0:T], src).then_inc(*done("down_hi", (layer, j)))
                    if it is None:
                        ahead(s + j)
                    else:
                        round_weights(nxt[0] + b, it)
                for j in range(5):
                    down(j, j)
                dn_first = nxt[0]
                with act.Fori(0, 2) as it:
                    for b in range(8):
                        down(5 + b, b, it)
                nxt[0] = dn_first + 16
                again("down_hi", 8)
                down(FF_C - 1, 0)

            def network2(layer):
                s = first["l2", layer]
                tag = ("n2", layer)
                if layer == 0:
                    norm(("fin", 1), X, SEQ, lambda c: ("down_out", (1, c)))
                    act.wait_ge(*after("down_done", 1))
                    for r, (dst, name, rows) in enumerate(((oneh[0:32, 0, :], "onehot", 32), (oneh[0:12, 1, :], "vmask", 12))):
                        act.dma_start(dst, tb[0:rows, TAB[name][0]:TAB[name][1]]).then_inc(*done("vec_in", r, 16))
                    act.dma_start(relb[0:32, :], A["rel_bias"]).then_inc(*done("vec_in", 2, 16))
                    act.dma_start(decay0[0:16, :, :], tb[0:16, TAB["decay0"][0]:TAB["decay0"][1]]
                                  .rearrange("p (h n) -> p h n", h=4)).then_inc(*done("tab2_in", 0, 16))
                    for c in range(DC):
                        act.wait_ge(*after("fin1", c))
                    act.dma_start(H[:, :, 0:META], A["meta"]).then_inc(*done("meta_in", 0, 16))
                    act.dma_start(tab2[:, :], tb[:, TAB["cos2"][0]:TAB["decay1"][1]]).then_inc(*done("tab2_in", 1, 16))
                    act.wait_ge(*after("vec_ready", 0))
                    act.dma_start(by_distance, vec[0:12, :].unsqueeze(1).to_broadcast((12, P, VLEN))).then_inc(*done("vec_out", 0, 16))
                    act.wait_ge(*after("vec_out", 0))
                    nh = A_HEADS + B_HEADS
                    for r, (lo, n, off) in enumerate(((S1, N1, T2 - 1 - META), (S2, N2, T2 - 1 - META - P), (S0, N0, T2 - 1))):
                        act.dma_start(bias2[:, :, lo:lo + n],
                                      bass.AP(by_distance.tensor, off, [[VLEN - 1, P], [P * VLEN, nh], [1, n]]))\
                            .then_inc(*done("bias2_in", r, 16))
                    act.wait_ge(*after("meta_in", 0))
                act.dma_start(lamp[:, :], A["lam"][layer:layer + 1, :].to_broadcast((P, P)))\
                    .then_inc(*done("lam_in", layer, 16))
                if layer == 0:
                    act.wait_ge(*after("fin1", DC - 1))
                else:
                    act.wait_ge(*after("ff2_out", (0, DC - 1)))
                act.wait_ge(*after("lam_sum", (layer, 1)))
                act.activation(small[:, 28:30], small[:, 24:26], ACT.Exp).then_inc(*done("lam_exp", layer))
                act.dma_start(wi_r[:, :, :], A["wi"][layer]).then_inc(*done("wi_in", layer, 16))
                act.wait_ge(*after("wi_in", layer))
                copy(wi_w[:, 0, :, :], wi_r[:, :, :]).then_inc(*done("wi_hi", layer))
                norm((layer, 3), H, T2, None if layer == 0 else lambda c: ("ff2_out", (0, c)))
                ahead(s)
                norm_round((layer, 3), u_hi, T2)
                for step in L2_STEPS:
                    kind, k = step
                    if kind == "slab":
                        c = k
                        ahead(s + L2_AT[step])
                        act.wait_ge(*after("chunk", (layer, "p2", c)))
                        ps = lin[l2_bank(step)][:, 0:T2]
                        if c >= GC:
                            act.activation(nt[:, c % 2, 0:T2], ps, ACT.Tanh, scale=0.5).then_inc(*done("p2_out", (layer, c)))
                        else:
                            scale = HD ** -0.5 if QA <= c < KA or KCR <= c < QB else 32 ** -0.5 if QB <= c < KB else 1.0
                            copy(pj[:, c, :], ps, scale=scale).then_inc(*done("p2_out", (layer, c)))
                    elif kind == "vals":
                        ahead(s + L2_AT[step])
                        ahead(s + L2_AT[step] + 3)
                        for tt in range(3):
                            n = P if tt else META
                            act.wait_ge(*after("chunk", (layer, "v2", k, tt)))
                            copy(V2[0:n, tt, k * 512:(k + 1) * 512], lin[l2_vbank(step, tt)][0:n, :])\
                                .then_inc(*done("v2_out", (layer, k, tt)))
                    elif kind == "index":
                        for h in range(IDX_HEADS):
                            act.wait_ge(*after("index_dot", (layer, h)))
                            if h >= 2:
                                act.wait_ge(*after("index_sum", (layer, h - 2)))
                            act.activation(relu2[:, h % 2, :], aux[h % 2][:, 0:N1 + N2], ACT.Relu)\
                                .then_inc(*done("index_relu", (layer, h)))
                    elif kind in "ab":
                        comps = (0, 1) if kind == "b" else (0,)
                        for c in comps:
                            for t, (lo, n) in enumerate(((S1, N1), (S2, N2), (S0, N0))):
                                if t == 0:
                                    act.wait_ge(*after("max2", (layer, kind, k, c, 2)))
                                act.activation(p2[:, c, lo:lo + n], aux[c][:, lo:lo + n], ACT.Exp,
                                               bias=small[:, 3 * c + t:3 * c + t + 1],
                                               accum_out=small[:, 8 + 3 * c + t:9 + 3 * c + t])\
                                    .then_inc(*done("exp2", (layer, kind, k, c, t)))
                        unit_out(layer, kind, k)
                    elif kind == "c":
                        unit_out(layer, kind, k)
                    elif kind == "bcnorm":
                        for c in range(4):
                            if c == 0:
                                act.wait_ge(*after("unit_out", (layer, "b", B_HEADS - 1)))
                            if c >= 2:
                                act.wait_ge(*after("bc_summed", (layer, c - 2)))
                            act.activation(sq[:, c % 2, 0:T2], bc_raw[:, c, :], ACT.Square).then_inc(*done("bc_sq", (layer, c)))
                            if c:
                                bc_root(layer, c - 1)
                        bc_root(layer, 3)
                        for c in range(4):
                            act.wait_ge(*after("bc_normed", (layer, c)))
                            copy(o_hi[:, 4 + c, :], nr[:, c % 2, 0:T2]).then_inc(*done("bc_hi", (layer, c)))
                s += L2_FRONT + 8
                for m in range(DC):
                    ahead(s)
                    s += 1
                norm((layer, 4), H, T2, lambda c: ("mix2_out", (layer, c)))
                ahead(s)
                norm_round((layer, 4), u_hi, T2)

                def ff1(j, b, it=None):
                    plus = 0 if it is None else it * 8
                    if it is None:
                        ahead(s + j)
                    else:
                        round_weights(nxt[0] + b, it)
                    act.wait_ge(sem("slab_used"), split_no[s] + j + 1 + plus)
                    if it is not None or j >= 2:
                        act.wait_ge(sem("ff1_out"), base + j - 1 + plus)
                    act.activation(up_t[:, b % 2, 0:T2], lin[b % 4][:, 0:T2], ACT.Relu).then_inc(*done("ff1_relu", (layer, j)))
                base = FF2_C * layer
                for j in range(8):
                    ff1(j, j)
                f1 = nxt[0]
                with act.Fori(0, 3) as it:
                    for b in range(8):
                        ff1(8 + b, b, it)
                nxt[0] = f1 + 24
                again("ff1_relu", 16)
                s += FF2_C

                def ff2(j, b, it=None):
                    plus = 0 if it is None else it * 8
                    if it is not None or j >= 2:
                        act.wait_ge(sem("slab_used"), split_no[s] + j - 1 + plus)
                    src = ff2a[:, j, :] if it is None else ff2a[:, bass.ds(j + plus, 1), :].rearrange("p a t -> p (a t)")
                    if j == 0:
                        act.wait_ge(*after("ff1_all", layer))
                    copy(dn_hi[:, j % 2, 0:T2], src).then_inc(*done("ff2_hi", (layer, j)))
                    if it is None:
                        ahead(s + j)
                    else:
                        round_weights(nxt[0] + b, it)
                for j in range(7):
                    ff2(j, j)
                reps = 3 if layer == 0 else 2
                f2 = nxt[0]
                with act.Fori(0, reps) as it:
                    for b in range(8):
                        ff2(7 + b, b, it)
                nxt[0] = f2 + reps * 8
                again("ff2_hi", 8 * (reps - 1))
                for j in range(7 + reps * 8, FF2_C):
                    ff2(j, j)

            def bc_root(layer, c):
                act.wait_ge(*after("bc_summed", (layer, c)))
                root(bc_r[:, c, :], aux[c % 2][:, 0:T2], "bc_root", (layer, c))

            def unit_out(layer, kind, k):
                if kind != "c":
                    act.wait_ge(*after("pv2", (layer, *prev_unit(kind, k))))
                    act.wait_ge(*after("turned2", (layer, kind, k)))
                    copy(pt0[0:META, 0, :], aux[0][0:META, 0:T2]).then_inc(*done("pt2", (layer, kind, k, 0)))
                    copy(pt1[:, 0, :], aux[1][:, 0:384]).then_inc(*done("pt2", (layer, kind, k, 1)))
                act.wait_ge(*after("pv2", (layer, kind, k)))
                r = slice((k % 2) * HD, (k % 2) * HD + HD)
                if kind == "a":
                    copy(o_hi[r, k // 2, :], aux[3][r, 0:T2]).then_inc(*done("unit_out", (layer, kind, k)))
                else:
                    c = k // 2 + (2 if kind == "c" else 0)
                    copy(bc_raw[r, c, :], aux[3][r, 0:T2]).then_inc(*done("unit_out", (layer, kind, k)))

            ada()
            for layer in range(DEPTH):
                network1(layer)
            for layer in range(DEPTH):
                network2(layer)
            norm(("fin", 2), H, T2, lambda c: ("ff2_out", (1, c)))

        @block.tensor
        def _(pe):
            readers = {}

            def claim(b):
                if b in readers:
                    pe.wait_ge(*after(*readers.pop(b)))

            def weights(i, it=None):
                pe.wait_ge(sem("w_lo_ready"), split_no[i] + 1 + (0 if it is None else it * 8))

            def three(o, i, k, a_hi, a_lo, start, stop, col=None):
                s = i % RING
                hi, lo = w_hi[:, s, k * P:(k + 1) * P], w_lo[:, s, k * P:(k + 1) * P]
                pe.matmul(o, hi, a_hi, start=start, stop=False)
                pe.matmul(o, hi, a_lo, start=False, stop=False)
                return pe.matmul(o, lo, a_hi, start=False, stop=stop)

            def chunk(i, b, T, a_hi, a_lo, key, reader, h_key=None):
                weights(i)
                claim(b)
                for k in range(DC):
                    if h_key:
                        pe.wait_ge(*after("norm_lo", (h_key, k)))
                    mm = three(bank[b][:, 0:T], i, k, a_hi[:, k, 0:T], a_lo[:, k, 0:T], k == 0, k == DC - 1)
                mm.then_inc(*done("slab_used", i))
                seen["chunk", key] = seen["slab_used", i]
                readers[b] = reader

            def norm_sum(tag, T, reader_key):
                claim(4)
                for c in range(DC):
                    pe.wait_ge(*after("norm_sq", (tag, c)))
                    pe.matmul(aux[0][:, 0:T], ones_d, sq[:, c % 2, 0:T], start=c == 0, stop=c == DC - 1)\
                        .then_inc(*done("norm_summed", (tag, c)))
                readers[4] = ("norm_root", tag)

            def ada():
                pe.wait_ge(*after("c_silu", 0))
                with pe.Fori(0, DEPTH * 6) as it:
                    for b in range(2):
                        for s in range(4):
                            i = 4 * b + s
                            a, n = landed(i)
                            pe.wait_ge(a, n + it * (8 // RING) * 16)
                            for j in range(2):
                                k = 2 * s + j
                                g = 32 * (k % 4)
                                mm = pe.matmul(lin[b][g:g + 32, :], cs[:, k, :], raw[:, i % RING, j * 512:(j + 1) * 512],
                                               start=k < 4, stop=k >= 4, tile_position=(0, g))
                            mm.then_inc(*done("ada_slab_read", i))
                    for b in range(2):
                        pe.wait_ge(sem("ada_part_out"), b + 1 + it * 2)
                        for j in range(4):
                            o = aux[0][:, bass.ds((4 * b + j) * 2 + it * 16, 2)]
                            mm = pe.matmul(o, ada_part[:, b, j * P:(j + 1) * P], sel, start=True, stop=True)
                        mm.then_inc(*done("ada_turned", b))
                again("ada_slab_read", 8 * (DEPTH * 6 - 1))
                again("ada_turned", 2 * (DEPTH * 6 - 1))
                seen["ada_turned", "all"] = counts["ada_turned"]
                readers[4] = ("mod_ready", DEPTH - 1)

            def network1(layer):
                T = n_tok(layer)
                norm_sum((layer, 1), T_BOTH, None)
                s = first["l1", layer]
                nb = 0
                for c in range(CONV_C):
                    chunk(s, (2 * c) % 4, T, h_hi, h_lo, (layer, "glu_g", c), ("glu_tanh", (layer, c)),
                          (layer, 1) if c == 0 else None)
                    chunk(s + 1, (2 * c + 1) % 4, T, h_hi, h_lo, (layer, "glu_a", c), ("glu_out", (layer, c)))
                    s += 2
                for c in range(2 * QC):
                    Tq = T if c < QC else T_BOTH
                    chunk(s, c % 4, Tq, h_hi, h_lo, (layer, "qk", c), ("qk_out", (layer, c)))
                    if c:
                        rope(layer, c - 1)
                    s += 1
                for q in range(QKV_V_SLABS):
                    weights(s)
                    for j in range(2):
                        k = 2 * q + j
                        wh, wl = (w[:, s % RING, j * 512:(j + 1) * 512] for w in (w_hi, w_lo))
                        for tt in range(4):
                            if k == 0:
                                claim(tt)
                            a, b = (x[:, k, tt * P:(tt + 1) * P] for x in (h_hi, h_lo))
                            pe.matmul(lin[tt][:, :], a, wh, start=k == 0, stop=False)
                            pe.matmul(lin[tt][:, :], b, wh, start=False, stop=False)
                            mm = pe.matmul(lin[tt][:, :], a, wl, start=False, stop=k == DC - 1)
                    mm.then_inc(*done("slab_used", s))
                    if q == 0:
                        rope(layer, 2 * QC - 1)
                    s += 1
                for tt in range(4):
                    seen["chunk", (layer, "v", tt)] = seen["slab_used", s - 1]
                    readers[tt] = ("v_out", (layer, tt))
                for h in range(HEADS):
                    scores(layer, h)
                    g = 2 * h
                    chunk(s, g % 4, T, h_hi, h_lo, (layer, "gate", g), ("gate_out", (layer, g)))
                    turn(layer, h)
                    chunk(s + 1, (g + 1) % 4, T, h_hi, h_lo, (layer, "gate", g + 1), ("gate_out", (layer, g + 1)))
                    values(layer, h)
                    s += 2
                claim(4)
                for c in range(CONV_C):
                    pe.wait_ge(*after("conv_tap", (layer, c, TAPS - 1)))
                    mm = pe.matmul(aux[0][:, 0:T], ones_c, cv[:, c, 0:T], start=c == 0, stop=c == CONV_C - 1)
                mm.then_inc(*done("ln_mean", layer))
                readers[4] = ("conv_centred", (layer, CONV_C - 1))
                claim(5)
                for c in range(CONV_C):
                    pe.wait_ge(*after("ln_sq", (layer, c)))
                    pe.matmul(aux[1][:, 0:T], ones_c, sq[:, c % 2, 0:T], start=c == 0, stop=c == CONV_C - 1)\
                        .then_inc(*done("ln_var", (layer, c)))
                readers[5] = ("ln_root", layer)
                for m in range(DC):
                    weights(s)
                    b = (2 * m) % 4
                    claim(b)
                    for k in range(4):
                        if m == 0:
                            pe.wait_ge(*after("conv_lo", (layer, k)))
                        three(bank[b][:, 0:T], s, k, cv_hi[:, k, 0:T], cv_lo[:, k, 0:T], k == 0, k == 3)
                    claim(b + 1)
                    if m == 0:
                        pe.wait_ge(*after("attn_lo", (layer, HEADS - 1)))
                    for k in range(4):
                        mm = three(bank[b + 1][:, 0:T], s, 4 + k, at_hi[:, k, 0:T], at_lo[:, k, 0:T], k == 0, k == 3)
                    mm.then_inc(*done("slab_used", s))
                    seen["chunk", (layer, "branch", m)] = seen["slab_used", s]
                    readers[b] = readers[b + 1] = ("merged", (layer, m))
                    s += 1
                for m in range(DC):
                    if m == 0:
                        pe.wait_ge(*after("merge_lo", (layer, DC - 1)))
                    chunk(s, m % 4, T, y_hi, y_lo, (layer, "mix", m), ("mix_out", (layer, m)))
                    s += 1
                norm_sum((layer, 2), T, None)

                def up(j, b, it=None):
                    plus = 0 if it is None else it * 4
                    for w in range(2):
                        i = s + 2 * j + w
                        weights(i, it)
                        bk = (2 * b + w) % 4
                        if it is None:
                            claim(bk)
                        else:
                            pe.wait_ge(sem("up_conv"), 2 * (FF_C * layer + j - 2) + w + 1 + plus * 2)
                        for k in range(DC):
                            if j == 0 and w == 0:
                                pe.wait_ge(*after("norm_lo", ((layer, 2), k)))
                            mm = three(bank[bk][:, 0:T], i, k, h_hi[:, k, 0:T], h_lo[:, k, 0:T], k == 0, k == DC - 1)
                        mm.then_inc(*done("slab_used", i))
                for j in range(2):
                    up(j, j)
                with pe.Fori(0, 5) as it:
                    for b in range(4):
                        up(2 + b, b, it)
                again("slab_used", 4 * 8)
                s += 2 * FF_C
                pe.wait_ge(*after("up_all", layer))

                def down(j, b, it=None):
                    plus = 0 if it is None else it * 8
                    weights(s + j, it)
                    pe.wait_ge(sem("down_lo"), FF_C * layer + j + 1 + plus)
                    for m in range(DC):
                        if j == 0:
                            claim(m)
                        mm = three(bank[m][:, 0:T], s + j, m, dn_hi[:, j % 2, 0:T], dn_lo[:, j % 2, 0:T],
                                   j == 0, j == FF_C - 1)
                    mm.then_inc(*done("slab_used", s + j))
                for j in range(5):
                    down(j, j)
                with pe.Fori(0, 2) as it:
                    for b in range(8):
                        down(5 + b, b, it)
                again("slab_used", 8)
                down(FF_C - 1, 0)
                seen["chunk", (layer, "down")] = counts["slab_used"]
                for m in range(DC):
                    readers[m] = ("down_out", (layer, m))

            def rope(layer, c):
                claim(5)
                src = qT[:, c, 0:SEQ] if c < QC else kT[:, c - QC, 0:SEQ]
                pe.wait_ge(*after("qk_out", (layer, c)))
                pe.matmul(aux[1][:, 0:SEQ], perm1, src, start=True, stop=True).then_inc(*done("rope_turn", (layer, c)))
                readers[5] = ("rope_part", (layer, c))

            def scores(layer, h):
                r = slice((h % 2) * HD, (h % 2) * HD + HD)
                c = h // 2
                pe.wait_ge(*after("rope_out", (layer, 2 * QC - 1)))
                for t in range(2):
                    claim(4 + t)
                    pe.matmul(aux[t][:, :], qT[r, c, t * P:(t + 1) * P], kT[r, c, :], start=True, stop=True)\
                        .then_inc(*done("attn_score", (layer, h, t)))
                if layer == 0:
                    claim(6)
                    for t in range(2):
                        pe.matmul(aux[2][:, t * 256:(t + 1) * 256], qT[r, c, SEQ + t * P:SEQ + (t + 1) * P],
                                  kT[r, c, SEQ:T_BOTH], start=True, stop=True)\
                            .then_inc(*done("attn_score", (layer, h, 2 + t)))

            def turn(layer, h):
                for t in range(2):
                    pe.wait_ge(*after("attn_prob", (layer, h, t)))
                    for k in range(4):
                        mm = pe.transpose(aux[t][:, k * P:(k + 1) * P], p_x[:, t, k * P:(k + 1) * P], ident)
                    mm.then_inc(*done("attn_turned", (layer, h, t)))
                    readers[4 + t] = ("attn_pt", (layer, h, t))
                if layer == 0:
                    pe.wait_ge(*after("attn_prob", (layer, h, 3)))
                    for t in range(2):
                        for k in range(2):
                            mm = pe.transpose(aux[2][:, (2 * t + k) * P:(2 * t + k + 1) * P],
                                              p_c[:, t, k * P:(k + 1) * P], ident)
                    mm.then_inc(*done("attn_turned", (layer, h, 2)))
                    readers[6] = ("attn_pt", (layer, h, 2))

            def values(layer, h):
                r = slice((h % 2) * HD, (h % 2) * HD + HD)
                claim(7)
                pe.wait_ge(*after("v_out", (layer, 3)))
                pe.wait_ge(*after("attn_pt", (layer, h, 2 if layer == 0 else 1)))
                for k in range(4):
                    mm = pe.matmul(aux[3][r, 0:SEQ], V[:, k, h * HD:(h + 1) * HD], pt_x[:, k, :],
                                   start=k == 0, stop=k == 3)
                if layer == 0:
                    for k in range(2):
                        mm = pe.matmul(aux[3][r, SEQ:T_BOTH], V[:, 2 + k, h * HD:(h + 1) * HD], pt_c[:, k, :],
                                       start=k == 0, stop=k == 1)
                mm.then_inc(*done("attn_pv", (layer, h)))
                readers[7] = ("attn_lo", (layer, h))

            def network2(layer):
                s = first["l2", layer]
                if layer == 0:
                    norm_sum(("fin", 1), SEQ, None)
                    pe.wait_ge(*after("vec_in", 2))
                    for b, (lo, hi) in enumerate(((0, 512), (512, VLEN))):
                        claim(5 + b)
                        mm = pe.matmul(aux[1 + b][0:12, 0:hi - lo], relb[0:32, :], oneh[0:32, 0, lo:hi], start=True, stop=True)
                    mm.then_inc(*done("vec_made", 0))
                    readers[5] = readers[6] = ("vec_ready", 0)
                norm_sum((layer, 3), T2, None)
                fresh = True
                for step in L2_STEPS:
                    kind, k = step
                    if kind == "slab":
                        reader = ("p2_out", (layer, k)) if k < GC else ("gate2", (layer, k))
                        chunk(s + L2_AT[step], l2_bank(step), T2, u_hi, u_lo, (layer, "p2", k), reader,
                              (layer, 3) if fresh else None)
                        fresh = False
                        if QCR < k <= QB:
                            rope2(layer, k - 1)
                    elif kind == "vals":
                        for q in range(4):
                            i = s + L2_AT[step] + q
                            weights(i)
                            for j in range(2):
                                kk = 2 * q + j
                                wh, wl = (w[:, i % RING, j * 512:(j + 1) * 512] for w in (w_hi, w_lo))
                                for tt in range(3):
                                    b = l2_vbank(step, tt)
                                    if kk == 0:
                                        claim(b)
                                    t0 = 0 if tt == 0 else META + (tt - 1) * P
                                    a, al = (x[:, kk, t0:t0 + P] for x in (u_hi, u_lo))
                                    pe.matmul(lin[b][:, :], a, wh, start=kk == 0, stop=False)
                                    pe.matmul(lin[b][:, :], al, wh, start=False, stop=False)
                                    mm = pe.matmul(lin[b][:, :], a, wl, start=False, stop=kk == DC - 1)
                            mm.then_inc(*done("slab_used", i))
                        for tt in range(3):
                            seen["chunk", (layer, "v2", k, tt)] = seen["slab_used", i]
                            readers[l2_vbank(step, tt)] = ("v2_out", (layer, k, tt))
                    elif kind == "wi":
                        pe.wait_ge(*after("wi_lo", layer))
                        claim(6)
                        for t in range(2):
                            for kk in range(DC):
                                t0 = META + t * P
                                a, al = (x[:, kk, t0:t0 + P] for x in (u_hi, u_lo))
                                o = aux[2][:, 8 * t:8 * t + 8]
                                pe.matmul(o, a, wi_w[:, 0, kk, :], start=kk == 0, stop=False)
                                pe.matmul(o, al, wi_w[:, 0, kk, :], start=False, stop=False)
                                mm = pe.matmul(o, a, wi_w[:, 1, kk, :], start=False, stop=kk == DC - 1)
                        mm.then_inc(*done("wi_made", layer))
                        readers[6] = ("wi_out", layer)
                    elif kind == "index":
                        for h in range(IDX_HEADS):
                            r = slice((h % 2) * HD, (h % 2) * HD + HD)
                            claim(4 + h % 2)
                            pe.wait_ge(*after("p2_out", (layer, QI + 3)))
                            q = pj[r, QI + h // 2, :]
                            pe.matmul(aux[h % 2][:, S1:S1 + N1], q[:, META:META + P], pj[r, KI, 0:N1], start=True, stop=True)
                            pe.matmul(aux[h % 2][:, S2:S2 + N2], q[:, META + P:T2], pj[r, KI, 0:N2], start=True, stop=True)\
                                .then_inc(*done("index_dot", (layer, h)))
                            readers[4 + h % 2] = ("index_relu", (layer, h))
                    elif kind == "a" or kind == "b":
                        comps = (0, 1) if kind == "b" else (0,)
                        for c in comps:
                            if kind == "a":
                                r = slice((k % 2) * HD, (k % 2) * HD + HD)
                                q, kk = pj[r, QA + k // 2, :], pj[r, KA + k // 2, :]
                                if k == 0:
                                    pe.wait_ge(*after("p2_out", (layer, KA + 3)))
                            else:
                                r = slice((k % 2) * HD + 32 * c, (k % 2) * HD + 32 * c + 32)
                                q, kk = pj[r, QB + k // 2, :], pj[r, KB + k // 2, :]
                                if k == 0 and c == 0:
                                    pe.wait_ge(*after("p2_out", (layer, KB + 1)))
                            claim(4 + c)
                            pe.matmul(aux[c][:, S1:S1 + N1], q[:, META:META + P], kk[:, 0:N1], start=True, stop=True)
                            pe.matmul(aux[c][:, S2:S2 + N2], q[:, META + P:T2], kk[:, 0:N2], start=True, stop=True)
                            pe.matmul(aux[c][:, S0:S0 + N0], q[:, 0:P], kk[:, 0:N0], start=True, stop=True)\
                                .then_inc(*done("score2", (layer, kind, k, c)))
                        pe.wait_ge(*after("prob2", (layer, kind, k)))
                        claim(4)
                        claim(5)
                        pr = p2[:, 0, :]
                        o0 = aux[0][0:META, :]
                        pe.matmul(o0[:, 0:META], pr[0:META, S0:S0 + META], ident[0:META, 0:META], start=True, stop=True)
                        pe.matmul(o0[:, META:META + P], pr[:, S1:S1 + META], ident, start=True, stop=True)
                        pe.matmul(o0[:, META + P:T2], pr[:, S2:S2 + META], ident, start=True, stop=True)
                        pe.transpose(aux[1][:, 0:P], pr[:, S1 + META:S1 + META + P], ident)
                        pe.transpose(aux[1][:, P:2 * P], pr[:, S2 + META:S2 + META + P], ident)
                        pe.transpose(aux[1][:, 2 * P:3 * P], pr[:, S2 + META + P:S2 + T2], ident)\
                            .then_inc(*done("turned2", (layer, kind, k)))
                        readers[4] = ("pt2", (layer, kind, k, 0))
                        readers[5] = ("pt2", (layer, kind, k, 1))
                        values2(layer, kind, k)
                    elif kind == "c":
                        r = slice((k % 2) * HD, (k % 2) * HD + HD)
                        q, kk = pj[r, QCR + k // 2, :], pj[r, KCR + k // 2, :]
                        if k == 0:
                            pe.wait_ge(*after("rope2_out", (layer, QB - 1)))
                        claim(4)
                        claim(5)
                        pe.matmul(aux[0][0:META, 0:T2], kk[:, 0:META], q, start=True, stop=True)
                        pe.matmul(aux[1][:, 0:256], kk[:, META:META + P], q[:, META:T2], start=True, stop=True)
                        pe.matmul(aux[1][:, 256:384], kk[:, META + P:T2], q[:, META + P:T2], start=True, stop=True)\
                            .then_inc(*done("score2", (layer, kind, k, 0)))
                        readers[4] = readers[5] = ("pt2c", (layer, k, 1))
                        values2(layer, kind, k)
                    elif kind == "bcnorm":
                        for c in range(4):
                            pe.wait_ge(*after("bc_sq", (layer, c)))
                            claim(4 + c % 2)
                            pe.matmul(aux[c % 2][:, 0:T2], ones_h, sq[:, c % 2, 0:T2], start=True, stop=True)\
                                .then_inc(*done("bc_summed", (layer, c)))
                            readers[4 + c % 2] = ("bc_root", (layer, c))
                s += L2_FRONT + 8
                for m in range(DC):
                    if m == 0:
                        pe.wait_ge(*after("unit_lo", (layer, A_HEADS - 1)))
                        pe.wait_ge(*after("bc_lo", (layer, 3)))
                    chunk(s, m % 4, T2, o_hi, o_lo, (layer, "mix2", m), ("mix2_out", (layer, m)))
                    s += 1
                norm_sum((layer, 4), T2, None)

                def ff1(j, b, it=None):
                    plus = 0 if it is None else it * 8
                    weights(s + j, it)
                    if it is None:
                        if j < 4:
                            claim(b % 4)
                        else:
                            pe.wait_ge(*after("ff1_out", (layer, j - 4)))
                    else:
                        pe.wait_ge(sem("ff1_out"), FF2_C * layer + j - 3 + plus)
                    for k in range(DC):
                        if j == 0:
                            pe.wait_ge(*after("norm_lo", ((layer, 4), k)))
                        mm = three(lin[b % 4][:, 0:T2], s + j, k, u_hi[:, k, :], u_lo[:, k, :], k == 0, k == DC - 1)
                    mm.then_inc(*done("slab_used", s + j))
                for j in range(8):
                    ff1(j, j)
                with pe.Fori(0, 3) as it:
                    for b in range(8):
                        ff1(8 + b, b, it)
                again("slab_used", 16)
                s += FF2_C
                pe.wait_ge(*after("ff1_all", layer))

                def ff2(j, b, it=None):
                    plus = 0 if it is None else it * 8
                    weights(s + j, it)
                    pe.wait_ge(sem("ff2_lo"), FF2_C * layer + j + 1 + plus)
                    for m in range(DC):
                        if j == 0:
                            claim(m)
                        mm = three(bank[m][:, 0:T2], s + j, m, dn_hi[:, j % 2, 0:T2], dn_lo[:, j % 2, 0:T2], j == 0, j == FF2_C - 1)
                    mm.then_inc(*done("slab_used", s + j))
                for j in range(7):
                    ff2(j, j)
                with pe.Fori(0, 3) as it:
                    for b in range(8):
                        ff2(7 + b, b, it)
                again("slab_used", 16)
                ff2(FF2_C - 1, 0)
                seen["chunk", (layer, "ff2")] = counts["slab_used"]
                for m in range(DC):
                    readers[m] = ("ff2_out", (layer, m))

            def rope2(layer, c):
                claim(5)
                pe.wait_ge(*after("p2_out", (layer, c)))
                pe.matmul(aux[1][:, 0:T2], perm2, pj[:, c, :], start=True, stop=True).then_inc(*done("rope2_turn", (layer, c)))
                readers[5] = ("rope2_part", (layer, c))

            def values2(layer, kind, k):
                r = slice((k % 2) * HD, (k % 2) * HD + HD)
                col = {"a": 0, "b": 512, "c": 768}[kind] + k * HD
                claim(7)
                if kind == "c":
                    pe.wait_ge(*after("pt2c", (layer, k, 1)))
                else:
                    pe.wait_ge(*after("pt2", (layer, kind, k, 1)))
                pe.wait_ge(*after("v2_out", (layer, 0 if kind == "a" else 1, 2)))
                pe.matmul(aux[3][r, 0:T2], V2[0:META, 0, col:col + HD], pt0[0:META, 0, :], start=True, stop=False)
                pe.matmul(aux[3][r, META:T2], V2[:, 1, col:col + HD], pt1[:, 0, 0:256], start=False, stop=False)
                pe.matmul(aux[3][r, META + P:T2], V2[:, 2, col:col + HD], pt1[:, 0, 256:384], start=False, stop=True)\
                    .then_inc(*done("pv2", (layer, kind, k)))
                readers[7] = ("unit_lo", (layer, k)) if kind == "a" else ("unit_out", (layer, kind, k))

            pe.wait_ge(*after("const_in", 4))
            ada()
            for layer in range(DEPTH):
                network1(layer)
            for layer in range(DEPTH):
                network2(layer)
            norm_sum(("fin", 2), T2, None)

        @block.vector
        def _(dve):
            def tt(o, a, b, op):
                return dve.tensor_tensor(o, a, b, op)

            def ts(o, a, s1, op0, s2=None, op1=None):
                if op1 is None:
                    return dve.tensor_scalar(o, a, s1, None, op0)
                return dve.tensor_scalar(o, a, s1, s2, op0, op1)

            def stt(o, a, s, b, op0, op1):
                return dve.scalar_tensor_tensor(out=o, in0=a, scalar=s, in1=b, op0=op0, op1=op1)

            def inverse(ap, root, name, key):
                dve.wait_ge(*after(root, key))
                dve.reciprocal(ap, ap).then_inc(*done(name, key))
                dve.wait_ge(*after(name, key))

            def norm(tag, X_, T, hi, lo, affine, k_ready=None):
                inverse(rinv[:, 0:T], "norm_root", "norm_rinv", tag)

                def rest(c):
                    dve.wait_ge(*after("norm_hi", (tag, c)))
                    tt(lo[:, c, 0:T], nr[:, c % 2, 0:T], hi[:, c, 0:T].bitcast(F32), ALU.subtract)\
                        .then_inc(*done("norm_lo", (tag, c)))
                for c in range(DC):
                    tt(nt[:, c % 2, 0:T], X_[:, c, 0:T], rinv[:, 0:T], ALU.mult).then_inc(*done("norm_x", (tag, c)))
                    dve.wait_ge(*after("norm_x", (tag, c)))
                    affine(c).then_inc(*done("normed", (tag, c)))
                    if c:
                        rest(c - 1)
                rest(DC - 1)

            dve.wait_ge(*after("const_in", 4))
            dve.memset(eps[:, :], EPS).then_inc(*done("c_silu_part", "eps"))
            dve.memset(cs[:, :, :], 0.0).then_inc(*done("c_silu_part", 0))
            dve.wait_ge(*after("c_tanh", 0))
            ts(cth[:, :, :], cth[:, :, :], 1.0, ALU.add, 0.5, ALU.mult).then_inc(*done("c_silu_part", 1))
            dve.wait_ge(*after("c_silu_part", 1))
            tt(cs[:, :, 0:2], cth[:, :, :], cvec[:, :, :], ALU.mult).then_inc(*done("c_silu", 0))

            def modulation(layer):
                for n, (name, lo, hi) in enumerate((("dw", 0, CONV_C * TAPS), ("lng", 0, CONV_C), ("lnb", 0, CONV_C),
                                                    ("fdwb", FF_C, 2 * FF_C))):
                    v = par(layer, name)[:, lo:hi]
                    ts(v, v, 0.5, ALU.mult).then_inc(*done("prm_half", (layer, n)))
                fdw = par(layer, "fdw").rearrange("p (t c) -> p t c", t=3)[:, :, FF_C:2 * FF_C]
                ts(fdw, fdw, 0.5, ALU.mult).then_inc(*done("prm_half", (layer, 4)))
                dve.wait_ge(*after("ada_turned", "all"))
                a = 12 * DC * layer
                for st in range(2):
                    src = aux[0][:, a:a + 12 * DC].rearrange("p (c s) -> p c s", s=2)[:, :, st]
                    tt(mod[:, layer, :, st], src, par(layer, "bada"), ALU.add).then_inc(*done("mod_part", (layer, st)))
                dve.wait_ge(*after("mod_part", (layer, 1)))
                for st in range(2):
                    stt(a1[:, layer, :, st], mod[:, layer, DC:2 * DC, st], 1.0, par(layer, "n1g"), ALU.add, ALU.mult)\
                        .then_inc(*done("mod_part", (layer, 2, st)))
                    stt(a2[:, layer, :, st], mod[:, layer, 4 * DC:5 * DC, st], 1.0, par(layer, "n2g"), ALU.add, ALU.mult)\
                        .then_inc(*done("mod_part", (layer, 3, st)))
                ts(gh[:, layer, 0, :, :], mod[:, layer, 2 * DC:3 * DC, :], 0.5, ALU.mult).then_inc(*done("mod_part", (layer, 4)))
                dve.tensor_copy(gh[:, layer, 1, :, :], mod[:, layer, 5 * DC:6 * DC, :]).then_inc(*done("mod_ready", layer))

            def network1(layer):
                T = n_tok(layer)
                if layer:
                    dve.wait_ge(*after("down_done", layer - 1))
                dve.memset(upad[:, :, :, 0:HALO], 0.0).then_inc(*done("halo", (layer, 0)))
                dve.memset(upad[:, :, :, HALO + SEQ:], 0.0).then_inc(*done("halo", (layer, 1)))

                def affine(scale, shift_at, streams_):
                    def f(c):
                        for st, cols in streams_:
                            i = ts(nr[:, c % 2, cols], nt[:, c % 2, cols], scale[:, layer, c, st:st + 1], ALU.mult,
                                   mod[:, layer, shift_at + c, st:st + 1], ALU.add)
                            if (st, cols) != streams_[-1]:
                                i.then_inc(*done("normed_part", (layer, shift_at, c, st)))
                        return i
                    return f
                if layer == 0:
                    dve.wait_ge(*after("x_in", 0))
                norm((layer, 1), X, T_BOTH, h_hi, h_lo, affine(a1, 0, parts(0)))
                for c in range(CONV_C):
                    dve.wait_ge(*after("glu_tanh", (layer, c)))
                    dve.wait_ge(*after("chunk", (layer, "glu_a", c), ))
                    n = 2 if layer == 0 else 1
                    stt(upad[:, c, 0:n, HALO:HALO + SEQ], streams(glu_t[:, c % 2, :], layer), 1.0,
                        streams(lin[(2 * c + 1) % 4], layer), ALU.add, ALU.mult).then_inc(*done("glu_out", (layer, c)))
                for c in range(2 * QC):
                    src = qT[:, c, 0:SEQ] if c < QC else kT[:, c - QC, 0:SEQ]
                    dve.wait_ge(*after("rope_turn", (layer, c)))
                    tt(nt[:, c % 2, 0:SEQ], aux[1][:, 0:SEQ], sin1, ALU.mult).then_inc(*done("rope_part", (layer, c)))
                    tt(src, src, cos1, ALU.mult).then_inc(*done("rope_cos", (layer, c)))
                    dve.wait_ge(*after("rope_cos", (layer, c)))
                    dve.wait_ge(*after("rope_part", (layer, c)))
                    tt(src, src, nt[:, c % 2, 0:SEQ], ALU.add).then_inc(*done("rope_out", (layer, c)))
                taps = [(c, t) for c in range(CONV_C) for t in range(TAPS)]

                def tap():
                    if not taps:
                        return
                    c, t = taps.pop(0)
                    n = 2 if layer == 0 else 1
                    src = upad[:, c, 0:n, t:t + SEQ]
                    w = par(layer, "dw", c * TAPS + t)
                    dst = streams(cv[:, c, :], layer)
                    if t == 0:
                        if c == 0:
                            dve.wait_ge(*after("glu_out", (layer, CONV_C - 1)))
                        ts(dst, src, w, ALU.mult, par(layer, "dwb", c), ALU.add).then_inc(*done("conv_tap", (layer, c, t)))
                    else:
                        dve.wait_ge(*after("conv_tap", (layer, c, t - 1)))
                        stt(dst, src, w, dst, ALU.mult, ALU.add).then_inc(*done("conv_tap", (layer, c, t)))

                units = [0, 1] + ([2, 3] if layer == 0 else [])
                for h in range(HEADS):
                    bh = biash[:, h % 2, :, :]
                    dve.wait_ge(*after(f"bias_in{h % 2}", (layer, h, 1, 1)))
                    m = win.unsqueeze(1).to_broadcast((P, 8, GRID_W))
                    tt(bh.rearrange("p t (a b) -> p (t a) b", a=4), bh.rearrange("p t (a b) -> p (t a) b", a=4), m, ALU.add)\
                        .then_inc(*done("bias_masked", (layer, h)))
                    dve.wait_ge(*after("bias_masked", (layer, h)))
                    for u in units:
                        dve.wait_ge(*after("attn_score", (layer, h, u if u < 2 else 3)))
                        if u < 2:
                            tt(aux[u][:, 0:SEQ], aux[u][:, 0:SEQ], bh[:, u, :], ALU.add).then_inc(*done("attn_added", (layer, h, u)))
                            dve.wait_ge(*after("attn_added", (layer, h, u)))
                            s = aux[u][:, :]
                        else:
                            s = aux[2][:, (u - 2) * 256:(u - 1) * 256]
                        if h:
                            dve.wait_ge(*after("attn_exp", (layer, h - 1, u)))
                        dve.tensor_reduce(small[:, u:u + 1], s, AXX, ALU.max, negate=True).then_inc(*done("attn_max", (layer, h, u)))
                    for _ in range(8):
                        tap()
                    for u in units:
                        dve.wait_ge(*after("attn_exp", (layer, h, u)))
                        dve.reciprocal(small[:, 16 + u:17 + u], small[:, 8 + u:9 + u]).then_inc(*done("attn_recip", (layer, h, u)))
                        dve.wait_ge(*after("attn_recip", (layer, h, u)))
                        pr = p_x[:, u, :] if u < 2 else p_c[:, u - 2, :]
                        ts(pr, pr, small[:, 16 + u:17 + u], ALU.mult).then_inc(*done("attn_prob", (layer, h, u)))
                    for _ in range(8):
                        tap()
                    r = slice((h % 2) * HD, (h % 2) * HD + HD)
                    dve.wait_ge(*after("attn_hi", (layer, h)))
                    tt(at_lo[r, h // 2, 0:T], aux[3][r, 0:T], at_hi[r, h // 2, 0:T].bitcast(F32), ALU.subtract)\
                        .then_inc(*done("attn_lo", (layer, h)))
                while taps:
                    tap()
                dve.wait_ge(*after("ln_mean", layer))
                for c in range(CONV_C):
                    tt(cv[:, c, 0:T], cv[:, c, 0:T], aux[0][:, 0:T], ALU.subtract).then_inc(*done("conv_centred", (layer, c)))
                inverse(rinv[:, 0:T], "ln_root", "ln_rstd", layer)
                for c in range(CONV_C):
                    tt(cv[:, c, 0:T], cv[:, c, 0:T], rinv[:, 0:T], ALU.mult).then_inc(*done("conv_scaled", (layer, c)))
                    dve.wait_ge(*after("conv_scaled", (layer, c)))
                    ts(nr[:, c % 2, 0:T], cv[:, c, 0:T], par(layer, "lng", c), ALU.mult, par(layer, "lnb", c), ALU.add)\
                        .then_inc(*done("conv_affine", (layer, c)))
                    dve.wait_ge(*after("conv_tanh", (layer, c)))
                    stt(sq[:, c % 2, 0:T], nt[:, c % 2, 0:T], 1.0, nr[:, c % 2, 0:T], ALU.add, ALU.mult)\
                        .then_inc(*done("conv_silu", (layer, c)))
                    dve.wait_ge(*after("conv_hi", (layer, c)))
                    tt(cv_lo[:, c, 0:T], sq[:, c % 2, 0:T], cv_hi[:, c, 0:T].bitcast(F32), ALU.subtract)\
                        .then_inc(*done("conv_lo", (layer, c)))
                def merge_rest(m):
                    dve.wait_ge(*after("merge_hi", (layer, m)))
                    tt(y_lo[:, m, 0:T], nr[:, m % 2, 0:T], y_hi[:, m, 0:T].bitcast(F32), ALU.subtract)\
                        .then_inc(*done("merge_lo", (layer, m)))
                for m in range(DC):
                    b = (2 * m) % 4
                    dve.wait_ge(*after("chunk", (layer, "branch", m)))
                    if m == 0:
                        dve.wait_ge(*after("gate_out", (layer, 2 * DC - 1)))
                    if m:
                        dve.wait_ge(*after("merged", (layer, m - 1)))
                    stt(nt[:, 0, 0:T], gates[:, 2 * m, 0:T], 1.0, lin[b][:, 0:T], ALU.add, ALU.mult)\
                        .then_inc(*done("merge_part", (layer, m, 0)))
                    stt(nt[:, 1, 0:T], gates[:, 2 * m + 1, 0:T], 1.0, lin[b + 1][:, 0:T], ALU.add, ALU.mult)\
                        .then_inc(*done("merge_part", (layer, m, 1)))
                    dve.wait_ge(*after("merge_part", (layer, m, 1)))
                    tt(nr[:, m % 2, 0:T], nt[:, 0, 0:T], nt[:, 1, 0:T], ALU.add).then_inc(*done("merged", (layer, m)))
                    if m:
                        merge_rest(m - 1)
                merge_rest(DC - 1)
                for m in range(DC):
                    dve.wait_ge(*after("chunk", (layer, "mix", m)))
                    ps = parts(layer)
                    for st, cols in ps:
                        i = stt(X[:, m, cols], lin[m % 4][:, cols], gh[:, layer, 0, m, st:st + 1], X[:, m, cols], ALU.mult, ALU.add)
                        i.then_inc(*(done("mix_out", (layer, m)) if st == ps[-1][0] else done("mix_part", (layer, m))))
                norm((layer, 2), X, T, h_hi, h_lo, affine(a2, 3 * DC, parts(layer)))

                base = FF_C * layer

                def up(j, b, it=None):
                    plus = 0 if it is None else it * 4
                    for w, buf in enumerate((up_a, up_g)):
                        cc = w * FF_C + j
                        ps = streams(lin[(2 * b + w) % 4], layer)
                        acc = streams(buf[:, b % 2, :], layer)
                        dve.wait_ge(sem("up_mid"), 2 * (base + j) + w + 1 + plus * 2)
                        for t, (o, i) in ((0, (slice(1, SEQ), slice(0, SEQ - 1))), (2, (slice(0, SEQ - 1), slice(1, SEQ)))):
                            wcol = par(layer, "fdw", t * 2 * FF_C + cc, plus)
                            ins = stt(acc[:, :, o], ps[:, :, i], wcol, acc[:, :, o], ALU.mult, ALU.add)
                            if t == 0:
                                ins.then_inc(*done("up_left", (layer, j, w)))
                                dve.wait_ge(sem("up_left"), 2 * (base + j) + w + 1 + plus * 2)
                            else:
                                ins.then_inc(*done("up_conv", (layer, j, w)))
                    dve.wait_ge(sem("up_tanh"), base + j + 1 + plus)
                    t_ = up_t[:, b % 2, 0:T]
                    stt(t_, t_, 1.0, up_g[:, b % 2, 0:T], ALU.add, ALU.mult).then_inc(*done("up_silu", (layer, j)))
                    dve.wait_ge(sem("up_silu"), base + j + 1 + plus)
                    dst = ffa[:, j, 0:T] if it is None else ffa[:, bass.ds(j + plus, 1), 0:T].rearrange("p a t -> p (a t)")
                    tt(dst, t_, up_a[:, b % 2, 0:T], ALU.mult).then_inc(*done("up_out", (layer, j)))
                for j in range(2):
                    up(j, j)
                with dve.Fori(0, 5) as it:
                    for b in range(4):
                        up(2 + b, b, it)
                for n, k in (("up_left", 32), ("up_conv", 32), ("up_silu", 16), ("up_out", 16)):
                    again(n, k)
                seen["up_all", layer] = counts["up_out"]

                def down(j, b, it=None):
                    plus = 0 if it is None else it * 8
                    dve.wait_ge(sem("down_hi"), base + j + 1 + plus)
                    src = ffa[:, j, 0:T] if it is None else ffa[:, bass.ds(j + plus, 1), 0:T].rearrange("p a t -> p (a t)")
                    tt(dn_lo[:, j % 2, 0:T], src, dn_hi[:, j % 2, 0:T].bitcast(F32), ALU.subtract)\
                        .then_inc(*done("down_lo", (layer, j)))
                for j in range(5):
                    down(j, j)
                with dve.Fori(0, 2) as it:
                    for b in range(8):
                        down(5 + b, b, it)
                again("down_lo", 8)
                down(FF_C - 1, 0)
                dve.wait_ge(*after("chunk", (layer, "down")))
                for m in range(DC):
                    ps = parts(layer)
                    for st, cols in ps:
                        i = stt(X[:, m, cols], bank[m][:, cols], gh[:, layer, 1, m, st:st + 1], X[:, m, cols], ALU.mult, ALU.add)
                        i.then_inc(*(done("down_out", (layer, m)) if st == ps[-1][0] else done("down_part", (layer, m))))
                seen["down_done", layer] = seen["down_out", (layer, DC - 1)]

            def network2(layer):
                if layer == 0:
                    inverse(rinv[:, 0:SEQ], "norm_root", "norm_rinv", ("fin", 1))
                    for c in range(DC):
                        tt(nt[:, c % 2, 0:SEQ], X[:, c, 0:SEQ], rinv[:, 0:SEQ], ALU.mult).then_inc(*done("fin1_x", c))
                        dve.wait_ge(*after("fin1_x", c))
                        ts(H[:, c, META:T2], nt[:, c % 2, 0:SEQ], fin_g[:, 0, c:c + 1], ALU.mult).then_inc(*done("fin1", c))
                    dve.wait_ge(*after("vec_made", 0))
                    for b, (lo, hi) in enumerate(((0, 512), (512, VLEN))):
                        i = tt(vec[0:12, lo:hi], aux[1 + b][0:12, 0:hi - lo], oneh[0:12, 1, lo:hi], ALU.add)
                        i.then_inc(*(done("vec_ready", 0) if b else done("vec_part", 0)))
                    dve.wait_ge(*after("meta_in", 0))
                dve.wait_ge(*after("lam_in", layer))
                for j in range(2):
                    if j:
                        dve.wait_ge(*after("lam_sum", (layer, 0)))
                    dve.tensor_tensor_reduce(small[:, 64:96], lamp[:, 64 * j:64 * j + 32], lamp[:, 64 * j + 32:64 * j + 64],
                                             1.0, 0.0, ALU.mult, ALU.add, small[:, 24 + j:25 + j])\
                        .then_inc(*done("lam_sum", (layer, j)))
                lam_i = lambda_init(layer)
                dve.wait_ge(*after("lam_exp", layer))
                tt(small[:, 30:31], small[:, 29:30], small[:, 28:29], ALU.subtract).then_inc(*done("lam_part", (layer, 2)))
                dve.wait_ge(*after("lam_part", (layer, 2)))
                ts(small[:, 31:32], small[:, 30:31], lam_i, ALU.subtract).then_inc(*done("lam_part", (layer, 3)))
                a = PRM2["dnorm"][0]
                ts(prm2[:, layer, a:a + 1], prm2[:, layer, a:a + 1], 1.0 - lam_i, ALU.mult).then_inc(*done("lam_part", (layer, 4)))
                a = PRM2["rnorm"][0]
                ts(prm2[:, layer, a:a + 2], prm2[:, layer, a:a + 2], 0.5, ALU.mult).then_inc(*done("lam_part", (layer, 5)))
                dve.wait_ge(*after("wi_hi", layer))
                tt(wi_w[:, 1, :, :], wi_r[:, :, :], wi_w[:, 0, :, :].bitcast(F32), ALU.subtract).then_inc(*done("wi_lo", layer))

                def gain(name):
                    return lambda c: ts(nr[:, c % 2, 0:T2], nt[:, c % 2, 0:T2], par2(layer, name, c), ALU.mult)
                norm((layer, 3), H, T2, u_hi, u_lo, gain("nmix"))
                for step in L2_STEPS:
                    kind, k = step
                    if kind == "wi":
                        dve.wait_ge(*after("wi_made", layer))
                        ts(wis, aux[2][:, 0:16], IDX_HEADS ** -0.5 * 64 ** -0.5, ALU.mult).then_inc(*done("wi_out", layer))
                        if layer == 0:
                            dve.wait_ge(*after("tab2_in", 1))
                        dve.wait_ge(*after("wi_out", layer))
                    elif kind == "index":
                        for h in range(IDX_HEADS):
                            dve.wait_ge(*after("index_relu", (layer, h)))
                            for t, (lo, n) in enumerate(((S1, N1), (S2, N2))):
                                w = wis[:, 8 * t + h:8 * t + h + 1]
                                src = relu2[:, h % 2, lo:lo + n]
                                if h == 0:
                                    i = ts(score[:, lo:lo + n], src, w, ALU.mult)
                                else:
                                    if t == 0:
                                        dve.wait_ge(*after("index_sum", (layer, h - 1)))
                                    i = stt(score[:, lo:lo + n], src, w, score[:, lo:lo + n], ALU.mult, ALU.add)
                                i.then_inc(*(done("index_sum", (layer, h)) if t else done("index_part", (layer, h))))
                        dve.wait_ge(*after("index_sum", (layer, IDX_HEADS - 1)))
                        tt(score[:, :], score[:, :], causal, ALU.add).then_inc(*done("top", (layer, 0)))
                        dve.wait_ge(*after("top", (layer, 0)))
                        for r in range(TOPK // 8):
                            for t, (lo, n) in enumerate(((S1, N1), (S2, N2))):
                                dve.max(small[:, 48 + 8 * t:56 + 8 * t], score[:, lo:lo + n]).then_inc(*done("top", (layer, 1, r, t)))
                            for t, (lo, n) in enumerate(((S1, N1), (S2, N2))):
                                dve.wait_ge(*after("top", (layer, 1, r, t)))
                                dve.match_replace(score[:, lo:lo + n], small[:, 48 + 8 * t:56 + 8 * t], score[:, lo:lo + n], TAKEN)\
                                    .then_inc(*done("top", (layer, 2, r, t)))
                            dve.wait_ge(*after("top", (layer, 2, r, 1)))
                        ts(nsel[:, :], score[:, :], TAKEN / 2, ALU.is_gt, NEG, ALU.mult).then_inc(*done("selected", layer))
                        dve.wait_ge(*after("selected", layer))
                    elif kind == "slab":
                        if QCR < k <= QB:
                            c = k - 1
                            src = pj[:, c, :]
                            dve.wait_ge(*after("rope2_turn", (layer, c)))
                            tt(nt[:, c % 2, 0:T2], aux[1][:, 0:T2], sin2, ALU.mult).then_inc(*done("rope2_part", (layer, c)))
                            tt(src, src, cos2, ALU.mult).then_inc(*done("rope2_cos", (layer, c)))
                            dve.wait_ge(*after("rope2_part", (layer, c)))
                            dve.wait_ge(*after("rope2_cos", (layer, c)))
                            tt(src, src, nt[:, c % 2, 0:T2], ALU.add).then_inc(*done("rope2_out", (layer, c)))
                        if k >= GC:
                            dve.wait_ge(*after("p2_out", (layer, k)))
                            stt(pj[:, k, :], nt[:, k % 2, 0:T2], 1.0, lin[l2_bank(step)][:, 0:T2], ALU.add, ALU.mult)\
                                .then_inc(*done("gate2", (layer, k)))
                    elif kind == "c":
                        if k == 0 and layer == 0:
                            dve.wait_ge(*after("tab2_in", 1))
                        dve.wait_ge(*after("score2", (layer, kind, k, 0)))
                        if k:
                            dve.wait_ge(*after("pv2", (layer, kind, k - 1)))
                        tt(pt0[0:META, 0, :], aux[0][0:META, 0:T2], decay0[0:META, k, :], ALU.mult).then_inc(*done("pt2c", (layer, k, 0)))
                        tt(pt1[:, 0, :], aux[1][:, 0:384], decay1[:, k, :], ALU.mult).then_inc(*done("pt2c", (layer, k, 1)))
                    elif kind in ("a", "b"):
                        comps = (0, 1) if kind == "b" else (0,)
                        hh = k if kind == "a" else A_HEADS + k
                        if kind == "b" and k == 0 and layer == 0:
                            dve.wait_ge(*after("bias2_in", 2))
                        for c in comps:
                            s = aux[c][:, 0:S_ALL]
                            dve.wait_ge(*after("score2", (layer, kind, k, c)))
                            tt(s, s, bias2[:, hh, :], ALU.add).then_inc(*done("biased2", (layer, kind, k, c)))
                            dve.wait_ge(*after("biased2", (layer, kind, k, c)))
                            if kind == "a":
                                tt(s[:, 0:N1 + N2], s[:, 0:N1 + N2], nsel[:, :], ALU.add).then_inc(*done("chosen2", (layer, k)))
                                dve.wait_ge(*after("chosen2", (layer, k)))
                            for t, (lo, n) in enumerate(((S1, N1), (S2, N2), (S0, N0))):
                                dve.tensor_reduce(small[:, 3 * c + t:3 * c + t + 1], aux[c][:, lo:lo + n], AXX, ALU.max, negate=True)\
                                    .then_inc(*done("max2", (layer, kind, k, c, t)))
                        nc_ = 3 * len(comps)
                        dve.wait_ge(*after("exp2", (layer, kind, k, comps[-1], 2)))
                        dve.reciprocal(small[:, 16:16 + nc_], small[:, 8:8 + nc_]).then_inc(*done("recip2", (layer, kind, k)))
                        dve.wait_ge(*after("recip2", (layer, kind, k)))
                        if kind == "b":
                            ts(small[:, 19:22], small[:, 19:22], small[:, 31:32], ALU.mult).then_inc(*done("recip2b", (layer, k)))
                            dve.wait_ge(*after("recip2b", (layer, k)))
                        for t, (lo, n) in enumerate(((S1, N1), (S2, N2), (S0, N0))):
                            pr = p2[:, 0, lo:lo + n]
                            i = ts(pr, pr, small[:, 16 + t:17 + t], ALU.mult)
                            if kind == "b":
                                i.then_inc(*done("prob2b", (layer, k, t)))
                            else:
                                i.then_inc(*(done("prob2", (layer, kind, k)) if t == 2 else done("prob2a", (layer, k, t))))
                        if kind == "b":
                            for t, (lo, n) in enumerate(((S1, N1), (S2, N2), (S0, N0))):
                                dve.wait_ge(*after("prob2b", (layer, k, t)))
                                i = stt(p2[:, 0, lo:lo + n], p2[:, 1, lo:lo + n], small[:, 19 + t:20 + t], p2[:, 0, lo:lo + n],
                                        ALU.mult, ALU.add)
                                i.then_inc(*(done("prob2", (layer, kind, k)) if t == 2 else done("prob2c", (layer, k, t))))
                        else:
                            r = slice((k % 2) * HD, (k % 2) * HD + HD)
                            dve.wait_ge(*after("unit_out", (layer, kind, k)))
                            tt(o_lo[r, k // 2, :], aux[3][r, 0:T2], o_hi[r, k // 2, :].bitcast(F32), ALU.subtract)\
                                .then_inc(*done("unit_lo", (layer, k)))
                    elif kind == "bcnorm":
                        def bc_rest(c):
                            dve.wait_ge(*after("bc_hi", (layer, c)))
                            tt(o_lo[:, 4 + c, :], nr[:, c % 2, 0:T2], o_hi[:, 4 + c, :].bitcast(F32), ALU.subtract)\
                                .then_inc(*done("bc_lo", (layer, c)))
                        for c in range(4):
                            inverse(bc_r[:, c, :], "bc_root", "bc_rinv", (layer, c))
                            tt(nt[:, c % 2, 0:T2], bc_raw[:, c, :], bc_r[:, c, :], ALU.mult).then_inc(*done("bc_x", (layer, c)))
                            dve.wait_ge(*after("bc_x", (layer, c)))
                            if c < 2:
                                i = ts(nr[:, c % 2, 0:T2], nt[:, c % 2, 0:T2], par2(layer, "dnorm", 0), ALU.mult)
                            else:
                                i = stt(nr[:, c % 2, 0:T2], nt[:, c % 2, 0:T2], par2(layer, "rnorm", c - 2), pj[:, GC + c - 2, :],
                                        ALU.mult, ALU.mult)
                            i.then_inc(*done("bc_normed", (layer, c)))
                            if c:
                                bc_rest(c - 1)
                        bc_rest(3)
                for m in range(DC):
                    dve.wait_ge(*after("chunk", (layer, "mix2", m)))
                    tt(H[:, m, :], lin[m % 4][:, 0:T2], H[:, m, :], ALU.add).then_inc(*done("mix2_out", (layer, m)))
                norm((layer, 4), H, T2, u_hi, u_lo, gain("nff"))
                base = FF2_C * layer

                def ff1(j, b, it=None):
                    plus = 0 if it is None else it * 8
                    dve.wait_ge(sem("ff1_relu"), base + j + 1 + plus)
                    dst = ff2a[:, j, :] if it is None else ff2a[:, bass.ds(j + plus, 1), :].rearrange("p a t -> p (a t)")
                    t_ = up_t[:, b % 2, 0:T2]
                    tt(dst, t_, t_, ALU.mult).then_inc(*done("ff1_out", (layer, j)))
                for j in range(8):
                    ff1(j, j)
                with dve.Fori(0, 3) as it:
                    for b in range(8):
                        ff1(8 + b, b, it)
                again("ff1_out", 16)
                seen["ff1_all", layer] = counts["ff1_out"]

                def ff2(j, b, it=None):
                    plus = 0 if it is None else it * 8
                    dve.wait_ge(sem("ff2_hi"), base + j + 1 + plus)
                    src = ff2a[:, j, :] if it is None else ff2a[:, bass.ds(j + plus, 1), :].rearrange("p a t -> p (a t)")
                    tt(dn_lo[:, j % 2, 0:T2], src, dn_hi[:, j % 2, 0:T2].bitcast(F32), ALU.subtract)\
                        .then_inc(*done("ff2_lo", (layer, j)))
                for j in range(7):
                    ff2(j, j)
                with dve.Fori(0, 3) as it:
                    for b in range(8):
                        ff2(7 + b, b, it)
                again("ff2_lo", 16)
                ff2(FF2_C - 1, 0)
                dve.wait_ge(*after("chunk", (layer, "ff2")))
                for m in range(DC):
                    tt(H[:, m, :], bank[m][:, 0:T2], H[:, m, :], ALU.add).then_inc(*done("ff2_out", (layer, m)))

            wis = small[:, 32:48]
            dve.wait_ge(*after("prm_in", 0))
            for layer in range(DEPTH):
                modulation(layer)
            dve.wait_ge(*after("mod_ready", DEPTH - 1))
            for layer in range(DEPTH):
                network1(layer)
            for layer in range(DEPTH):
                network2(layer)
            tag = ("fin", 2)
            inverse(rinv[:, 0:T2], "norm_root", "norm_rinv", tag)
            for c in range(DC):
                tt(nt[:, c % 2, 0:SEQ], H[:, c, META:T2], rinv[:, META:T2], ALU.mult).then_inc(*done("fin2_x", c))
                dve.wait_ge(*after("fin2_x", c))
                if c >= 2:
                    dve.wait_ge(*after(f"stored{c % 2}", c - 2))
                ts(nr[:, c % 2, 0:SEQ], nt[:, c % 2, 0:SEQ], fin_g[:, 1, c:c + 1], ALU.mult).then_inc(*done("out_ready", c))
    return seen


def shape_tables():
    t = np.zeros((P, TAB_N), np.float32)

    def put(name, v):
        a, b = TAB[name]
        t[:v.shape[0], a:b] = v
    i = np.arange(P)
    put("ident", np.eye(P))
    put("ones_d", np.full((P, P), 1 / D))
    put("ones_c", np.full((P, P), 1 / (CONV_C * P)))
    put("ones_h", (i[:, None] // HD == i[None, :] // HD) / HD)
    for name, half in (("perm1", 16), ("perm2", 32)):
        m = np.zeros((P, P))
        for j in range(P):
            low = j % (2 * half) < half
            m[j + half if low else j - half, j] = -1 if low else 1
        put(name, m)
    sel = np.zeros((P, 2))
    for g in range(4):
        for s in range(2):
            sel[32 * g + s, s] = 1
    put("sel", sel)
    f = np.float32
    pos = np.arange(SEQ)
    inv = (f(10000.0) ** (-np.arange(0, 32, 2, dtype=f) / f(32))).astype(f)
    ang = np.zeros((P, SEQ), f)
    for j in range(P):
        d = j % HD
        where = pos // GRID_W if d < 32 else pos % GRID_W
        ang[j] = where.astype(f) * inv[d % 16]
    put("cos1", np.cos(ang))
    put("sin1", np.sin(ang))
    q, k = np.arange(GRID_W)[:, None], np.arange(GRID_W)[None, :]
    start = np.clip(q - 8, 0, GRID_W - 16)
    w = np.where((k >= start) & (k < start + 16), 0.0, NEG)
    put("win", np.concatenate([w, w]))
    inv = (f(10000.0) ** (-np.arange(0, 64, 2, dtype=f) / f(64))).astype(f)
    ang = inv[(i % HD) % 32][:, None] * np.arange(T2, dtype=f)[None, :]
    put("cos2", np.cos(ang))
    put("sin2", np.sin(ang))
    c = np.zeros((P, N1 + N2))
    c[:, :N1] = np.where(np.arange(N1)[None] <= META + i[:, None], 0, NEG)
    c[:, N1:] = np.where(np.arange(N2)[None] <= META + P + i[:, None], 0, NEG)
    put("causal", c)
    lg = np.log1p(-np.exp2(-5.0 - np.arange(C_HEADS)))

    def decay(keys, queries):
        d = queries[None, None, :] - keys[:, None, None]
        return np.where(d >= 0, np.exp(lg[None, :, None] * np.maximum(d, 0)), 0.0)
    d1 = np.concatenate([decay(META + i, np.arange(META, T2)), decay(META + P + i, np.arange(META + P, T2))], axis=2)
    put("decay1", d1.reshape(P, -1))
    put("decay0", decay(np.arange(META), np.arange(T2)).reshape(META, -1))
    dist = T2 - 1 - np.arange(VLEN)
    n = np.maximum(dist, 0)
    large = 16 + (np.log(np.maximum(n, 1).astype(f) / f(16)) / f(math.log(8)) * f(16)).astype(np.int32)
    bucket = np.where(n < 16, n, np.minimum(large, 31))
    put("onehot", (bucket[None, :] == np.arange(32)[:, None]) & (dist >= 0)[None, :])
    put("vmask", np.broadcast_to(np.where(dist >= 0, 0.0, NEG), (12, VLEN)))
    return t


def by_feature(v):
    v = v.reshape(*v.shape[:-1], -1, P)
    return np.moveaxis(v, -1, 0)


def weight_stream(w):
    slabs = []

    def tiles(m, c0):
        return m[:, c0:c0 + P].reshape(-1, P, P).transpose(1, 0, 2).reshape(P, -1)

    def wide(m):
        for q in range(m.shape[0] // (2 * P)):
            slabs.append(m[2 * P * q:2 * P * (q + 1)].reshape(2, P, 512).transpose(1, 0, 2).reshape(P, -1))
    for l in range(DEPTH):
        for n in range(12):
            wide(w["w_ada"][l][:, n * 512:(n + 1) * 512])
    for l in range(DEPTH):
        m = w["w_in"][l]
        for c in range(CONV_C):
            slabs += [tiles(m, 512 + c * P), tiles(m, c * P)]
        for c in range(2 * QC):
            slabs.append(tiles(m, 1024 + c * P))
        wide(m[:, 2048:2560])
        for c in range(DC):
            slabs += [tiles(m, 2560 + c * P), tiles(m, 2560 + D + c * P)]
        for c in range(DC):
            slabs.append(np.concatenate([tiles(w["w_conv_out"][l], c * P), tiles(w["w_na_out"][l], c * P)], axis=1))
        for c in range(DC):
            slabs.append(tiles(w["w_out"][l], c * P))
        for j in range(FF_C):
            slabs += [tiles(w["w_up"][l], j * P), tiles(w["w_up"][l], (FF_C + j) * P)]
        slabs += list(w["w_down"][l].reshape(FF_C, P, D))
    for l in range(DEPTH):
        m = w["w_in_2"][l]
        at = {"qa": 0, "ka": 512, "va": 1024, "qi": 1536, "ki": 2048, "qb": 2120, "kb": 2376, "vb": 2632,
              "qc": 2888, "kc": 3144, "vc": 3400, "gc": 3656}

        def feature(names):
            for name, n in names:
                for c in range(n):
                    slabs.append(tiles(m, at[name] + c * P))
        slabs.append(tiles(np.concatenate([m[:, 2048:2112]] * 2, axis=1), 0))
        feature([("qi", 4), ("qc", 2), ("kc", 2)])
        wide(np.concatenate([m[:, at["vb"]:at["vb"] + 256], m[:, at["vc"]:at["vc"] + 256]], axis=1))
        feature([("qb", 2), ("kb", 2), ("qa", 4), ("ka", 4), ("gc", 2)])
        wide(m[:, at["va"]:at["va"] + 512])
        for c in range(DC):
            slabs.append(tiles(w["w_out_2"][l], c * P))
        for c in range(FF2_C):
            slabs.append(tiles(w["w_ff1_2"][l], c * P))
        slabs += list(w["w_ff2_2"][l].reshape(FF2_C, P, D))
    return np.stack(slabs)


def kernel(**inputs):
    import concourse.bacc as bacc
    from concourse.bass_utils import run_bass_kernel_spmd as run

    w = {k: np.asarray(v) for k, v in inputs.items()}
    prm1, prm2 = [], []
    for l in range(DEPTH):
        dw = by_feature(w["conv_dw"][l]).transpose(0, 2, 1).reshape(P, -1)
        prm1.append(np.concatenate([
            by_feature(w["norm1_g"][l]), dw, by_feature(w["conv_dw_b"][l]), by_feature(w["conv_ln_g"][l]),
            by_feature(w["conv_ln_b"][l]), by_feature(w["norm2_g"][l]), by_feature(w["ffn_dw"][l]).reshape(P, -1),
            by_feature(w["ffn_dw_b"][l]), by_feature(w["b_ada"][l])], axis=1))
        dn = w["diff_norm_2"][l]
        prm2.append(np.concatenate([
            by_feature(w["norm_mix_2"][l]), np.concatenate([dn, dn])[:, None], by_feature(w["ret_norm_2"][l]),
            by_feature(w["norm_ff_2"][l])], axis=1))
    rpb = np.zeros((DEPTH, HEADS, 15, RPB_PAD), w["na_rpb"].dtype)
    rpb[..., 48:79] = w["na_rpb"]
    arrays = {
        "wstream": weight_stream(w),
        "tables": shape_tables(),
        "x_in": np.concatenate([by_feature(w["x"][0]).transpose(0, 2, 1), by_feature(w["ctx"][0]).transpose(0, 2, 1)], axis=2),
        "cvec": np.stack([by_feature(w["c"][0]), by_feature(w["c_ctx"])], axis=2),
        "prm1": np.stack(prm1, axis=1),
        "prm2": np.stack(prm2, axis=1),
        "fin_g": np.stack([by_feature(w["final_norm_g"]), by_feature(w["final_norm_2"])], axis=1),
        "rpb": rpb,
        "meta": by_feature(w["meta_2"]).transpose(0, 2, 1),
        "rel_bias": w["rel_bias_2"],
        "lam": w["diff_lambda_2"].reshape(DEPTH, P),
        "wi": w["w_in_2"][:, :, 2112:2120].reshape(DEPTH, DC, P, 8).transpose(0, 2, 1, 3),
    }
    arrays = {k: np.ascontiguousarray(v) for k, v in arrays.items()}

    def emit(marks):
        nc = bacc.Bacc("TRN2", target_bir_lowering=False, num_devices=1)
        args = {k: nc.dram_tensor(f"in_{k}", v.shape, mybir.dt.from_np(v.dtype), kind="ExternalInput").ap()
                for k, v in arrays.items()}
        out = nc.dram_tensor("out_x", (D, SEQ), F32, kind="ExternalOutput").ap()
        return nc, build(nc, args, out, marks)

    _, marks = emit({})
    nc, again = emit(marks)
    assert marks == again
    r = run(nc, [{f"in_{k}": v for k, v in arrays.items()}], core_ids=[0])
    return np.ascontiguousarray(r.results[0]["out_x"].T)[None]
```

```python
import math
from contextlib import ExitStack

import concourse.bass as bass
import numpy as np
from concourse import mybir

F32 = mybir.dt.float32
F32R = mybir.dt.float32r
ALU = mybir.AluOpType
ACT = mybir.ActivationFunctionType
AXX = mybir.AxisListType.X

P = 128
D = 1024
DC = D // P
SEQ = 256
CTX = 256
DEPTH = 2
EPS = 1e-6
NEG = -1e30
TAKEN = -3e38

GRID_W = 64
CONV_C = 512 // P
TAPS = 31
HALO = TAPS // 2
HEADS = 8
HD = 64
QC = HEADS * HD // P
FF_C = 2816 // P
RPB_PAD = 128
T_BOTH = SEQ + CTX

META = 16
T2 = SEQ + META
TOPK = 64
A_HEADS = 8
IDX_HEADS = 8
B_HEADS = 4
C_HEADS = 4
FF2_C = 4 * D // P
N1, N2, N0 = META + P, T2, META
S1, S2, S0 = 0, N1, N1 + N2
S_ALL = N1 + N2 + N0
VLEN = 544

TILE = P * P
SLAB = 8 * P
RING = 4
ADA_SLABS = 6 * DC
ADA_RING = 8
ADA_UNITS = DEPTH * 12
ADA_BUBBLE = 6
ADA_FIRST = 4
GLU_SLABS = 2 * CONV_C
QKV_V_SLABS = 4
L1_SLABS = GLU_SLABS + 2 * QC + QKV_V_SLABS + 2 * DC + DC + DC + 2 * FF_C + FF_C
L2_FRONT = 23
L2_SLABS = L2_FRONT + 8 + DC + FF2_C + FF2_C
N_SLABS = DEPTH * (L1_SLABS + L2_SLABS)

PRM1 = {}
_n = 0
for _name, _w in (("n1g", DC), ("dw", CONV_C * TAPS), ("dwb", CONV_C), ("lng", CONV_C), ("lnb", CONV_C),
                  ("n2g", DC), ("fdw", 3 * 2 * FF_C), ("fdwb", 2 * FF_C), ("bada", 6 * DC)):
    PRM1[_name] = (_n, _n + _w)
    _n += _w
PRM1_N = _n
PRM2 = {}
_n = 0
for _name, _w in (("nmix", DC), ("dnorm", 1), ("rnorm", 2), ("nff", DC)):
    PRM2[_name] = (_n, _n + _w)
    _n += _w
PRM2_N = _n
TAB = {}
_n = 0
for _name, _w in (("ident", P), ("ones_d", P), ("ones_c", P), ("ones_h", P), ("perm1", P), ("perm2", P),
                  ("sel", 2), ("cos1", SEQ), ("sin1", SEQ), ("win", GRID_W),
                  ("cos2", T2), ("sin2", T2), ("causal", N1 + N2), ("decay1", 4 * 384), ("decay0", 4 * T2),
                  ("onehot", VLEN), ("vmask", VLEN)):
    TAB[_name] = (_n, _n + _w)
    _n += _w
TAB_N = _n


def lambda_init(layer):
    return 0.8 - 0.6 * math.exp(-0.3 * layer)


def build(nc, A, out, marks):
    SAME = {"chunk": "slab_used", "up_all": "up_out", "down_done": "down_out", "ff1_all": "ff1_out"}
    GROUP = {n: "vector_part" for n in ("prm_half", "halo", "mod_part", "normed_part", "norm_lo_part", "down_part",
                                        "mix_part", "index_part", "prob2a", "vec_part")}
    seen = {}
    sems = {}
    counts = {}
    ctx = ExitStack()

    def sem(name):
        if name not in sems:
            sems[name] = ctx.enter_context(nc.semaphore(name))
            counts[name] = 0
        return sems[name]

    def done(name, key, by=1):
        s = sem(GROUP.get(name, name))
        counts[GROUP.get(name, name)] += by
        assert (name, key) not in seen, (name, key)
        seen[name, key] = counts[GROUP.get(name, name)]
        return s, by

    def again(name, n):
        counts[name] += n

    def after(name, key, plus=0):
        return sem(SAME.get(name, name)), marks.get((name, key), 1) + plus

    with ctx:
        top = [16512]

        def at(name, shape, dt, offset):
            t = nc.alloc_sbuf_tensor_at(name, [P, *shape], dt, offset=offset)
            return t[(slice(None),) * (len(shape) + 1)]

        def sb(name, shape, dt=F32):
            n = int(np.prod(shape)) * 4
            t = at(name, shape, dt, top[0])
            top[0] += -(-n // 32) * 32
            assert top[0] <= nc.sbuf_usable_end, name
            return t

        bank = [ctx.enter_context(nc.psum_tensor(f"bank{i}", [P, 512], F32)) for i in range(8)]
        lin, aux = bank[0:4], bank[4:8]

        raw = sb("raw", [RING, SLAB])
        w_hi = sb("w_hi", [RING, SLAB], F32R)
        w_lo = sb("w_lo", [RING, SLAB], F32R)
        cst = sb("cst", [6 * P + 2])
        prm = sb("prm", [DEPTH, PRM1_N])
        prm2 = sb("prm2", [DEPTH, PRM2_N])
        fin_g = sb("fin_g", [2, DC])
        cvec = sb("cvec", [DC, 2])
        cth = sb("cth", [DC, 2])
        mod = sb("mod", [DEPTH, 6 * DC, 2])
        a1 = sb("a1", [DEPTH, DC, 2])
        a2 = sb("a2", [DEPTH, DC, 2])
        gh = sb("gh", [DEPTH, 2, DC, 2])
        small = sb("small", [128])
        eps = sb("eps", [8])
        sq = sb("sq", [2, 512])
        nb = sb("nb", [4, 512])
        nt, nr = nb[:, 0:2, :], nb[:, 2:4, :]
        work = top[0]
        top[0] += 12288
        rinv = at("rinv", [512], F32, work + 10240)
        p_x = at("p_x", [2, 512], F32, work)
        p_c = at("p_c", [2, 256], F32, work + 4096)
        pt_x = at("pt_x", [4, 256], F32, work + 6144)
        pt_c = at("pt_c", [2, 256], F32, work + 10240)
        up_a = at("up_a", [2, 512], F32, work)
        up_g = at("up_g", [2, 512], F32, work + 4096)
        up_t = at("up_t", [2, 512], F32, work + 8192)
        glu_t = at("glu_t", [2, 512], F32, work)
        dn_hi = at("dn_hi", [2, 512], F32R, work)
        dn_lo = at("dn_lo", [2, 512], F32R, work + 4096)
        ada_part = at("ada_part", [2, 512], F32, work + 4096)
        p2 = at("p2", [3, S_ALL], F32, work)
        pt0 = at("pt0", [2, T2], F32, work + 5184)
        pt1 = at("pt1", [2, 384], F32, work + 7360)
        relu2 = at("relu2", [2, N1 + N2], F32, work + 5184)

        x_at = top[0]
        X = sb("X", [DC, T_BOTH])
        h_at = top[0]
        h_hi = sb("h_hi", [DC, T_BOTH], F32R)
        h_lo = sb("h_lo", [DC, T_BOTH], F32R)
        y_hi = at("y_hi", [DC, T_BOTH], F32R, h_at)
        y_lo = at("y_lo", [DC, T_BOTH], F32R, h_at + DC * T_BOTH * 4)
        g_at = top[0]
        gates = sb("gates", [2 * DC, T_BOTH])
        ada_raw = at("ada_raw", [ADA_RING, SLAB], F32, g_at)
        ffa = at("ffa", [FF_C, T_BOTH], F32, g_at)
        q_at = top[0]
        qT = sb("qT", [QC, T_BOTH])
        kT = sb("kT", [QC, T_BOTH])
        at_hi = at("at_hi", [QC, T_BOTH], F32R, q_at)
        at_lo = at("at_lo", [QC, T_BOTH], F32R, q_at + QC * T_BOTH * 4)
        V = sb("V", [4, 512])
        up_at = top[0]
        upad = sb("upad", [CONV_C, 2, SEQ + 2 * HALO])
        cv_at = top[0]
        cv = sb("cv", [CONV_C, T_BOTH])
        cv_hi = at("cv_hi", [CONV_C, T_BOTH], F32R, up_at)
        cv_lo = at("cv_lo", [CONV_C, T_BOTH], F32R, cv_at)
        biash = sb("biash", [2, 2, 256])
        cs = at("cs", [DC, 32], F32, top[0] - 2 * 2 * 256 * 4)
        tab1 = sb("tab1", [2 * SEQ + GRID_W])
        end1 = top[0]
        cos1, sin1, win = tab1[:, 0:SEQ], tab1[:, SEQ:2 * SEQ], tab1[:, 2 * SEQ:2 * SEQ + GRID_W]

        o = h_at
        u_hi = at("u_hi", [DC, T2], F32R, o)
        u_lo = at("u_lo", [DC, T2], F32R, o + DC * T2 * 4)
        H = at("H", [DC, T2], F32, o + 2 * DC * T2 * 4)
        decay0 = at("decay0", [4, T2], F32, o + 3 * DC * T2 * 4)
        assert 3 * DC * T2 * 4 + 4 * T2 * 4 <= 2 * DC * T_BOTH * 4
        tab2 = at("tab2", [2 * T2 + N1 + N2 + 4 * 384], F32, x_at)
        cos2, sin2, causal = tab2[:, 0:T2], tab2[:, T2:2 * T2], tab2[:, 2 * T2:2 * T2 + N1 + N2]
        decay1 = tab2[:, 2 * T2 + N1 + N2:].rearrange("p (h n) -> p h n", h=4)
        n_tab2 = 2 * T2 + N1 + N2 + 4 * 384
        score = at("score", [N1 + N2], F32, x_at + n_tab2 * 4)
        nsel = at("nsel", [N1 + N2], F32, x_at + (n_tab2 + N1 + N2) * 4)
        assert n_tab2 + 2 * (N1 + N2) <= DC * T_BOTH
        o = g_at
        pj = at("pj", [L2_FRONT, T2], F32, o)
        V2 = at("V2", [3, 1024], F32, o + L2_FRONT * T2 * 4)
        ff2a = at("ff2a", [FF2_C, T2], F32, o)
        o += (L2_FRONT * T2 + 3 * 1024) * 4
        assert FF2_C * T2 <= L2_FRONT * T2 + 3 * 1024
        o_hi = at("o_hi", [DC, T2], F32R, o)
        o_lo = at("o_lo", [DC, T2], F32R, o + DC * T2 * 4)
        o += 2 * DC * T2 * 4
        bias2 = at("bias2", [A_HEADS + B_HEADS, S_ALL], F32, o)
        o += (A_HEADS + B_HEADS) * S_ALL * 4
        wi_w = at("wi_w", [2, DC, 8], F32R, o)
        wi_r = at("wi_r", [DC, 8], F32, o + 512)
        lamp = at("lamp", [4 * 32], F32, o + 768)
        assert o + 1280 <= end1, (o, end1)
        KI, QI, QCR, KCR, QB, KB, QA, KA, GC = 0, 1, 5, 7, 9, 11, 13, 17, 21
        bc_raw = pj[:, QI:QI + 4, :]
        bc_r = pj[:, QCR:QCR + 4, :]
        vec = at("vec", [VLEN], F32, cv_at)
        oneh = at("oneh", [2, VLEN], F32, cv_at + VLEN * 4)
        relb = at("relb", [A_HEADS + B_HEADS], F32, cv_at + 3 * VLEN * 4)

        wis, lam = small[:, 32:48], small[:, 96:104]
        ident = cst[:, 0:P]
        ones_d, ones_c, ones_h = (cst[:, i * P:(i + 1) * P] for i in (1, 2, 3))
        perm1, perm2, sel = cst[:, 4 * P:5 * P], cst[:, 5 * P:6 * P], cst[:, 6 * P:6 * P + 2]
        by_distance = nc.dram_tensor("bias_by_distance", (A_HEADS + B_HEADS, P, VLEN), F32).ap()
        by_offset = nc.dram_tensor("rpb_by_offset", (DEPTH, HEADS, 7, GRID_W, RPB_PAD), F32).ap()

        def par(layer, name, c=None, plus=0):
            a, b = PRM1[name]
            if c is None:
                return prm[:, layer, a:b]
            return prm[:, layer, a + c:a + c + 1] if type(plus) is int else prm[:, layer, bass.ds(a + c + plus, 1)]

        def par2(layer, name, c):
            return prm2[:, layer, PRM2[name][0] + c:PRM2[name][0] + c + 1]

        first = {}
        n = 0
        for kind, size in (("l1", L1_SLABS), ("l2", L2_SLABS)):
            for layer in range(DEPTH):
                first[kind, layer] = n
                n += size
        assert n == N_SLABS

        def streams(ap, layer, lo=0, hi=SEQ):
            n = 2 if layer == 0 else 1
            return ap[:, 0:n * SEQ].rearrange("p (s t) -> p s t", s=n)[:, :, lo:hi]

        def n_tok(layer):
            return T_BOTH if layer == 0 else SEQ

        def parts(layer):
            return [(s, slice(s * SEQ, (s + 1) * SEQ)) for s in range(2 if layer == 0 else 1)]

        UNITS = [("a", h, 0) for h in range(A_HEADS)] + [("c", h, 0) for h in range(C_HEADS)]
        UNITS += [("b", h, c) for h in range(B_HEADS) for c in range(2)]
        N_UNITS = len(UNITS)

        def unit_steps(t, slab=None):
            steps = []
            if t < N_UNITS:
                steps.append(("S", t))
            if 0 <= t - 2:
                steps.append(("V", t - 2))
            if slab:
                steps.append(slab)
            if 0 <= t - 1 < N_UNITS:
                steps.append(("T", t - 1))
            return steps
        L2_PLAN = [("slab", c) for c in range(KI, QCR)] + [("wi", 0)]
        for h, c in enumerate(range(QA, GC)):
            L2_PLAN += [("slab", c), ("index", h)]
        for q in range(4):
            L2_PLAN += [("vals", 0, q), ("top", 2 * q), ("top", 2 * q + 1)]
        L2_PLAN += [("slab", c) for c in range(QCR, QB)]
        beside = [("vals", 1, q) for q in range(4)] + [("slab", c) for c in range(QB, QA)]
        beside += [None, ("slab", GC), None, ("slab", GC + 1)]
        for t in range(N_UNITS + 2):
            L2_PLAN += unit_steps(t, beside[t] if t < len(beside) else None)
        L2_AT = {}
        for st in L2_PLAN:
            if st[0] in ("slab", "vals"):
                L2_AT[st] = len(L2_AT)
        assert len(L2_AT) == L2_FRONT + 8
        TILES = ((S1, N1), (S2, N2), (S0, N0))

        def has_values(t):
            return UNITS[t][0::2] != ("b", 0)

        def l2_bank(step):
            at_ = L2_AT[step[0], step[1], 0] if step[0] == "vals" else L2_AT[step]
            return at_ % 4

        block = ctx.enter_context(nc.Block())

        @block.sync
        def _(sp):
            def load(i, it=None):
                plus = 0 if it is None else it * 8
                if i >= RING:
                    sp.wait_ge(sem("w_lo_ready"), i - RING + 1 + plus)
                src = A["wstream"][i] if it is None else A["wstream"][bass.ds(i + plus, 1)].rearrange("a p n -> (a p) n")
                sp.dma_start(raw[:, i % RING, :], src).then_inc(sem(f"slab_landed{i % RING}"), 16)

            def load_ada(u):
                for a in range(4 * u, 4 * u + 4):
                    if a >= ADA_RING:
                        sp.wait_ge(sem("ada_slab_read"), a - ADA_RING + 1)
                    sp.dma_start(ada_raw[:, a % ADA_RING, :], A["wada"][a]).then_inc(sem(f"ada_landed{a % ADA_RING}"), 16)

            for u in range(ADA_FIRST):
                load_ada(u)
            for i in range(RING):
                load(i)
            for u in range(ADA_FIRST, ADA_BUBBLE):
                load_ada(u)
            for i in range(ADA_UNITS - ADA_BUBBLE):
                load_ada(ADA_BUBBLE + i)
                load(RING + i)
            start = RING + ADA_UNITS - ADA_BUBBLE
            reps = (N_SLABS - start) // 8
            with sp.Fori(0, reps) as it:
                for b in range(8):
                    load(start + b, it)
            for i in range(start + reps * 8, N_SLABS):
                load(i)
            for c in range(DC):
                sp.wait_ge(*after("out_ready", c))
                sp.dma_start(out[c * P:(c + 1) * P, :], nb[:, c % 4, 0:SEQ]).then_inc(*done(f"stored{c % 4}", c, 16))
            for c in range(DC - 4, DC):
                sp.wait_ge(*after(f"stored{c % 4}", c))

        def ada_landed(a):
            return sem(f"ada_landed{a % ADA_RING}"), 16 * (a // ADA_RING + 1)

        def landed(i):
            return sem(f"slab_landed{i % RING}"), 16 * (i // RING + 1)

        @block.gpsimd
        def _(pool):
            def rest(q, it=None):
                plus = 0 if it is None else it * 8
                pool.wait_ge(sem("w_hi_ready"), q + 1 + plus)
                s = q % RING
                pool.tensor_tensor(w_lo[:, s, :], raw[:, s, :], w_hi[:, s, :].bitcast(F32), ALU.subtract)\
                    .then_inc(sem("w_lo_ready"), 1)

            reps = N_SLABS // 8
            with pool.Fori(0, reps) as it:
                for b in range(8):
                    rest(b, it)
            for q in range(reps * 8, N_SLABS):
                rest(q)

        @block.scalar
        def _(act):
            nxt = [0]
            summed_slab = [0]

            def round_weights(q, it=None):
                i, s = q, q % RING
                a, n = landed(i)
                act.wait_ge(a, n + (0 if it is None else it * (8 // RING) * 16))
                if q >= RING:
                    act.wait_ge(sem("slab_used"), q - RING + 1 + (0 if it is None else it * 8))
                act.activation(w_hi[:, s, :], raw[:, s, :], ACT.Copy).then_inc(sem("w_hi_ready"), 1)

            def ahead(i):
                while nxt[0] <= min(i + RING - 1, N_SLABS - 1):
                    round_weights(nxt[0])
                    nxt[0] += 1

            def copy(dst, src, **kw):
                return act.activation(dst, src, ACT.Copy, **kw)

            tb = A["tables"]
            act.dma_start(cst[:, :], tb[:, TAB["ident"][0]:TAB["sel"][1]]).then_inc(*done("const_in", 0, 16))
            act.dma_start(cvec[:, :, :], A["cvec"]).then_inc(*done("const_in", 1, 16))
            act.dma_start(X[:, :, :], A["x_in"]).then_inc(*done("x_in", 0, 16))
            act.dma_start(prm[:, :, :], A["prm1"]).then_inc(*done("prm_in", 0, 16))
            act.dma_start(tab1[:, :], tb[:, TAB["cos1"][0]:TAB["win"][1]]).then_inc(*done("tab1_in", 0, 16))
            act.dma_start(prm2[:, :, :], A["prm2"]).then_inc(*done("const2_in", 0, 16))
            act.dma_start(fin_g[:, :, :], A["fin_g"]).then_inc(*done("const2_in", 1, 16))
            act.dma_start(oneh[0:32, 0, :], tb[0:32, TAB["onehot"][0]:TAB["onehot"][1]]).then_inc(*done("vec_in", 0, 16))
            act.dma_start(oneh[0:12, 1, :], tb[0:12, TAB["vmask"][0]:TAB["vmask"][1]]).then_inc(*done("vec_in", 1, 16))
            act.dma_start(relb[0:32, :], A["rel_bias"]).then_inc(*done("vec_in", 2, 16))
            for layer in range(DEPTH):
                for h in range(HEADS):
                    off = ((layer * HEADS + h) * 15 + 4) * RPB_PAD
                    src = bass.AP(A["rpb"].tensor, off, [[RPB_PAD, 7], [0, GRID_W], [1, RPB_PAD]])
                    act.dma_start(by_offset[layer, h], src).then_inc(*done(f"rpb_rows{layer}", h, 16))
            act.wait_ge(*after("const_in", 1))
            act.activation(cth[:, :, :], cvec[:, :, :], ACT.Tanh, scale=0.5).then_inc(*done("c_tanh", 0))

            def ada_copy(u):
                act.wait_ge(sem("ada_slab_read"), 4 * (u + 1))
                if u >= 2:
                    act.wait_ge(*after("ada_turned", u - 2))
                copy(ada_part[:, u % 2, :], aux[2 + u % 2][:, :]).then_inc(*done("ada_part_out", u))

            def load_bias(layer, h):
                for t in range(2):
                    for r in range(2):
                        off = ((layer * HEADS + h) * 7 + 3 - (2 * t + r)) * GRID_W * RPB_PAD + GRID_W - 1
                        src = bass.AP(by_offset.tensor, off, [[RPB_PAD - 1, GRID_W], [GRID_W * RPB_PAD, 4], [1, GRID_W]])
                        act.dma_start(biash[r * GRID_W:(r + 1) * GRID_W, h % 2, t, :]
                                      .rearrange("p (a b) -> p a b", a=4), src)\
                            .then_inc(*done(f"bias_in{h % 2}", (layer, h, t, r), 16))

            def root(dst, mean, name, key):
                act.activation(dst, mean, ACT.Sqrt, bias=eps[:, 0:1]).then_inc(*done(name, key))

            def norm(tag, X_, T, k_ready, summed=True):
                for c in range(DC):
                    if not summed:
                        ahead(summed_slab[0] + c)
                    if k_ready:
                        act.wait_ge(*after(*k_ready(c)))
                    if c >= (2 if summed else 3):
                        act.wait_ge(*after("norm_summed" if summed else "norm_added", (tag, c - 2)))
                    dst = rinv[:, 0:T] if not summed and c == 0 else sq[:, c % 2, 0:T]
                    act.activation(dst, X_[:, c, 0:T], ACT.Square).then_inc(*done("norm_sq", (tag, c)))
                act.wait_ge(*after("norm_summed", (tag, DC - 1)))
                root(rinv[:, 0:T], aux[0][:, 0:T], "norm_root", tag)

            def norm_round(tag, hi, shift, streams_):
                for c in range(DC):
                    act.wait_ge(*after("normed", (tag, c)))
                    for st, cols in streams_:
                        if shift is None:
                            i = copy(hi[:, c, cols], nb[:, c % 4, cols])
                        else:
                            i = act.activation(hi[:, c, cols], nb[:, c % 4, cols], ACT.Identity, bias=shift(c, st))
                        i.then_inc(*(done("norm_hi", (tag, c)) if st == streams_[-1][0] else done("norm_hi_part", (tag, c, st))))

            def network1(layer):
                T = n_tok(layer)
                first_slab = first["l1", layer]
                def shift(row):
                    return lambda c, st: mod[:, layer, row + c, st:st + 1]
                if layer == 0:
                    act.wait_ge(*after("x_in", 0))
                    act.wait_ge(*after("eps_set", 0))
                norm((layer, 1), X, T_BOTH, None if layer == 0 else lambda c: ("down_out", (layer - 1, c)))
                if layer == 0:
                    for u in range(ADA_FIRST):
                        ada_copy(u)
                ahead(first_slab)
                if layer == 0:
                    act.wait_ge(*after("ada_mod", ADA_FIRST - 1))
                norm_round((layer, 1), h_hi, shift(0), parts(0))
                if layer == 0:
                    for u in range(ADA_FIRST, ADA_BUBBLE):
                        ada_copy(u)
                    act.wait_ge(*after("vec_ready", 0))
                    act.dma_start(by_distance, vec[0:12, :].unsqueeze(1).to_broadcast((12, P, VLEN)))\
                        .then_inc(*done("vec_out", 0, 16))

                def ada_here(i):
                    if layer == 0 and i < ADA_UNITS - ADA_BUBBLE:
                        ada_copy(ADA_BUBBLE + i)
                s = first_slab
                for c in range(CONV_C):
                    ahead(s)
                    act.wait_ge(*after("chunk", (layer, "glu_g", c)))
                    if c >= 2:
                        act.wait_ge(*after("glu_out", (layer, c - 2)))
                    act.activation(glu_t[:, c % 2, 0:T], lin[(2 * c) % 4][:, 0:T], ACT.Tanh, scale=0.5)\
                        .then_inc(*done("glu_tanh", (layer, c)))
                    ada_here(2 * c)
                    ahead(s + 1)
                    ada_here(2 * c + 1)
                    s += 2
                for c in range(2 * QC):
                    ahead(s)
                    act.wait_ge(*after("chunk", (layer, "qk", c)))
                    Tq = T if c < QC else T_BOTH
                    dst = (qT[:, c, 0:Tq] if c < QC else kT[:, c - QC, 0:Tq])
                    copy(dst, lin[c % 4][:, 0:Tq], scale=HD ** -0.5 if c < QC else 1.0)\
                        .then_inc(*done("qk_out", (layer, c)))
                    ada_here(GLU_SLABS + c)
                    s += 1
                for q in range(QKV_V_SLABS):
                    ahead(s + q)
                    ada_here(GLU_SLABS + 2 * QC + q)
                for tt in range(4):
                    act.wait_ge(*after("chunk", (layer, "v", tt)))
                    copy(V[:, tt, :], lin[tt][:, :]).then_inc(*done("v_out", (layer, tt)))
                s += QKV_V_SLABS
                act.wait_ge(*after("glu_out", (layer, CONV_C - 1)))
                if layer > 0:
                    act.wait_ge(*after("attn_added", (layer - 1, HEADS - 1, 1)))
                act.wait_ge(*after(f"rpb_rows{layer}", HEADS - 1))
                load_bias(layer, 0)
                load_bias(layer, 1)
                for h in range(HEADS):
                    def gate(g):
                        ahead(s + g)
                        act.wait_ge(*after("chunk", (layer, "gate", g)))
                        act.activation(gates[:, g, 0:T], lin[g % 4][:, 0:T], ACT.Tanh, scale=0.5)\
                            .then_inc(*done("gate_out", (layer, g)))
                    for t in range(2):
                        act.wait_ge(*after("attn_max", (layer, h, t)))
                        act.activation(p_x[:, t, :], aux[t][:, :], ACT.Exp, bias=small[:, t:t + 1],
                                       accum_out=small[:, 8 + t:9 + t]).then_inc(*done("attn_exp", (layer, h, t)))
                    if layer == 0:
                        for t in range(2):
                            act.wait_ge(*after("attn_max", (layer, h, 3)))
                            act.activation(p_c[:, t, :], aux[2][:, t * 256:(t + 1) * 256], ACT.Exp,
                                           bias=small[:, 2 + t:3 + t], accum_out=small[:, 10 + t:11 + t])\
                                .then_inc(*done("attn_exp", (layer, h, 2 + t)))
                    if h + 2 < HEADS:
                        load_bias(layer, h + 2)
                    gate(2 * h)
                    if h:
                        act.wait_ge(*after("attn_pv", (layer, h - 1)))
                    for t in range(2):
                        act.wait_ge(*after("attn_turned", (layer, h, t)))
                        copy(pt_x[:, :, t * P:(t + 1) * P], aux[t][:, :].rearrange("p (k q) -> p k q", k=4))\
                            .then_inc(*done("attn_pt", (layer, h, t)))
                    if layer == 0:
                        act.wait_ge(*after("attn_turned", (layer, h, 2)))
                        copy(pt_c.rearrange("p k (t q) -> p t k q", t=2),
                             aux[2][:, :].rearrange("p (t k q) -> p t k q", t=2, k=2))\
                            .then_inc(*done("attn_pt", (layer, h, 2)))
                    gate(2 * h + 1)
                    act.wait_ge(*after("attn_pv", (layer, h)))
                    r = slice((h % 2) * HD, (h % 2) * HD + HD)
                    copy(at_hi[r, h // 2, 0:T], aux[3][r, 0:T]).then_inc(*done("attn_hi", (layer, h)))
                s += 2 * DC
                for c in range(CONV_C):
                    act.wait_ge(*after("conv_centred", (layer, c)))
                    if c >= 2:
                        act.wait_ge(*after("ln_var", (layer, c - 2)))
                    act.activation(sq[:, c % 2, 0:T], cv[:, c, 0:T], ACT.Square).then_inc(*done("ln_sq", (layer, c)))
                act.wait_ge(*after("ln_var", (layer, CONV_C - 1)))
                root(rinv[:, 0:T], aux[1][:, 0:T], "ln_root", layer)
                ahead(s)
                for c in range(CONV_C):
                    act.wait_ge(*after("conv_affine", (layer, c)))
                    act.activation(nt[:, c % 2, 0:T], nr[:, c % 2, 0:T], ACT.Tanh).then_inc(*done("conv_tanh", (layer, c)))
                    act.wait_ge(*after("conv_silu", (layer, c)))
                    copy(cv_hi[:, c, 0:T], sq[:, c % 2, 0:T]).then_inc(*done("conv_hi", (layer, c)))
                for m in range(DC):
                    ahead(s)
                    act.wait_ge(*after("merged", (layer, m)))
                    copy(y_hi[:, m, 0:T], nr[:, m % 2, 0:T]).then_inc(*done("merge_hi", (layer, m)))
                    s += 1
                summed_slab[0] = s
                s += DC
                norm((layer, 2), X, T, lambda c: ("mix_out", (layer, c)), summed=False)
                norm_round((layer, 2), h_hi, shift(3 * DC), parts(layer))

                def up(j, b, it=None):
                    plus = 0 if it is None else it * 4
                    for w, buf in enumerate((up_a, up_g)):
                        if it is None:
                            ahead(s + 2 * j + w)
                        else:
                            round_weights(nxt[0] + 2 * b + w, it)
                        act.wait_ge(sem("slab_used"), s + 2 * j + w + 1 + plus * 2)
                        if j >= 2 or it is not None:
                            act.wait_ge(sem("up_out"), base_up + j - 1 + plus)
                        cc = w * FF_C + j
                        wcol, bcol = par(layer, "fdw", 2 * FF_C + cc, plus), par(layer, "fdwb", cc, plus)
                        ps = lin[(2 * b + w) % 4]
                        act.activation(buf[:, b % 2, 0:T], ps[:, 0:T], ACT.Identity, bias=bcol, scale=wcol)\
                            .then_inc(*done("up_mid", (layer, j, w)))
                    act.wait_ge(sem("up_conv"), 2 * (base_up + j + 1) + plus * 2)
                    act.activation(up_t[:, b % 2, 0:T], up_g[:, b % 2, 0:T], ACT.Tanh)\
                        .then_inc(*done("up_tanh", (layer, j)))

                base_up = FF_C * layer
                for j in range(2):
                    up(j, j)
                up_first = nxt[0]
                with act.Fori(0, 5) as it:
                    for b in range(4):
                        up(2 + b, b, it)
                nxt[0] = up_first + 40
                again("up_mid", 4 * 2 * 4)
                again("up_tanh", 4 * 4)
                s += 2 * FF_C

                def down(j, b, it=None):
                    plus = 0 if it is None else it * 8
                    if it is not None or j >= 2:
                        act.wait_ge(sem("slab_used"), s + j - 1 + plus)
                    src = ffa[:, j, 0:T] if it is None else ffa[:, bass.ds(j + plus, 1), 0:T].rearrange("p a t -> p (a t)")
                    if j == 0:
                        act.wait_ge(*after("up_all", layer))
                    if j == 1 and layer == DEPTH - 1:
                        act.wait_ge(*after("vec_out", 0))
                        act.dma_start(H[:, :, 0:META], A["meta"]).then_inc(*done("meta_in", 0, 16))
                        act.dma_start(wi_r[:, :, :], A["wi"][0]).then_inc(*done("wi_in", 0, 16))
                        act.dma_start(lamp[:, :], A["lam"][0:1, :].to_broadcast((P, P))).then_inc(*done("lam_in", 0, 16))
                        act.dma_start(decay0[0:16, :, :], tb[0:16, TAB["decay0"][0]:TAB["decay0"][1]]
                                      .rearrange("p (h n) -> p h n", h=4)).then_inc(*done("tab2_in", 0, 16))
                        nh = A_HEADS + B_HEADS
                        for r, (lo, n, off) in enumerate(((S1, N1, T2 - 1 - META), (S2, N2, T2 - 1 - META - P), (S0, N0, T2 - 1))):
                            act.dma_start(bias2[:, :, lo:lo + n],
                                          bass.AP(by_distance.tensor, off, [[VLEN - 1, P], [P * VLEN, nh], [1, n]]))\
                                .then_inc(*done("bias2_in", r, 16))
                    copy(dn_hi[:, j % 2, 0:T], src).then_inc(*done("down_hi", (layer, j)))
                    if it is None:
                        ahead(s + j)
                    else:
                        round_weights(nxt[0] + b, it)
                for j in range(5):
                    down(j, j)
                dn_first = nxt[0]
                with act.Fori(0, 2) as it:
                    for b in range(8):
                        down(5 + b, b, it)
                nxt[0] = dn_first + 16
                again("down_hi", 8)
                down(FF_C - 1, 0)

            def network2(layer):
                s = first["l2", layer]
                tag = ("n2", layer)
                if layer == 0:
                    norm(("fin", 1), X, SEQ, lambda c: ("down_out", (1, c)))
                    for c in range(DC):
                        act.wait_ge(*after("fin1", c))
                    act.dma_start(tab2[:, :], tb[:, TAB["cos2"][0]:TAB["decay1"][1]]).then_inc(*done("tab2_in", 1, 16))
                    act.wait_ge(*after("meta_in", 0))
                    act.wait_ge(*after("wi_in", 0))
                else:
                    act.dma_start(lamp[:, :], A["lam"][layer:layer + 1, :].to_broadcast((P, P)))\
                        .then_inc(*done("lam_in", layer, 16))
                    act.wait_ge(*after("ff2_out", (0, DC - 1)))
                    act.dma_start(wi_r[:, :, :], A["wi"][layer]).then_inc(*done("wi_in", layer, 16))
                    act.wait_ge(*after("wi_in", layer))
                act.wait_ge(*after("lam_sum", (layer, 1)))
                act.activation(lam[:, 2:4], lam[:, 0:2], ACT.Exp).then_inc(*done("lam_exp", layer))
                copy(wi_w[:, 0, :, :], wi_r[:, :, :]).then_inc(*done("wi_hi", layer))
                norm((layer, 3), H, T2, None if layer == 0 else lambda c: ("ff2_out", (0, c)))
                ahead(s)
                both = [(0, slice(0, T2))]
                norm_round((layer, 3), u_hi, None, both)
                for step in L2_PLAN:
                    kind, k = step[0:2]
                    if kind == "slab":
                        c = k
                        ahead(s + L2_AT[step])
                        act.wait_ge(*after("chunk", (layer, "p2", c)))
                        ps = lin[l2_bank(step)][:, 0:T2]
                        if c >= GC:
                            act.activation(nt[:, c % 2, 0:T2], ps, ACT.Tanh, scale=0.5).then_inc(*done("p2_out", (layer, c)))
                        else:
                            scale = HD ** -0.5 if QA <= c < KA or KCR <= c < QB else 32 ** -0.5 if QB <= c < KB else 1.0
                            copy(pj[:, c, :], ps, scale=scale).then_inc(*done("p2_out", (layer, c)))
                    elif kind == "vals":
                        ahead(s + L2_AT[step])
                        if step[2] == 3:
                            for tt in range(3):
                                n = P if tt else META
                                act.wait_ge(*after("chunk", (layer, "v2", k, tt)))
                                copy(V2[0:n, tt, k * 512:(k + 1) * 512], lin[(l2_bank(step) + tt) % 4][0:n, :])\
                                    .then_inc(*done("v2_out", (layer, k, tt)))
                    elif kind == "index":
                        act.wait_ge(*after("index_dot", (layer, k)))
                        if k >= 2:
                            act.wait_ge(*after("index_sum", (layer, k - 2)))
                        act.activation(relu2[:, k % 2, :], aux[k % 2][:, 0:N1 + N2], ACT.Relu)\
                            .then_inc(*done("index_relu", (layer, k)))
                    elif kind == "S" and UNITS[k][0] != "c":
                        act.wait_ge(*after("max2", (layer, k, 2)))
                        if k >= 3:
                            act.wait_ge(*after("prob2", (layer, k - 2)))
                            if UNITS[k - 3][0] != "c" and UNITS[k - 3][0::2] != ("b", 0):
                                act.wait_ge(*after("turned2", (layer, k - 3)))
                        for t, (lo, n) in enumerate(TILES):
                            m = 3 * (k % 3) + t
                            act.activation(p2[:, k % 3, lo:lo + n], aux[k % 2][:, lo:lo + n], ACT.Exp,
                                           bias=small[:, m:m + 1], accum_out=small[:, 9 + m:10 + m])\
                                .then_inc(*done("exp2", (layer, k, t)))
                    elif kind == "T" and UNITS[k][0] != "c" and UNITS[k][0::2] != ("b", 0):
                        if k >= 2 and has_values(k - 2):
                            act.wait_ge(*after("pv2", (layer, k - 2)))
                        act.wait_ge(*after("turned2", (layer, k)))
                        copy(pt0[0:META, k % 2, :], aux[k % 2][0:META, 0:T2]).then_inc(*done("pt2", (layer, k, 0)))
                        copy(pt1[:, k % 2, :], aux[2][:, 0:384]).then_inc(*done("pt2", (layer, k, 1)))
                    elif kind == "V" and has_values(k):
                        name, h, _ = UNITS[k]
                        act.wait_ge(*after("pv2", (layer, k)))
                        r = slice((h % 2) * HD, (h % 2) * HD + HD)
                        if name == "a":
                            dst = o_hi[r, h // 2, :]
                        else:
                            dst = bc_raw[r, h // 2 + (2 if name == "c" else 0), :]
                        copy(dst, aux[3][r, 0:T2]).then_inc(*done("unit_out", (layer, k)))
                act.wait_ge(*after("unit_out", (layer, N_UNITS - 1)))
                for c in range(4):
                    if c >= 2:
                        act.wait_ge(*after("bc_summed", (layer, c - 2)))
                    act.activation(sq[:, c % 2, 0:T2], bc_raw[:, c, :], ACT.Square).then_inc(*done("bc_sq", (layer, c)))
                for c in range(4):
                    act.wait_ge(*after("bc_summed", (layer, c)))
                    root(bc_r[:, c, :], aux[c][:, 0:T2], "bc_root", (layer, c))
                for c in range(4):
                    act.wait_ge(*after("bc_normed", (layer, c)))
                    copy(o_hi[:, 4 + c, :], nr[:, c % 2, 0:T2]).then_inc(*done("bc_hi", (layer, c)))
                s += L2_FRONT + 8
                summed_slab[0] = s
                s += DC
                norm((layer, 4), H, T2, lambda c: ("mix2_out", (layer, c)), summed=False)
                norm_round((layer, 4), u_hi, None, both)

                def ff1(j, b, it=None):
                    plus = 0 if it is None else it * 8
                    if it is None:
                        ahead(s + j)
                    else:
                        round_weights(nxt[0] + b, it)
                    act.wait_ge(sem("slab_used"), s + j + 1 + plus)
                    if it is not None or j >= 2:
                        act.wait_ge(sem("ff1_out"), base + j - 1 + plus)
                    act.activation(up_t[:, b % 2, 0:T2], lin[b % 4][:, 0:T2], ACT.Relu).then_inc(*done("ff1_relu", (layer, j)))
                base = FF2_C * layer
                for j in range(8):
                    ff1(j, j)
                f1 = nxt[0]
                with act.Fori(0, 3) as it:
                    for b in range(8):
                        ff1(8 + b, b, it)
                nxt[0] = f1 + 24
                again("ff1_relu", 16)
                s += FF2_C

                def ff2(j, b, it=None):
                    plus = 0 if it is None else it * 8
                    if it is not None or j >= 2:
                        act.wait_ge(sem("slab_used"), s + j - 1 + plus)
                    src = ff2a[:, j, :] if it is None else ff2a[:, bass.ds(j + plus, 1), :].rearrange("p a t -> p (a t)")
                    if j == 0:
                        act.wait_ge(*after("ff1_all", layer))
                    copy(dn_hi[:, j % 2, 0:T2], src).then_inc(*done("ff2_hi", (layer, j)))
                    if it is None:
                        ahead(s + j)
                    else:
                        round_weights(nxt[0] + b, it)
                for j in range(7):
                    ff2(j, j)
                reps = 3 if layer == 0 else 2
                f2 = nxt[0]
                with act.Fori(0, reps) as it:
                    for b in range(8):
                        ff2(7 + b, b, it)
                nxt[0] = f2 + reps * 8
                again("ff2_hi", 8 * (reps - 1))
                for j in range(7 + reps * 8, FF2_C):
                    ff2(j, j)

            for layer in range(DEPTH):
                network1(layer)
            for layer in range(DEPTH):
                network2(layer)
            norm(("fin", 2), H, T2, lambda c: ("ff2_out", (1, c)))

        @block.tensor
        def _(pe):
            readers = {}

            def claim(b):
                if b in readers:
                    pe.wait_ge(*after(*readers.pop(b)))

            def weights(i, it=None):
                pe.wait_ge(sem("w_lo_ready"), i + 1 + (0 if it is None else it * 8))

            def three(o, i, k, a_hi, a_lo, start, stop, col=None):
                s = i % RING
                hi, lo = w_hi[:, s, k * P:(k + 1) * P], w_lo[:, s, k * P:(k + 1) * P]
                pe.matmul(o, hi, a_hi, start=start, stop=False)
                pe.matmul(o, hi, a_lo, start=False, stop=False)
                return pe.matmul(o, lo, a_hi, start=False, stop=stop)

            def chunk(i, b, T, a_hi, a_lo, key, reader, h_key=None):
                weights(i)
                claim(b)
                for k in range(DC):
                    if h_key:
                        pe.wait_ge(*after("norm_lo", (h_key, k)))
                    mm = three(bank[b][:, 0:T], i, k, a_hi[:, k, 0:T], a_lo[:, k, 0:T], k == 0, k == DC - 1)
                mm.then_inc(*done("slab_used", i))
                seen["chunk", key] = seen["slab_used", i]
                readers[b] = reader

            def norm_sum(tag, T, summed=True):
                claim(4)
                if not summed:
                    pe.wait_ge(*after("norm_added", (tag, DC - 1)))
                    pe.matmul(aux[0][:, 0:T], ones_d, rinv[:, 0:T], start=True, stop=True)\
                        .then_inc(*done("norm_summed", (tag, DC - 1)))
                for c in range(DC if summed else 0):
                    pe.wait_ge(*after("norm_sq", (tag, c)))
                    pe.matmul(aux[0][:, 0:T], ones_d, sq[:, c % 2, 0:T], start=c == 0, stop=c == DC - 1)\
                        .then_inc(*done("norm_summed", (tag, c)))
                readers[4] = ("norm_root", tag)

            def ada_turn(u):
                pe.wait_ge(*after("ada_part_out", u))
                for j in range(4):
                    mm = pe.matmul(aux[2 + u % 2][:, 2 * j:2 * j + 2], ada_part[:, u % 2, j * P:(j + 1) * P], sel,
                                   start=True, stop=True)
                mm.then_inc(*done("ada_turned", u))
                readers[6 + u % 2] = ("ada_mod", u)

            def ada(u):
                claim(6 + u % 2)
                for q in range(4):
                    a = 4 * u + q
                    pe.wait_ge(*ada_landed(a))
                    for j in range(2):
                        k = 2 * q + j
                        g = 32 * (k % 4)
                        mm = pe.matmul(aux[2 + u % 2][g:g + 32, :], cs[:, k, :], ada_raw[:, a % ADA_RING, j * 512:(j + 1) * 512],
                                       start=k < 4, stop=k >= 4, tile_position=(0, g))
                    mm.then_inc(*done("ada_slab_read", a))
                if u and u != ADA_FIRST:
                    ada_turn(u - 1)
                if u == ADA_FIRST - 1:
                    ada_turn(u)

            def network1(layer):
                T = n_tok(layer)
                norm_sum((layer, 1), T_BOTH)
                if layer == 0:
                    for u in range(ADA_BUBBLE):
                        ada(u)

                def ada_here(i):
                    if layer == 0 and i < ADA_UNITS - ADA_BUBBLE:
                        ada(ADA_BUBBLE + i)
                    elif layer == 0 and i == ADA_UNITS - ADA_BUBBLE:
                        ada_turn(ADA_UNITS - 1)
                s = first["l1", layer]
                for c in range(CONV_C):
                    chunk(s, (2 * c) % 4, T, h_hi, h_lo, (layer, "glu_g", c), ("glu_tanh", (layer, c)),
                          (layer, 1) if c == 0 else None)
                    ada_here(2 * c)
                    chunk(s + 1, (2 * c + 1) % 4, T, h_hi, h_lo, (layer, "glu_a", c), ("glu_out", (layer, c)))
                    ada_here(2 * c + 1)
                    s += 2
                for c in range(2 * QC):
                    Tq = T if c < QC else T_BOTH
                    chunk(s, c % 4, Tq, h_hi, h_lo, (layer, "qk", c), ("qk_out", (layer, c)))
                    if c:
                        rope(layer, c - 1)
                    ada_here(GLU_SLABS + c)
                    s += 1
                for q in range(QKV_V_SLABS):
                    weights(s)
                    for j in range(2):
                        k = 2 * q + j
                        wh, wl = (w[:, s % RING, j * 512:(j + 1) * 512] for w in (w_hi, w_lo))
                        for tt in range(4):
                            if k == 0:
                                claim(tt)
                            a, b = (x[:, k, tt * P:(tt + 1) * P] for x in (h_hi, h_lo))
                            pe.matmul(lin[tt][:, :], a, wh, start=k == 0, stop=False)
                            pe.matmul(lin[tt][:, :], b, wh, start=False, stop=False)
                            mm = pe.matmul(lin[tt][:, :], a, wl, start=False, stop=k == DC - 1)
                    mm.then_inc(*done("slab_used", s))
                    if q == 0:
                        rope(layer, 2 * QC - 1)
                    ada_here(GLU_SLABS + 2 * QC + q)
                    s += 1
                for tt in range(4):
                    seen["chunk", (layer, "v", tt)] = seen["slab_used", s - 1]
                    readers[tt] = ("v_out", (layer, tt))
                for h in range(HEADS):
                    scores(layer, h)
                    g = 2 * h
                    chunk(s, g % 4, T, h_hi, h_lo, (layer, "gate", g), ("gate_out", (layer, g)))
                    turn(layer, h)
                    chunk(s + 1, (g + 1) % 4, T, h_hi, h_lo, (layer, "gate", g + 1), ("gate_out", (layer, g + 1)))
                    values(layer, h)
                    s += 2
                claim(4)
                for c in range(CONV_C):
                    pe.wait_ge(*after("conv_tap", (layer, c, TAPS - 1)))
                    mm = pe.matmul(aux[0][:, 0:T], ones_c, cv[:, c, 0:T], start=c == 0, stop=c == CONV_C - 1)
                mm.then_inc(*done("ln_mean", layer))
                readers[4] = ("conv_centred", (layer, CONV_C - 1))
                claim(5)
                for c in range(CONV_C):
                    pe.wait_ge(*after("ln_sq", (layer, c)))
                    pe.matmul(aux[1][:, 0:T], ones_c, sq[:, c % 2, 0:T], start=c == 0, stop=c == CONV_C - 1)\
                        .then_inc(*done("ln_var", (layer, c)))
                readers[5] = ("ln_root", layer)
                for m in range(DC):
                    weights(s)
                    b = (2 * m) % 4
                    claim(b)
                    for k in range(4):
                        if m == 0:
                            pe.wait_ge(*after("conv_lo", (layer, k)))
                        three(bank[b][:, 0:T], s, k, cv_hi[:, k, 0:T], cv_lo[:, k, 0:T], k == 0, k == 3)
                    claim(b + 1)
                    if m == 0:
                        pe.wait_ge(*after("attn_lo", (layer, HEADS - 1)))
                    for k in range(4):
                        mm = three(bank[b + 1][:, 0:T], s, 4 + k, at_hi[:, k, 0:T], at_lo[:, k, 0:T], k == 0, k == 3)
                    mm.then_inc(*done("slab_used", s))
                    seen["chunk", (layer, "branch", m)] = seen["slab_used", s]
                    readers[b] = readers[b + 1] = ("merged", (layer, m))
                    s += 1
                for m in range(DC):
                    if m == 0:
                        pe.wait_ge(*after("merge_lo", (layer, DC - 1)))
                    chunk(s, m % 4, T, y_hi, y_lo, (layer, "mix", m), ("mix_out", (layer, m)))
                    s += 1
                norm_sum((layer, 2), T, summed=False)

                def up(j, b, it=None):
                    plus = 0 if it is None else it * 4
                    for w in range(2):
                        i = s + 2 * j + w
                        weights(i, it)
                        bk = (2 * b + w) % 4
                        if it is None:
                            claim(bk)
                        else:
                            pe.wait_ge(sem("up_conv"), 2 * (FF_C * layer + j - 2) + w + 1 + plus * 2)
                        for k in range(DC):
                            if j == 0 and w == 0:
                                pe.wait_ge(*after("norm_lo", ((layer, 2), k)))
                            mm = three(bank[bk][:, 0:T], i, k, h_hi[:, k, 0:T], h_lo[:, k, 0:T], k == 0, k == DC - 1)
                        mm.then_inc(*done("slab_used", i))
                for j in range(2):
                    up(j, j)
                with pe.Fori(0, 5) as it:
                    for b in range(4):
                        up(2 + b, b, it)
                again("slab_used", 4 * 8)
                s += 2 * FF_C
                pe.wait_ge(*after("up_all", layer))

                def down(j, b, it=None):
                    plus = 0 if it is None else it * 8
                    weights(s + j, it)
                    pe.wait_ge(sem("down_lo"), FF_C * layer + j + 1 + plus)
                    for m in range(DC):
                        if j == 0:
                            claim(m)
                        mm = three(bank[m][:, 0:T], s + j, m, dn_hi[:, j % 2, 0:T], dn_lo[:, j % 2, 0:T],
                                   j == 0, j == FF_C - 1)
                    mm.then_inc(*done("slab_used", s + j))
                for j in range(5):
                    down(j, j)
                with pe.Fori(0, 2) as it:
                    for b in range(8):
                        down(5 + b, b, it)
                again("slab_used", 8)
                down(FF_C - 1, 0)
                seen["chunk", (layer, "down")] = counts["slab_used"]
                for m in range(DC):
                    readers[m] = ("down_out", (layer, m))

            def rope(layer, c):
                claim(5)
                src = qT[:, c, 0:SEQ] if c < QC else kT[:, c - QC, 0:SEQ]
                pe.wait_ge(*after("qk_out", (layer, c)))
                pe.matmul(aux[1][:, 0:SEQ], perm1, src, start=True, stop=True).then_inc(*done("rope_turn", (layer, c)))
                readers[5] = ("rope_part", (layer, c))

            def scores(layer, h):
                r = slice((h % 2) * HD, (h % 2) * HD + HD)
                c = h // 2
                pe.wait_ge(*after("rope_out", (layer, 2 * QC - 1)))
                for t in range(2):
                    claim(4 + t)
                    pe.matmul(aux[t][:, :], qT[r, c, t * P:(t + 1) * P], kT[r, c, :], start=True, stop=True)\
                        .then_inc(*done("attn_score", (layer, h, t)))
                if layer == 0:
                    claim(6)
                    for t in range(2):
                        pe.matmul(aux[2][:, t * 256:(t + 1) * 256], qT[r, c, SEQ + t * P:SEQ + (t + 1) * P],
                                  kT[r, c, SEQ:T_BOTH], start=True, stop=True)\
                            .then_inc(*done("attn_score", (layer, h, 2 + t)))

            def turn(layer, h):
                for t in range(2):
                    pe.wait_ge(*after("attn_prob", (layer, h, t)))
                    for k in range(4):
                        mm = pe.transpose(aux[t][:, k * P:(k + 1) * P], p_x[:, t, k * P:(k + 1) * P], ident)
                    mm.then_inc(*done("attn_turned", (layer, h, t)))
                    readers[4 + t] = ("attn_pt", (layer, h, t))
                if layer == 0:
                    pe.wait_ge(*after("attn_prob", (layer, h, 3)))
                    for t in range(2):
                        for k in range(2):
                            mm = pe.transpose(aux[2][:, (2 * t + k) * P:(2 * t + k + 1) * P],
                                              p_c[:, t, k * P:(k + 1) * P], ident)
                    mm.then_inc(*done("attn_turned", (layer, h, 2)))
                    readers[6] = ("attn_pt", (layer, h, 2))

            def values(layer, h):
                r = slice((h % 2) * HD, (h % 2) * HD + HD)
                claim(7)
                pe.wait_ge(*after("v_out", (layer, 3)))
                pe.wait_ge(*after("attn_pt", (layer, h, 2 if layer == 0 else 1)))
                for k in range(4):
                    mm = pe.matmul(aux[3][r, 0:SEQ], V[:, k, h * HD:(h + 1) * HD], pt_x[:, k, :],
                                   start=k == 0, stop=k == 3)
                if layer == 0:
                    for k in range(2):
                        mm = pe.matmul(aux[3][r, SEQ:T_BOTH], V[:, 2 + k, h * HD:(h + 1) * HD], pt_c[:, k, :],
                                       start=k == 0, stop=k == 1)
                mm.then_inc(*done("attn_pv", (layer, h)))
                readers[7] = ("attn_lo", (layer, h))

            def network2(layer):
                s = first["l2", layer]
                if layer == 0:
                    norm_sum(("fin", 1), SEQ)
                norm_sum((layer, 3), T2)
                fresh = True
                for step in L2_PLAN:
                    kind, k = step[0:2]
                    if kind == "slab":
                        reader = ("p2_out", (layer, k)) if k < GC else ("gate2", (layer, k))
                        chunk(s + L2_AT[step], l2_bank(step), T2, u_hi, u_lo, (layer, "p2", k), reader,
                              (layer, 3) if fresh else None)
                        fresh = False
                        if QCR < k < QB:
                            rope2(layer, k - 1)
                    elif kind == "vals":
                        q = step[2]
                        i = s + L2_AT[step]
                        weights(i)
                        for j in range(2):
                            kk = 2 * q + j
                            wh, wl = (w[:, i % RING, j * 512:(j + 1) * 512] for w in (w_hi, w_lo))
                            for tt in range(3):
                                b = (l2_bank(step) + tt) % 4
                                if kk == 0:
                                    claim(b)
                                t0 = 0 if tt == 0 else META + (tt - 1) * P
                                a, al = (x[:, kk, t0:t0 + P] for x in (u_hi, u_lo))
                                pe.matmul(lin[b][:, :], a, wh, start=kk == 0, stop=False)
                                pe.matmul(lin[b][:, :], al, wh, start=False, stop=False)
                                mm = pe.matmul(lin[b][:, :], a, wl, start=False, stop=kk == DC - 1)
                        mm.then_inc(*done("slab_used", i))
                        if k == 1 and q == 0:
                            rope2(layer, QB - 1)
                        if q == 3:
                            for tt in range(3):
                                seen["chunk", (layer, "v2", k, tt)] = seen["slab_used", i]
                                readers[(l2_bank(step) + tt) % 4] = ("v2_out", (layer, k, tt))
                    elif kind == "wi":
                        pe.wait_ge(*after("wi_lo", layer))
                        claim(6)
                        for t in range(2):
                            for kk in range(DC):
                                t0 = META + t * P
                                a, al = (x[:, kk, t0:t0 + P] for x in (u_hi, u_lo))
                                o = aux[2][:, 8 * t:8 * t + 8]
                                pe.matmul(o, a, wi_w[:, 0, kk, :], start=kk == 0, stop=False)
                                pe.matmul(o, al, wi_w[:, 0, kk, :], start=False, stop=False)
                                mm = pe.matmul(o, a, wi_w[:, 1, kk, :], start=False, stop=kk == DC - 1)
                        mm.then_inc(*done("wi_made", layer))
                        readers[6] = ("wi_out", layer)
                    elif kind == "index":
                        r = slice((k % 2) * HD, (k % 2) * HD + HD)
                        claim(4 + k % 2)
                        pe.wait_ge(*after("p2_out", (layer, QI + 3)))
                        q = pj[r, QI + k // 2, :]
                        pe.matmul(aux[k % 2][:, S1:S1 + N1], q[:, META:META + P], pj[r, KI, 0:N1], start=True, stop=True)
                        pe.matmul(aux[k % 2][:, S2:S2 + N2], q[:, META + P:T2], pj[r, KI, 0:N2], start=True, stop=True)\
                            .then_inc(*done("index_dot", (layer, k)))
                        readers[4 + k % 2] = ("index_relu", (layer, k))
                    elif kind == "S" and UNITS[k][0] != "c" or kind == "T" and UNITS[k][0] == "c":
                        scores2(layer, k)
                    elif kind == "T" and has_values(k):
                        turn2(layer, k)
                    elif kind == "V" and has_values(k):
                        values2(layer, k)
                for c in range(4):
                    pe.wait_ge(*after("bc_sq", (layer, c)))
                    claim(4 + c)
                    pe.matmul(aux[c][:, 0:T2], ones_h, sq[:, c % 2, 0:T2], start=True, stop=True)\
                        .then_inc(*done("bc_summed", (layer, c)))
                    readers[4 + c] = ("bc_root", (layer, c))
                s += L2_FRONT + 8
                for m in range(DC):
                    if m == 0:
                        pe.wait_ge(*after("unit_lo", (layer, A_HEADS - 1)))
                        pe.wait_ge(*after("bc_lo", (layer, 3)))
                    chunk(s, m % 4, T2, o_hi, o_lo, (layer, "mix2", m), ("mix2_out", (layer, m)))
                    s += 1
                norm_sum((layer, 4), T2, summed=False)

                def ff1(j, b, it=None):
                    plus = 0 if it is None else it * 8
                    weights(s + j, it)
                    if it is None:
                        if j < 4:
                            claim(b % 4)
                        else:
                            pe.wait_ge(*after("ff1_out", (layer, j - 4)))
                    else:
                        pe.wait_ge(sem("ff1_out"), FF2_C * layer + j - 3 + plus)
                    for k in range(DC):
                        if j == 0:
                            pe.wait_ge(*after("norm_lo", ((layer, 4), k)))
                        mm = three(lin[b % 4][:, 0:T2], s + j, k, u_hi[:, k, :], u_lo[:, k, :], k == 0, k == DC - 1)
                    mm.then_inc(*done("slab_used", s + j))
                for j in range(8):
                    ff1(j, j)
                with pe.Fori(0, 3) as it:
                    for b in range(8):
                        ff1(8 + b, b, it)
                again("slab_used", 16)
                s += FF2_C
                pe.wait_ge(*after("ff1_all", layer))

                def ff2(j, b, it=None):
                    plus = 0 if it is None else it * 8
                    weights(s + j, it)
                    pe.wait_ge(sem("ff2_lo"), FF2_C * layer + j + 1 + plus)
                    for m in range(DC):
                        if j == 0:
                            claim(m)
                        mm = three(bank[m][:, 0:T2], s + j, m, dn_hi[:, j % 2, 0:T2], dn_lo[:, j % 2, 0:T2], j == 0, j == FF2_C - 1)
                    mm.then_inc(*done("slab_used", s + j))
                for j in range(7):
                    ff2(j, j)
                with pe.Fori(0, 3) as it:
                    for b in range(8):
                        ff2(7 + b, b, it)
                again("slab_used", 16)
                ff2(FF2_C - 1, 0)
                seen["chunk", (layer, "ff2")] = counts["slab_used"]
                for m in range(DC):
                    readers[m] = ("ff2_out", (layer, m))

            def rope2(layer, c):
                claim(5)
                pe.wait_ge(*after("p2_out", (layer, c)))
                pe.matmul(aux[1][:, 0:T2], perm2, pj[:, c, :], start=True, stop=True).then_inc(*done("rope2_turn", (layer, c)))
                readers[5] = ("rope2_part", (layer, c))

            def scores2(layer, t):
                name, h, c = UNITS[t]
                r = slice((h % 2) * HD + 32 * c, (h % 2) * HD + 32 * c + (32 if name == "b" else HD))
                Q, K = {"a": (QA, KA), "b": (QB, KB), "c": (QCR, KCR)}[name]
                q, kk = pj[r, Q + h // 2, :], pj[r, K + h // 2, :]
                if name == "c":
                    pe.wait_ge(*after("rope2_out", (layer, QB - 1)))
                    claim(4 + t % 2)
                    pe.matmul(aux[t % 2][0:META, 0:T2], kk[:, 0:META], q, start=True, stop=True)
                    claim(6)
                    pe.matmul(aux[2][:, 0:256], kk[:, META:META + P], q[:, META:T2], start=True, stop=True)
                    pe.matmul(aux[2][:, 256:384], kk[:, META + P:T2], q[:, META + P:T2], start=True, stop=True)\
                        .then_inc(*done("score2", (layer, t)))
                    readers[4 + t % 2] = ("pt2c", (layer, t, 0))
                    readers[6] = ("pt2c", (layer, t, 1))
                    return
                pe.wait_ge(*after("p2_out", (layer, K + (3 if name == "a" else 1))))
                claim(4 + t % 2)
                o = aux[t % 2]
                pe.matmul(o[:, S1:S1 + N1], q[:, META:META + P], kk[:, 0:N1], start=True, stop=True)
                pe.matmul(o[:, S2:S2 + N2], q[:, META + P:T2], kk[:, 0:N2], start=True, stop=True)
                pe.matmul(o[:, S0:S0 + N0], q[:, 0:P], kk[:, 0:N0], start=True, stop=True)\
                    .then_inc(*done("score2", (layer, t)))
                readers[4 + t % 2] = ("exp2", (layer, t, 2))

            def turn2(layer, t):
                pe.wait_ge(*after("prob2", (layer, t)))
                claim(4 + t % 2)
                pr = p2[:, t % 3, :]
                o0 = aux[t % 2][0:META, :]
                pe.matmul(o0[:, 0:META], pr[0:META, S0:S0 + META], ident[0:META, 0:META], start=True, stop=True)
                pe.matmul(o0[:, META:META + P], pr[:, S1:S1 + META], ident, start=True, stop=True)
                pe.matmul(o0[:, META + P:T2], pr[:, S2:S2 + META], ident, start=True, stop=True)
                claim(6)
                pe.transpose(aux[2][:, 0:P], pr[:, S1 + META:S1 + META + P], ident)
                pe.transpose(aux[2][:, P:2 * P], pr[:, S2 + META:S2 + META + P], ident)
                pe.transpose(aux[2][:, 2 * P:3 * P], pr[:, S2 + META + P:S2 + T2], ident)\
                    .then_inc(*done("turned2", (layer, t)))
                readers[4 + t % 2] = ("pt2", (layer, t, 0))
                readers[6] = ("pt2", (layer, t, 1))

            def values2(layer, t):
                name, h, _ = UNITS[t]
                r = slice((h % 2) * HD, (h % 2) * HD + HD)
                col = {"a": 0, "b": 512, "c": 768}[name] + h * HD
                claim(7)
                pe.wait_ge(*after("pt2c" if name == "c" else "pt2", (layer, t, 1)))
                pe.wait_ge(*after("v2_out", (layer, 0 if name == "a" else 1, 2)))
                pe.matmul(aux[3][r, 0:T2], V2[0:META, 0, col:col + HD], pt0[0:META, t % 2, :], start=True, stop=False)
                pe.matmul(aux[3][r, META:T2], V2[:, 1, col:col + HD], pt1[:, t % 2, 0:256], start=False, stop=False)
                pe.matmul(aux[3][r, META + P:T2], V2[:, 2, col:col + HD], pt1[:, t % 2, 256:384], start=False, stop=True)\
                    .then_inc(*done("pv2", (layer, t)))
                readers[7] = ("unit_lo", (layer, h)) if name == "a" else ("unit_out", (layer, t))

            pe.wait_ge(*after("vec_in", 2))
            for b, (lo, hi) in enumerate(((0, 512), (512, VLEN))):
                mm = pe.matmul(lin[b][0:12, 0:hi - lo], relb[0:32, :], oneh[0:32, 0, lo:hi], start=True, stop=True)
            mm.then_inc(*done("vec_made", 0))
            readers[0] = readers[1] = ("vec_ready", 0)
            pe.wait_ge(*after("const_in", 1))
            pe.wait_ge(*after("c_silu", 0))
            for layer in range(DEPTH):
                network1(layer)
            for layer in range(DEPTH):
                network2(layer)
            norm_sum(("fin", 2), T2)

        @block.vector
        def _(dve):
            def tt(o, a, b, op):
                return dve.tensor_tensor(o, a, b, op)

            def ts(o, a, s1, op0, s2=None, op1=None):
                if op1 is None:
                    return dve.tensor_scalar(o, a, s1, None, op0)
                return dve.tensor_scalar(o, a, s1, s2, op0, op1)

            def stt(o, a, s, b, op0, op1):
                return dve.scalar_tensor_tensor(out=o, in0=a, scalar=s, in1=b, op0=op0, op1=op1)

            def inverse(ap, root, name, key):
                dve.wait_ge(*after(root, key))
                dve.reciprocal(ap, ap).then_inc(*done(name, key))
                dve.wait_ge(*after(name, key))

            def norm_add(tag, c, T):
                dve.wait_ge(*after("norm_sq", (tag, c)))
                if c > 1:
                    dve.wait_ge(*after("norm_added", (tag, c - 1)))
                tt(rinv[:, 0:T], rinv[:, 0:T], sq[:, c % 2, 0:T], ALU.add).then_inc(*done("norm_added", (tag, c)))

            def norm(tag, X_, T, hi, lo, scale, shift, streams_):
                inverse(rinv[:, 0:T], "norm_root", "norm_rinv", tag)

                def rest(c):
                    dve.wait_ge(*after("norm_hi", (tag, c)))
                    for st, cols in streams_:
                        h = hi[:, c, cols].bitcast(F32)
                        if shift is None:
                            i = tt(lo[:, c, cols], nb[:, c % 4, cols], h, ALU.subtract)
                        else:
                            i = stt(lo[:, c, cols], nb[:, c % 4, cols], shift(c, st), h, ALU.add, ALU.subtract)
                        i.then_inc(*(done("norm_lo", (tag, c)) if st == streams_[-1][0] else done("norm_lo_part", (tag, c))))
                for c in range(DC):
                    if c >= 4:
                        dve.wait_ge(*after("norm_lo", (tag, c - 4)))
                    for st, cols in streams_:
                        i = stt(nb[:, c % 4, cols], X_[:, c, cols], scale(c, st), rinv[:, cols], ALU.mult, ALU.mult)
                        i.then_inc(*(done("normed", (tag, c)) if st == streams_[-1][0] else done("normed_part", (tag, c))))
                    if c >= 2:
                        rest(c - 2)
                rest(DC - 2)
                rest(DC - 1)

            dve.memset(eps[:, :], EPS).then_inc(*done("eps_set", 0))
            dve.memset(cs[:, :, :], 0.0).then_inc(*done("c_silu_part", 0))
            dve.wait_ge(*after("c_tanh", 0))
            dve.wait_ge(*after("c_silu_part", 0))
            ts(cth[:, :, :], cth[:, :, :], 1.0, ALU.add, 0.5, ALU.mult).then_inc(*done("c_silu_part", 1))
            dve.wait_ge(*after("c_silu_part", 1))
            tt(cs[:, :, 0:2], cth[:, :, :], cvec[:, :, :], ALU.mult).then_inc(*done("c_silu", 0))

            def ada_mod(u):
                layer, n = divmod(u, 12)
                dve.wait_ge(*after("ada_turned", u))
                rows = slice(4 * n, 4 * n + 4)
                b = par(layer, "bada")[:, rows].unsqueeze(2).to_broadcast((P, 4, 2))
                tt(mod[:, layer, rows, :], aux[2 + u % 2][:, 0:8].rearrange("p (c s) -> p c s", s=2), b, ALU.add)\
                    .then_inc(*done("ada_mod", u))
                if n == 3:
                    dve.wait_ge(*after("ada_mod", u))
                    for st in range(2):
                        stt(a1[:, layer, :, st], mod[:, layer, DC:2 * DC, st], 1.0, par(layer, "n1g"), ALU.add, ALU.mult)\
                            .then_inc(*done("scale1_ready", (layer, st)))
                if n == 11:
                    dve.wait_ge(*after("ada_mod", u))
                    for st in range(2):
                        stt(a2[:, layer, :, st], mod[:, layer, 4 * DC:5 * DC, st], 1.0, par(layer, "n2g"), ALU.add, ALU.mult)\
                            .then_inc(*done("mod_part", (layer, st)))
                    ts(gh[:, layer, 0, :, :], mod[:, layer, 2 * DC:3 * DC, :], 0.5, ALU.mult).then_inc(*done("mod_part", (layer, 4)))
                    dve.tensor_copy(gh[:, layer, 1, :, :], mod[:, layer, 5 * DC:6 * DC, :]).then_inc(*done("mod_ready", layer))

            def half_parameters(layer):
                for n, (name, lo, hi) in enumerate((("dw", 0, CONV_C * TAPS), ("lng", 0, CONV_C), ("lnb", 0, CONV_C),
                                                    ("fdwb", FF_C, 2 * FF_C))):
                    v = par(layer, name)[:, lo:hi]
                    ts(v, v, 0.5, ALU.mult).then_inc(*done("prm_half", (layer, n)))
                fdw = par(layer, "fdw").rearrange("p (t c) -> p t c", t=3)[:, :, FF_C:2 * FF_C]
                ts(fdw, fdw, 0.5, ALU.mult).then_inc(*done("prm_half", (layer, 4)))

            def network1(layer):
                T = n_tok(layer)
                if layer:
                    dve.wait_ge(*after("down_done", layer - 1))
                dve.memset(upad[:, :, :, 0:HALO], 0.0).then_inc(*done("halo", (layer, 0)))
                dve.memset(upad[:, :, :, HALO + SEQ:], 0.0).then_inc(*done("halo", (layer, 1)))

                def scale(of):
                    return lambda c, st: of[:, layer, c, st:st + 1]

                def shift(row):
                    return lambda c, st: mod[:, layer, row + c, st:st + 1]

                def ada_here(i):
                    if layer == 0 and i <= ADA_UNITS - ADA_BUBBLE:
                        ada_mod(ADA_BUBBLE + i - 1)
                if layer == 0:
                    for u in range(ADA_FIRST):
                        ada_mod(u)
                    dve.wait_ge(*after("x_in", 0))
                dve.wait_ge(*after("scale1_ready", (layer, 1)))
                norm((layer, 1), X, T_BOTH, h_hi, h_lo, scale(a1), shift(0), parts(0))
                if layer == 0:
                    for u in range(ADA_FIRST, ADA_BUBBLE - 1):
                        ada_mod(u)
                for c in range(CONV_C):
                    ada_here(2 * c)
                    dve.wait_ge(*after("glu_tanh", (layer, c)))
                    dve.wait_ge(*after("chunk", (layer, "glu_a", c), ))
                    n = 2 if layer == 0 else 1
                    stt(upad[:, c, 0:n, HALO:HALO + SEQ], streams(glu_t[:, c % 2, :], layer), 1.0,
                        streams(lin[(2 * c + 1) % 4], layer), ALU.add, ALU.mult).then_inc(*done("glu_out", (layer, c)))
                    ada_here(2 * c + 1)
                if layer == 0:
                    dve.wait_ge(*after("tab1_in", 0))
                for c in range(2 * QC):
                    ada_here(GLU_SLABS + c)
                    src = qT[:, c, 0:SEQ] if c < QC else kT[:, c - QC, 0:SEQ]
                    dve.wait_ge(*after("rope_turn", (layer, c)))
                    tt(nt[:, c % 2, 0:SEQ], aux[1][:, 0:SEQ], sin1, ALU.mult).then_inc(*done("rope_part", (layer, c)))
                    tt(src, src, cos1, ALU.mult).then_inc(*done("rope_cos", (layer, c)))
                    dve.wait_ge(*after("rope_cos", (layer, c)))
                    dve.wait_ge(*after("rope_part", (layer, c)))
                    tt(src, src, nt[:, c % 2, 0:SEQ], ALU.add).then_inc(*done("rope_out", (layer, c)))
                for q in range(QKV_V_SLABS):
                    ada_here(GLU_SLABS + 2 * QC + q)
                taps = [(c, t) for c in range(CONV_C) for t in range(TAPS)]

                def tap():
                    if not taps:
                        return
                    c, t = taps.pop(0)
                    n = 2 if layer == 0 else 1
                    src = upad[:, c, 0:n, t:t + SEQ]
                    w = par(layer, "dw", c * TAPS + t)
                    dst = streams(cv[:, c, :], layer)
                    if t == 0:
                        if c == 0:
                            dve.wait_ge(*after("glu_out", (layer, CONV_C - 1)))
                            dve.wait_ge(*after("vec_out", 0))
                        ts(dst, src, w, ALU.mult, par(layer, "dwb", c), ALU.add).then_inc(*done("conv_tap", (layer, c, t)))
                    else:
                        dve.wait_ge(*after("conv_tap", (layer, c, t - 1)))
                        stt(dst, src, w, dst, ALU.mult, ALU.add).then_inc(*done("conv_tap", (layer, c, t)))

                units = [0, 1] + ([2, 3] if layer == 0 else [])
                for h in range(HEADS):
                    bh = biash[:, h % 2, :, :]
                    dve.wait_ge(*after(f"bias_in{h % 2}", (layer, h, 1, 1)))
                    m = win.unsqueeze(1).to_broadcast((P, 8, GRID_W))
                    tt(bh.rearrange("p t (a b) -> p (t a) b", a=4), bh.rearrange("p t (a b) -> p (t a) b", a=4), m, ALU.add)\
                        .then_inc(*done("bias_masked", (layer, h)))
                    dve.wait_ge(*after("bias_masked", (layer, h)))
                    for u in units:
                        dve.wait_ge(*after("attn_score", (layer, h, u if u < 2 else 3)))
                        if u < 2:
                            tt(aux[u][:, 0:SEQ], aux[u][:, 0:SEQ], bh[:, u, :], ALU.add).then_inc(*done("attn_added", (layer, h, u)))
                            dve.wait_ge(*after("attn_added", (layer, h, u)))
                            s = aux[u][:, :]
                        else:
                            s = aux[2][:, (u - 2) * 256:(u - 1) * 256]
                        if h:
                            dve.wait_ge(*after("attn_exp", (layer, h - 1, u)))
                        dve.tensor_reduce(small[:, u:u + 1], s, AXX, ALU.max, negate=True).then_inc(*done("attn_max", (layer, h, u)))
                    for _ in range(8):
                        tap()
                    for u in units:
                        dve.wait_ge(*after("attn_exp", (layer, h, u)))
                        dve.reciprocal(small[:, 16 + u:17 + u], small[:, 8 + u:9 + u]).then_inc(*done("attn_recip", (layer, h, u)))
                        dve.wait_ge(*after("attn_recip", (layer, h, u)))
                        pr = p_x[:, u, :] if u < 2 else p_c[:, u - 2, :]
                        ts(pr, pr, small[:, 16 + u:17 + u], ALU.mult).then_inc(*done("attn_prob", (layer, h, u)))
                    for _ in range(8):
                        tap()
                    r = slice((h % 2) * HD, (h % 2) * HD + HD)
                    dve.wait_ge(*after("attn_hi", (layer, h)))
                    tt(at_lo[r, h // 2, 0:T], aux[3][r, 0:T], at_hi[r, h // 2, 0:T].bitcast(F32), ALU.subtract)\
                        .then_inc(*done("attn_lo", (layer, h)))
                while taps:
                    tap()
                dve.wait_ge(*after("ln_mean", layer))
                for c in range(CONV_C):
                    tt(cv[:, c, 0:T], cv[:, c, 0:T], aux[0][:, 0:T], ALU.subtract).then_inc(*done("conv_centred", (layer, c)))
                inverse(rinv[:, 0:T], "ln_root", "ln_rstd", layer)
                for c in range(CONV_C):
                    tt(cv[:, c, 0:T], cv[:, c, 0:T], rinv[:, 0:T], ALU.mult).then_inc(*done("conv_scaled", (layer, c)))
                    dve.wait_ge(*after("conv_scaled", (layer, c)))
                    ts(nr[:, c % 2, 0:T], cv[:, c, 0:T], par(layer, "lng", c), ALU.mult, par(layer, "lnb", c), ALU.add)\
                        .then_inc(*done("conv_affine", (layer, c)))
                    dve.wait_ge(*after("conv_tanh", (layer, c)))
                    stt(sq[:, c % 2, 0:T], nt[:, c % 2, 0:T], 1.0, nr[:, c % 2, 0:T], ALU.add, ALU.mult)\
                        .then_inc(*done("conv_silu", (layer, c)))
                    dve.wait_ge(*after("conv_hi", (layer, c)))
                    tt(cv_lo[:, c, 0:T], sq[:, c % 2, 0:T], cv_hi[:, c, 0:T].bitcast(F32), ALU.subtract)\
                        .then_inc(*done("conv_lo", (layer, c)))
                def merge_rest(m):
                    dve.wait_ge(*after("merge_hi", (layer, m)))
                    tt(y_lo[:, m, 0:T], nr[:, m % 2, 0:T], y_hi[:, m, 0:T].bitcast(F32), ALU.subtract)\
                        .then_inc(*done("merge_lo", (layer, m)))
                for m in range(DC):
                    b = (2 * m) % 4
                    dve.wait_ge(*after("chunk", (layer, "branch", m)))
                    if m == 0:
                        dve.wait_ge(*after("gate_out", (layer, 2 * DC - 1)))
                    if m:
                        dve.wait_ge(*after("merged", (layer, m - 1)))
                    stt(nt[:, 0, 0:T], gates[:, 2 * m, 0:T], 1.0, lin[b][:, 0:T], ALU.add, ALU.mult)\
                        .then_inc(*done("merge_part", (layer, m, 0)))
                    stt(nt[:, 1, 0:T], gates[:, 2 * m + 1, 0:T], 1.0, lin[b + 1][:, 0:T], ALU.add, ALU.mult)\
                        .then_inc(*done("merge_part", (layer, m, 1)))
                    dve.wait_ge(*after("merge_part", (layer, m, 1)))
                    tt(nr[:, m % 2, 0:T], nt[:, 0, 0:T], nt[:, 1, 0:T], ALU.add).then_inc(*done("merged", (layer, m)))
                    if m:
                        merge_rest(m - 1)
                merge_rest(DC - 1)
                dve.wait_ge(*after("mod_ready", layer))
                for m in range(DC):
                    dve.wait_ge(*after("chunk", (layer, "mix", m)))
                    ps = parts(layer)
                    for st, cols in ps:
                        i = stt(X[:, m, cols], lin[m % 4][:, cols], gh[:, layer, 0, m, st:st + 1], X[:, m, cols], ALU.mult, ALU.add)
                        i.then_inc(*(done("mix_out", (layer, m)) if st == ps[-1][0] else done("mix_part", (layer, m))))
                    if m >= 2:
                        norm_add((layer, 2), m - 1, T)
                norm_add((layer, 2), DC - 1, T)
                norm((layer, 2), X, T, h_hi, h_lo, scale(a2), shift(3 * DC), parts(layer))

                base = FF_C * layer

                def up(j, b, it=None):
                    plus = 0 if it is None else it * 4
                    for w, buf in enumerate((up_a, up_g)):
                        cc = w * FF_C + j
                        ps = streams(lin[(2 * b + w) % 4], layer)
                        acc = streams(buf[:, b % 2, :], layer)
                        dve.wait_ge(sem("up_mid"), 2 * (base + j) + w + 1 + plus * 2)
                        for t, (o, i) in ((0, (slice(1, SEQ), slice(0, SEQ - 1))), (2, (slice(0, SEQ - 1), slice(1, SEQ)))):
                            wcol = par(layer, "fdw", t * 2 * FF_C + cc, plus)
                            ins = stt(acc[:, :, o], ps[:, :, i], wcol, acc[:, :, o], ALU.mult, ALU.add)
                            if t == 0:
                                ins.then_inc(*done("up_left", (layer, j, w)))
                                dve.wait_ge(sem("up_left"), 2 * (base + j) + w + 1 + plus * 2)
                            else:
                                ins.then_inc(*done("up_conv", (layer, j, w)))
                    dve.wait_ge(sem("up_tanh"), base + j + 1 + plus)
                    t_ = up_t[:, b % 2, 0:T]
                    stt(t_, t_, 1.0, up_g[:, b % 2, 0:T], ALU.add, ALU.mult).then_inc(*done("up_silu", (layer, j)))
                    dve.wait_ge(sem("up_silu"), base + j + 1 + plus)
                    dst = ffa[:, j, 0:T] if it is None else ffa[:, bass.ds(j + plus, 1), 0:T].rearrange("p a t -> p (a t)")
                    tt(dst, t_, up_a[:, b % 2, 0:T], ALU.mult).then_inc(*done("up_out", (layer, j)))
                for j in range(2):
                    up(j, j)
                with dve.Fori(0, 5) as it:
                    for b in range(4):
                        up(2 + b, b, it)
                for n, k in (("up_left", 32), ("up_conv", 32), ("up_silu", 16), ("up_out", 16)):
                    again(n, k)
                seen["up_all", layer] = counts["up_out"]

                def down(j, b, it=None):
                    plus = 0 if it is None else it * 8
                    dve.wait_ge(sem("down_hi"), base + j + 1 + plus)
                    src = ffa[:, j, 0:T] if it is None else ffa[:, bass.ds(j + plus, 1), 0:T].rearrange("p a t -> p (a t)")
                    tt(dn_lo[:, j % 2, 0:T], src, dn_hi[:, j % 2, 0:T].bitcast(F32), ALU.subtract)\
                        .then_inc(*done("down_lo", (layer, j)))
                for j in range(5):
                    down(j, j)
                with dve.Fori(0, 2) as it:
                    for b in range(8):
                        down(5 + b, b, it)
                again("down_lo", 8)
                down(FF_C - 1, 0)
                dve.wait_ge(*after("chunk", (layer, "down")))
                for m in range(DC):
                    ps = parts(layer)
                    for st, cols in ps:
                        i = stt(X[:, m, cols], bank[m][:, cols], gh[:, layer, 1, m, st:st + 1], X[:, m, cols], ALU.mult, ALU.add)
                        i.then_inc(*(done("down_out", (layer, m)) if st == ps[-1][0] else done("down_part", (layer, m))))
                seen["down_done", layer] = seen["down_out", (layer, DC - 1)]

            def rope2(layer, c):
                src = pj[:, c, :]
                dve.wait_ge(*after("rope2_turn", (layer, c)))
                tt(nt[:, c % 2, 0:T2], aux[1][:, 0:T2], sin2, ALU.mult).then_inc(*done("rope2_part", (layer, c)))
                tt(src, src, cos2, ALU.mult).then_inc(*done("rope2_cos", (layer, c)))
                dve.wait_ge(*after("rope2_part", (layer, c)))
                dve.wait_ge(*after("rope2_cos", (layer, c)))
                tt(src, src, nt[:, c % 2, 0:T2], ALU.add).then_inc(*done("rope2_out", (layer, c)))

            def biased_max(layer, t):
                name, h, _ = UNITS[t]
                if name == "c":
                    return
                if layer == 0 and t == 0:
                    dve.wait_ge(*after("bias2_in", 2))
                dve.wait_ge(*after("score2", (layer, t)))
                s = aux[t % 2][:, 0:S_ALL]
                tt(s, s, bias2[:, h if name == "a" else A_HEADS + h, :], ALU.add).then_inc(*done("biased2", (layer, t)))
                dve.wait_ge(*after("biased2", (layer, t)))
                if name == "a":
                    tt(s[:, 0:N1 + N2], s[:, 0:N1 + N2], nsel[:, :], ALU.add).then_inc(*done("chosen2", (layer, t)))
                    dve.wait_ge(*after("chosen2", (layer, t)))
                for n_, (lo, n) in enumerate(TILES):
                    m = 3 * (t % 3) + n_
                    dve.tensor_reduce(small[:, m:m + 1], aux[t % 2][:, lo:lo + n], AXX, ALU.max, negate=True)\
                        .then_inc(*done("max2", (layer, t, n_)))

            def probabilities(layer, t):
                name, h, comp = UNITS[t]
                if name == "c":
                    if layer == 0:
                        dve.wait_ge(*after("tab2_in", 1))
                    dve.wait_ge(*after("score2", (layer, t)))
                    if has_values(t - 2):
                        dve.wait_ge(*after("pv2", (layer, t - 2)))
                    tt(pt0[0:META, t % 2, :], aux[t % 2][0:META, 0:T2], decay0[0:META, h, :], ALU.mult)\
                        .then_inc(*done("pt2c", (layer, t, 0)))
                    tt(pt1[:, t % 2, :], aux[2][:, 0:384], decay1[:, h, :], ALU.mult).then_inc(*done("pt2c", (layer, t, 1)))
                    return
                m = 3 * (t % 3)
                dve.wait_ge(*after("exp2", (layer, t, 2)))
                dve.reciprocal(small[:, 18 + m:21 + m], small[:, 9 + m:12 + m]).then_inc(*done("recip2", (layer, t)))
                dve.wait_ge(*after("recip2", (layer, t)))
                if name == "b" and comp:
                    ts(small[:, 18 + m:21 + m], small[:, 18 + m:21 + m], lam[:, 5:6], ALU.mult).then_inc(*done("recip2b", (layer, t)))
                    dve.wait_ge(*after("recip2b", (layer, t)))
                for n_, (lo, n) in enumerate(TILES):
                    pr = p2[:, t % 3, lo:lo + n]
                    w = small[:, 18 + m + n_:19 + m + n_]
                    if name == "b" and comp:
                        dve.wait_ge(*after("prob2", (layer, t - 1)))
                        i = stt(pr, pr, w, p2[:, (t - 1) % 3, lo:lo + n], ALU.mult, ALU.add)
                    else:
                        i = ts(pr, pr, w, ALU.mult)
                    i.then_inc(*(done("prob2", (layer, t)) if n_ == 2 else done("prob2a", (layer, t, n_))))

            def network2(layer):
                if layer == 0:
                    inverse(rinv[:, 0:SEQ], "norm_root", "norm_rinv", ("fin", 1))
                    dve.wait_ge(*after("const2_in", 1))
                    for c in range(DC):
                        stt(H[:, c, META:T2], X[:, c, 0:SEQ], fin_g[:, 0, c:c + 1], rinv[:, 0:SEQ], ALU.mult, ALU.mult)\
                            .then_inc(*done("fin1", c))
                    dve.wait_ge(*after("meta_in", 0))
                dve.wait_ge(*after("lam_in", layer))
                for j in range(2):
                    if j:
                        dve.wait_ge(*after("lam_sum", (layer, 0)))
                    dve.tensor_tensor_reduce(small[:, 64:96], lamp[:, 64 * j:64 * j + 32], lamp[:, 64 * j + 32:64 * j + 64],
                                             1.0, 0.0, ALU.mult, ALU.add, lam[:, j:j + 1])\
                        .then_inc(*done("lam_sum", (layer, j)))
                lam_i = lambda_init(layer)
                dve.wait_ge(*after("lam_exp", layer))
                tt(lam[:, 4:5], lam[:, 3:4], lam[:, 2:3], ALU.subtract).then_inc(*done("lam_part", (layer, 2)))
                dve.wait_ge(*after("lam_part", (layer, 2)))
                ts(lam[:, 5:6], lam[:, 4:5], lam_i, ALU.subtract).then_inc(*done("lam_part", (layer, 3)))
                a = PRM2["dnorm"][0]
                ts(prm2[:, layer, a:a + 1], prm2[:, layer, a:a + 1], 1.0 - lam_i, ALU.mult).then_inc(*done("lam_part", (layer, 4)))
                a = PRM2["rnorm"][0]
                ts(prm2[:, layer, a:a + 2], prm2[:, layer, a:a + 2], 0.5, ALU.mult).then_inc(*done("lam_part", (layer, 5)))
                dve.wait_ge(*after("wi_hi", layer))
                tt(wi_w[:, 1, :, :], wi_r[:, :, :], wi_w[:, 0, :, :].bitcast(F32), ALU.subtract).then_inc(*done("wi_lo", layer))

                def gain(name):
                    return lambda c, st: par2(layer, name, c)
                both = [(0, slice(0, T2))]
                norm((layer, 3), H, T2, u_hi, u_lo, gain("nmix"), None, both)
                for step in L2_PLAN:
                    kind, k = step[0:2]
                    if kind == "wi":
                        dve.wait_ge(*after("wi_made", layer))
                        ts(wis, aux[2][:, 0:16], IDX_HEADS ** -0.5 * 64 ** -0.5, ALU.mult).then_inc(*done("wi_out", layer))
                        if layer == 0:
                            dve.wait_ge(*after("tab2_in", 1))
                        dve.wait_ge(*after("wi_out", layer))
                    elif kind == "index":
                        h = k
                        dve.wait_ge(*after("index_relu", (layer, h)))
                        for t, (lo, n) in enumerate(((S1, N1), (S2, N2))):
                            w = wis[:, 8 * t + h:8 * t + h + 1]
                            src = relu2[:, h % 2, lo:lo + n]
                            if h == 0:
                                i = ts(score[:, lo:lo + n], src, w, ALU.mult)
                            else:
                                if t == 0:
                                    dve.wait_ge(*after("index_sum", (layer, h - 1)))
                                i = stt(score[:, lo:lo + n], src, w, score[:, lo:lo + n], ALU.mult, ALU.add)
                            i.then_inc(*(done("index_sum", (layer, h)) if t else done("index_part", (layer, h))))
                        if h == IDX_HEADS - 1:
                            dve.wait_ge(*after("index_sum", (layer, h)))
                            tt(score[:, :], score[:, :], causal, ALU.add).then_inc(*done("top", (layer, 0)))
                            dve.wait_ge(*after("top", (layer, 0)))
                    elif kind == "top":
                        r = k
                        for t, (lo, n) in enumerate(((S1, N1), (S2, N2))):
                            dve.max(small[:, 48 + 8 * t:56 + 8 * t], score[:, lo:lo + n]).then_inc(*done("top", (layer, 1, r, t)))
                        for t, (lo, n) in enumerate(((S1, N1), (S2, N2))):
                            dve.wait_ge(*after("top", (layer, 1, r, t)))
                            dve.match_replace(score[:, lo:lo + n], small[:, 48 + 8 * t:56 + 8 * t], score[:, lo:lo + n], TAKEN)\
                                .then_inc(*done("top", (layer, 2, r, t)))
                        dve.wait_ge(*after("top", (layer, 2, r, 1)))
                        if r == TOPK // 8 - 1:
                            ts(nsel[:, :], score[:, :], TAKEN / 2, ALU.is_gt, NEG, ALU.mult).then_inc(*done("selected", layer))
                            dve.wait_ge(*after("selected", layer))
                    elif kind == "slab":
                        if QCR < k < QB:
                            rope2(layer, k - 1)
                        if k >= GC:
                            dve.wait_ge(*after("p2_out", (layer, k)))
                            stt(pj[:, k, :], nt[:, k % 2, 0:T2], 1.0, lin[l2_bank(step)][:, 0:T2], ALU.add, ALU.mult)\
                                .then_inc(*done("gate2", (layer, k)))
                    elif kind == "vals" and step[1:] == (1, 0):
                        rope2(layer, QB - 1)
                    elif kind == "S":
                        biased_max(layer, k)
                    elif kind == "T":
                        probabilities(layer, k)
                    elif kind == "V" and UNITS[k][0] == "a":
                        h = UNITS[k][1]
                        r = slice((h % 2) * HD, (h % 2) * HD + HD)
                        dve.wait_ge(*after("unit_out", (layer, k)))
                        tt(o_lo[r, h // 2, :], aux[3][r, 0:T2], o_hi[r, h // 2, :].bitcast(F32), ALU.subtract)\
                            .then_inc(*done("unit_lo", (layer, h)))

                def bc_rest(c):
                    dve.wait_ge(*after("bc_hi", (layer, c)))
                    tt(o_lo[:, 4 + c, :], nr[:, c % 2, 0:T2], o_hi[:, 4 + c, :].bitcast(F32), ALU.subtract)\
                        .then_inc(*done("bc_lo", (layer, c)))
                for c in range(4):
                    inverse(bc_r[:, c, :], "bc_root", "bc_rinv", (layer, c))
                    tt(nt[:, c % 2, 0:T2], bc_raw[:, c, :], bc_r[:, c, :], ALU.mult).then_inc(*done("bc_x", (layer, c)))
                    dve.wait_ge(*after("bc_x", (layer, c)))
                    if c < 2:
                        i = ts(nr[:, c % 2, 0:T2], nt[:, c % 2, 0:T2], par2(layer, "dnorm", 0), ALU.mult)
                    else:
                        i = stt(nr[:, c % 2, 0:T2], nt[:, c % 2, 0:T2], par2(layer, "rnorm", c - 2), pj[:, GC + c - 2, :],
                                ALU.mult, ALU.mult)
                    i.then_inc(*done("bc_normed", (layer, c)))
                    if c:
                        bc_rest(c - 1)
                bc_rest(3)
                for m in range(DC):
                    dve.wait_ge(*after("chunk", (layer, "mix2", m)))
                    tt(H[:, m, :], lin[m % 4][:, 0:T2], H[:, m, :], ALU.add).then_inc(*done("mix2_out", (layer, m)))
                    if m >= 2:
                        norm_add((layer, 4), m - 1, T2)
                norm_add((layer, 4), DC - 1, T2)
                norm((layer, 4), H, T2, u_hi, u_lo, gain("nff"), None, both)
                base = FF2_C * layer

                def ff1(j, b, it=None):
                    plus = 0 if it is None else it * 8
                    dve.wait_ge(sem("ff1_relu"), base + j + 1 + plus)
                    dst = ff2a[:, j, :] if it is None else ff2a[:, bass.ds(j + plus, 1), :].rearrange("p a t -> p (a t)")
                    t_ = up_t[:, b % 2, 0:T2]
                    tt(dst, t_, t_, ALU.mult).then_inc(*done("ff1_out", (layer, j)))
                for j in range(8):
                    ff1(j, j)
                with dve.Fori(0, 3) as it:
                    for b in range(8):
                        ff1(8 + b, b, it)
                again("ff1_out", 16)
                seen["ff1_all", layer] = counts["ff1_out"]

                def ff2(j, b, it=None):
                    plus = 0 if it is None else it * 8
                    dve.wait_ge(sem("ff2_hi"), base + j + 1 + plus)
                    src = ff2a[:, j, :] if it is None else ff2a[:, bass.ds(j + plus, 1), :].rearrange("p a t -> p (a t)")
                    tt(dn_lo[:, j % 2, 0:T2], src, dn_hi[:, j % 2, 0:T2].bitcast(F32), ALU.subtract)\
                        .then_inc(*done("ff2_lo", (layer, j)))
                for j in range(7):
                    ff2(j, j)
                with dve.Fori(0, 3) as it:
                    for b in range(8):
                        ff2(7 + b, b, it)
                again("ff2_lo", 16)
                ff2(FF2_C - 1, 0)
                dve.wait_ge(*after("chunk", (layer, "ff2")))
                for m in range(DC):
                    tt(H[:, m, :], bank[m][:, 0:T2], H[:, m, :], ALU.add).then_inc(*done("ff2_out", (layer, m)))

            dve.wait_ge(*after("vec_made", 0))
            for b, (lo, hi) in enumerate(((0, 512), (512, VLEN))):
                i = tt(vec[0:12, lo:hi], lin[b][0:12, 0:hi - lo], oneh[0:12, 1, lo:hi], ALU.add)
                i.then_inc(*(done("vec_ready", 0) if b else done("vec_part", 0)))
            dve.wait_ge(*after("prm_in", 0))
            for layer in range(DEPTH):
                half_parameters(layer)
            for layer in range(DEPTH):
                network1(layer)
            for layer in range(DEPTH):
                network2(layer)
            tag = ("fin", 2)
            inverse(rinv[:, 0:T2], "norm_root", "norm_rinv", tag)
            for c in range(DC):
                if c >= 4:
                    dve.wait_ge(*after(f"stored{c % 4}", c - 4))
                stt(nb[:, c % 4, 0:SEQ], H[:, c, META:T2], fin_g[:, 1, c:c + 1], rinv[:, META:T2], ALU.mult, ALU.mult)\
                    .then_inc(*done("out_ready", c))
    return seen


def shape_tables():
    t = np.zeros((P, TAB_N), np.float32)

    def put(name, v):
        a, b = TAB[name]
        t[:v.shape[0], a:b] = v
    i = np.arange(P)
    put("ident", np.eye(P))
    put("ones_d", np.full((P, P), 1 / D))
    put("ones_c", np.full((P, P), 1 / (CONV_C * P)))
    put("ones_h", (i[:, None] // HD == i[None, :] // HD) / HD)
    for name, half in (("perm1", 16), ("perm2", 32)):
        m = np.zeros((P, P))
        for j in range(P):
            low = j % (2 * half) < half
            m[j + half if low else j - half, j] = -1 if low else 1
        put(name, m)
    sel = np.zeros((P, 2))
    for g in range(4):
        for s in range(2):
            sel[32 * g + s, s] = 1
    put("sel", sel)
    f = np.float32
    pos = np.arange(SEQ)
    inv = (f(10000.0) ** (-np.arange(0, 32, 2, dtype=f) / f(32))).astype(f)
    ang = np.zeros((P, SEQ), f)
    for j in range(P):
        d = j % HD
        where = pos // GRID_W if d < 32 else pos % GRID_W
        ang[j] = where.astype(f) * inv[d % 16]
    put("cos1", np.cos(ang))
    put("sin1", np.sin(ang))
    q, k = np.arange(GRID_W)[:, None], np.arange(GRID_W)[None, :]
    start = np.clip(q - 8, 0, GRID_W - 16)
    w = np.where((k >= start) & (k < start + 16), 0.0, NEG)
    put("win", np.concatenate([w, w]))
    inv = (f(10000.0) ** (-np.arange(0, 64, 2, dtype=f) / f(64))).astype(f)
    ang = inv[(i % HD) % 32][:, None] * np.arange(T2, dtype=f)[None, :]
    put("cos2", np.cos(ang))
    put("sin2", np.sin(ang))
    c = np.zeros((P, N1 + N2))
    c[:, :N1] = np.where(np.arange(N1)[None] <= META + i[:, None], 0, NEG)
    c[:, N1:] = np.where(np.arange(N2)[None] <= META + P + i[:, None], 0, NEG)
    put("causal", c)
    lg = np.log1p(-np.exp2(-5.0 - np.arange(C_HEADS)))

    def decay(keys, queries):
        d = queries[None, None, :] - keys[:, None, None]
        return np.where(d >= 0, np.exp(lg[None, :, None] * np.maximum(d, 0)), 0.0)
    d1 = np.concatenate([decay(META + i, np.arange(META, T2)), decay(META + P + i, np.arange(META + P, T2))], axis=2)
    put("decay1", d1.reshape(P, -1))
    put("decay0", decay(np.arange(META), np.arange(T2)).reshape(META, -1))
    dist = T2 - 1 - np.arange(VLEN)
    n = np.maximum(dist, 0)
    large = 16 + (np.log(np.maximum(n, 1).astype(f) / f(16)) / f(math.log(8)) * f(16)).astype(np.int32)
    bucket = np.where(n < 16, n, np.minimum(large, 31))
    put("onehot", (bucket[None, :] == np.arange(32)[:, None]) & (dist >= 0)[None, :])
    put("vmask", np.broadcast_to(np.where(dist >= 0, 0.0, NEG), (12, VLEN)))
    return t


def by_feature(v):
    v = v.reshape(*v.shape[:-1], -1, P)
    return np.moveaxis(v, -1, 0)


def weight_stream(w):
    slabs = []

    def tiles(m, c0):
        return m[:, c0:c0 + P].reshape(-1, P, P).transpose(1, 0, 2).reshape(P, -1)

    def wide(m):
        for q in range(m.shape[0] // (2 * P)):
            slabs.append(m[2 * P * q:2 * P * (q + 1)].reshape(2, P, 512).transpose(1, 0, 2).reshape(P, -1))
    for l in range(DEPTH):
        m = w["w_in"][l]
        for c in range(CONV_C):
            slabs += [tiles(m, 512 + c * P), tiles(m, c * P)]
        for c in range(2 * QC):
            slabs.append(tiles(m, 1024 + c * P))
        wide(m[:, 2048:2560])
        for c in range(DC):
            slabs += [tiles(m, 2560 + c * P), tiles(m, 2560 + D + c * P)]
        for c in range(DC):
            slabs.append(np.concatenate([tiles(w["w_conv_out"][l], c * P), tiles(w["w_na_out"][l], c * P)], axis=1))
        for c in range(DC):
            slabs.append(tiles(w["w_out"][l], c * P))
        for j in range(FF_C):
            slabs += [tiles(w["w_up"][l], j * P), tiles(w["w_up"][l], (FF_C + j) * P)]
        slabs += list(w["w_down"][l].reshape(FF_C, P, D))
    for l in range(DEPTH):
        m = w["w_in_2"][l]
        at = {"qa": 0, "ka": 512, "va": 1024, "qi": 1536, "ki": 2048, "qb": 2120, "kb": 2376, "vb": 2632,
              "qc": 2888, "kc": 3144, "vc": 3400, "gc": 3656}

        def feature(names):
            for name, n in names:
                for c in range(n):
                    slabs.append(tiles(m, at[name] + c * P))
        slabs.append(tiles(np.concatenate([m[:, 2048:2112]] * 2, axis=1), 0))
        feature([("qi", 4), ("qa", 4), ("ka", 4)])
        wide(m[:, at["va"]:at["va"] + 512])
        feature([("qc", 2), ("kc", 2)])
        wide(np.concatenate([m[:, at["vb"]:at["vb"] + 256], m[:, at["vc"]:at["vc"] + 256]], axis=1))
        feature([("qb", 2), ("kb", 2), ("gc", 2)])
        for c in range(DC):
            slabs.append(tiles(w["w_out_2"][l], c * P))
        for c in range(FF2_C):
            slabs.append(tiles(w["w_ff1_2"][l], c * P))
        slabs += list(w["w_ff2_2"][l].reshape(FF2_C, P, D))
    return np.stack(slabs)


def ada_stream(w_ada):
    w = w_ada.reshape(DEPTH, DC // 2, 2, P, 12, 512).transpose(0, 4, 1, 3, 2, 5)
    return w.reshape(DEPTH * 12 * (DC // 2), P, SLAB)


def kernel(**inputs):
    import concourse.bacc as bacc
    from concourse.bass_utils import run_bass_kernel_spmd as run

    w = {k: np.asarray(v) for k, v in inputs.items()}
    prm1, prm2 = [], []
    for l in range(DEPTH):
        dw = by_feature(w["conv_dw"][l]).transpose(0, 2, 1).reshape(P, -1)
        prm1.append(np.concatenate([
            by_feature(w["norm1_g"][l]), dw, by_feature(w["conv_dw_b"][l]), by_feature(w["conv_ln_g"][l]),
            by_feature(w["conv_ln_b"][l]), by_feature(w["norm2_g"][l]), by_feature(w["ffn_dw"][l]).reshape(P, -1),
            by_feature(w["ffn_dw_b"][l]), by_feature(w["b_ada"][l])], axis=1))
        dn = w["diff_norm_2"][l]
        prm2.append(np.concatenate([
            by_feature(w["norm_mix_2"][l]), np.concatenate([dn, dn])[:, None], by_feature(w["ret_norm_2"][l]),
            by_feature(w["norm_ff_2"][l])], axis=1))
    rpb = np.zeros((DEPTH, HEADS, 15, RPB_PAD), w["na_rpb"].dtype)
    rpb[..., 48:79] = w["na_rpb"]
    arrays = {
        "wstream": weight_stream(w),
        "wada": ada_stream(w["w_ada"]),
        "tables": shape_tables(),
        "x_in": np.concatenate([by_feature(w["x"][0]).transpose(0, 2, 1), by_feature(w["ctx"][0]).transpose(0, 2, 1)], axis=2),
        "cvec": np.stack([by_feature(w["c"][0]), by_feature(w["c_ctx"])], axis=2),
        "prm1": np.stack(prm1, axis=1),
        "prm2": np.stack(prm2, axis=1),
        "fin_g": np.stack([by_feature(w["final_norm_g"]), by_feature(w["final_norm_2"])], axis=1),
        "rpb": rpb,
        "meta": by_feature(w["meta_2"]).transpose(0, 2, 1),
        "rel_bias": w["rel_bias_2"],
        "lam": w["diff_lambda_2"].reshape(DEPTH, P),
        "wi": w["w_in_2"][:, :, 2112:2120].reshape(DEPTH, DC, P, 8).transpose(0, 2, 1, 3),
    }
    arrays = {k: np.ascontiguousarray(v) for k, v in arrays.items()}

    def emit(marks):
        nc = bacc.Bacc("TRN2", target_bir_lowering=False, num_devices=1)
        args = {k: nc.dram_tensor(f"in_{k}", v.shape, mybir.dt.from_np(v.dtype), kind="ExternalInput").ap()
                for k, v in arrays.items()}
        out = nc.dram_tensor("out_x", (D, SEQ), F32, kind="ExternalOutput").ap()
        return nc, build(nc, args, out, marks)

    _, marks = emit({})
    nc, again = emit(marks)
    assert marks == again
    r = run(nc, [{f"in_{k}": v for k, v in arrays.items()}], core_ids=[0])
    return np.ascontiguousarray(r.results[0]["out_x"].T)[None]
```

```python
import math
from contextlib import ExitStack

import concourse.bass as bass
import numpy as np
from concourse import mybir

F32 = mybir.dt.float32
F32R = mybir.dt.float32r
ALU = mybir.AluOpType
ACT = mybir.ActivationFunctionType
AXX = mybir.AxisListType.X

P = 128
D = 1024
DC = D // P
SEQ = 256
CTX = 256
DEPTH = 2
EPS = 1e-6
NEG = -1e30
TAKEN = -3e38

GRID_W = 64
CONV_C = 512 // P
TAPS = 31
HALO = TAPS // 2
HEADS = 8
HD = 64
QC = HEADS * HD // P
FF_C = 2816 // P
RPB_PAD = 128
T_BOTH = SEQ + CTX

META = 16
T2 = SEQ + META
TOPK = 64
A_HEADS = 8
IDX_HEADS = 8
B_HEADS = 4
C_HEADS = 4
FF2_C = 4 * D // P
N1, N2, N0 = META + P, T2, META
S1, S2, S0 = 0, N1, N1 + N2
S_ALL = N1 + N2 + N0
VLEN = 544

TILE = P * P
SLAB = 8 * P
RING = 4
ADA_SLABS = 6 * DC
ADA_RING = 8
ADA_UNITS = DEPTH * 12
ADA_BUBBLE = 6
ADA_FIRST = 4
GLU_SLABS = 2 * CONV_C
QKV_V_SLABS = 4
L1_SLABS = GLU_SLABS + 2 * QC + QKV_V_SLABS + 2 * DC + DC + DC + 2 * FF_C + FF_C
L2_FRONT = 23
L2_SLABS = L2_FRONT + 8 + DC + FF2_C + FF2_C
N_SLABS = DEPTH * (L1_SLABS + L2_SLABS)

PRM1 = {}
_n = 0
for _name, _w in (("n1g", DC), ("dw", CONV_C * TAPS), ("dwb", CONV_C), ("lng", CONV_C), ("lnb", CONV_C),
                  ("n2g", DC), ("fdw", 3 * 2 * FF_C), ("fdwb", 2 * FF_C), ("bada", 6 * DC)):
    PRM1[_name] = (_n, _n + _w)
    _n += _w
PRM1_N = _n
PRM2 = {}
_n = 0
for _name, _w in (("nmix", DC), ("dnorm", 1), ("rnorm", 2), ("nff", DC)):
    PRM2[_name] = (_n, _n + _w)
    _n += _w
PRM2_N = _n
TAB = {}
_n = 0
for _name, _w in (("ident", P), ("ones_d", P), ("ones_c", P), ("ones_h", P), ("perm1", P), ("perm2", P),
                  ("sel", 2), ("cos1", SEQ), ("sin1", SEQ), ("win", GRID_W),
                  ("cos2", T2), ("sin2", T2), ("causal", N1 + N2), ("decay1", 4 * 384), ("decay0", 4 * T2),
                  ("onehot", VLEN), ("vmask", VLEN)):
    TAB[_name] = (_n, _n + _w)
    _n += _w
TAB_N = _n


def lambda_init(layer):
    return 0.8 - 0.6 * math.exp(-0.3 * layer)


def build(nc, A, out, marks):
    SAME = {"chunk": "slab_used", "up_all": "up_out", "down_done": "down_out", "ff1_all": "ff1_out"}
    GROUP = {n: "vector_part" for n in ("prm_half", "halo", "mod_part", "normed_part", "norm_lo_part", "down_part",
                                        "mix_part", "index_part", "prob2a", "vec_part")}
    seen = {}
    sems = {}
    counts = {}
    ctx = ExitStack()

    def sem(name):
        if name not in sems:
            sems[name] = ctx.enter_context(nc.semaphore(name))
            counts[name] = 0
        return sems[name]

    def done(name, key, by=1):
        s = sem(GROUP.get(name, name))
        counts[GROUP.get(name, name)] += by
        assert (name, key) not in seen, (name, key)
        seen[name, key] = counts[GROUP.get(name, name)]
        return s, by

    def again(name, n):
        counts[name] += n

    def after(name, key, plus=0):
        return sem(SAME.get(name, name)), marks.get((name, key), 1) + plus

    with ctx:
        top = [16512]

        def at(name, shape, dt, offset):
            t = nc.alloc_sbuf_tensor_at(name, [P, *shape], dt, offset=offset)
            return t[(slice(None),) * (len(shape) + 1)]

        def sb(name, shape, dt=F32):
            n = int(np.prod(shape)) * 4
            t = at(name, shape, dt, top[0])
            top[0] += -(-n // 32) * 32
            assert top[0] <= nc.sbuf_usable_end, name
            return t

        bank = [ctx.enter_context(nc.psum_tensor(f"bank{i}", [P, 512], F32)) for i in range(8)]
        lin, aux = bank[0:4], bank[4:8]

        raw = sb("raw", [RING, SLAB])
        w_hi = sb("w_hi", [RING, SLAB], F32R)
        w_lo = sb("w_lo", [RING, SLAB], F32R)
        cst = sb("cst", [6 * P + 2])
        prm = sb("prm", [DEPTH, PRM1_N])
        prm2 = sb("prm2", [DEPTH, PRM2_N])
        fin_g = sb("fin_g", [2, DC])
        cvec = sb("cvec", [DC, 2])
        cth = sb("cth", [DC, 2])
        mod = sb("mod", [DEPTH, 6 * DC, 2])
        a1 = sb("a1", [DEPTH, DC, 2])
        a2 = sb("a2", [DEPTH, DC, 2])
        gh = sb("gh", [DEPTH, 2, DC, 2])
        small = sb("small", [128])
        eps = sb("eps", [8])
        sq_at = top[0]
        sq = sb("sq", [2, 512])
        nb_at = top[0]
        nb = sb("nb", [4, 512])
        nt, nr = nb[:, 0:2, :], nb[:, 2:4, :]
        work = top[0]
        top[0] += 12288
        rinv = at("rinv", [512], F32, work + 10240)
        p_x = at("p_x", [2, 512], F32, work)
        p_c = at("p_c", [2, 256], F32, work + 4096)
        pt_x = at("pt_x", [4, 256], F32, work + 6144)
        pt_c = at("pt_c", [2, 256], F32, work + 10240)
        up_a = at("up_a", [2, 512], F32, work)
        up_g = at("up_g", [2, 512], F32, work + 4096)
        up_t = at("up_t", [2, 512], F32, work + 8192)
        glu_t = at("glu_t", [2, 512], F32, work)
        dn_hi = at("dn_hi", [2, 512], F32R, nb_at)
        dn_lo = at("dn_lo", [2, 512], F32R, nb_at + 4096)
        ada_part = at("ada_part", [2, 512], F32, work + 4096)
        p2 = at("p2", [3, S_ALL], F32, work)
        pt0 = at("pt0", [2, T2], F32, work + 5184)
        pt1 = at("pt1", [2, 384], F32, work + 7360)
        relu2 = at("relu2", [2, N1 + N2], F32, work + 5184)

        x_at = top[0]
        X = sb("X", [DC, T_BOTH])
        h_at = top[0]
        h_hi = sb("h_hi", [DC, T_BOTH], F32R)
        h_lo = sb("h_lo", [DC, T_BOTH], F32R)
        y_hi = at("y_hi", [DC, T_BOTH], F32R, h_at)
        y_lo = at("y_lo", [DC, T_BOTH], F32R, h_at + DC * T_BOTH * 4)
        g_at = top[0]
        gates = sb("gates", [2 * DC, T_BOTH])
        ada_raw = at("ada_raw", [ADA_RING, SLAB], F32, g_at)
        ffa = at("ffa", [FF_C, T_BOTH], F32, g_at)
        q_at = top[0]
        qT = sb("qT", [QC, T_BOTH])
        kT = sb("kT", [QC, T_BOTH])
        at_hi = at("at_hi", [QC, T_BOTH], F32R, q_at)
        at_lo = at("at_lo", [QC, T_BOTH], F32R, q_at + QC * T_BOTH * 4)
        V = sb("V", [4, 512])
        up_at = top[0]
        upad = sb("upad", [CONV_C, 2, SEQ + 2 * HALO])
        cv_at = top[0]
        cv = sb("cv", [CONV_C, T_BOTH])
        cv_hi = at("cv_hi", [CONV_C, T_BOTH], F32R, up_at)
        cv_lo = at("cv_lo", [CONV_C, T_BOTH], F32R, cv_at)
        biash = sb("biash", [2, 2, 256])
        cs = at("cs", [DC, 32], F32, top[0] - 2 * 256 * 4)
        tab1 = sb("tab1", [2 * SEQ + GRID_W])
        end1 = top[0]
        cos1, sin1, win = tab1[:, 0:SEQ], tab1[:, SEQ:2 * SEQ], tab1[:, 2 * SEQ:2 * SEQ + GRID_W]

        o = h_at
        u_hi = at("u_hi", [DC, T2], F32R, o)
        u_lo = at("u_lo", [DC, T2], F32R, o + DC * T2 * 4)
        H = at("H", [DC, T2], F32, o + 2 * DC * T2 * 4)
        decay0 = at("decay0", [4, T2], F32, o + 3 * DC * T2 * 4)
        assert 3 * DC * T2 * 4 + 4 * T2 * 4 <= 2 * DC * T_BOTH * 4
        tab2 = at("tab2", [2 * T2 + N1 + N2 + 4 * 384], F32, x_at)
        cos2, sin2, causal = tab2[:, 0:T2], tab2[:, T2:2 * T2], tab2[:, 2 * T2:2 * T2 + N1 + N2]
        decay1 = tab2[:, 2 * T2 + N1 + N2:].rearrange("p (h n) -> p h n", h=4)
        n_tab2 = 2 * T2 + N1 + N2 + 4 * 384
        score = at("score", [N1 + N2], F32, x_at + n_tab2 * 4)
        nsel = at("nsel", [N1 + N2], F32, x_at + (n_tab2 + N1 + N2) * 4)
        assert n_tab2 + 2 * (N1 + N2) <= DC * T_BOTH
        o = g_at
        pj = at("pj", [L2_FRONT, T2], F32, o)
        V2 = at("V2", [3, 1024], F32, o + L2_FRONT * T2 * 4)
        ff2a = at("ff2a", [FF2_C, T2], F32, o)
        o += (L2_FRONT * T2 + 3 * 1024) * 4
        assert FF2_C * T2 <= L2_FRONT * T2 + 3 * 1024
        o_hi = at("o_hi", [DC, T2], F32R, o)
        o_lo = at("o_lo", [DC, T2], F32R, o + DC * T2 * 4)
        o += 2 * DC * T2 * 4
        bias2 = at("bias2", [A_HEADS + B_HEADS, S_ALL], F32, o)
        o += (A_HEADS + B_HEADS) * S_ALL * 4
        wi_w = at("wi_w", [2, DC, 8], F32R, o)
        wi_r = at("wi_r", [DC, 8], F32, o + 512)
        lamp = at("lamp", [4 * 32], F32, o + 768)
        assert o + 1280 <= end1, (o, end1)
        KI, QI, QCR, KCR, QB, KB, QA, KA, GC = 0, 1, 5, 7, 9, 11, 13, 17, 21
        bc_raw = pj[:, QI:QI + 4, :]
        bc_r = pj[:, QCR:QCR + 4, :]
        vec = at("vec", [VLEN], F32, cv_at)
        oneh = at("oneh", [2, VLEN], F32, cv_at + VLEN * 4)
        relb = at("relb", [A_HEADS + B_HEADS], F32, cv_at + 3 * VLEN * 4)

        wis, lam = small[:, 32:48], small[:, 96:104]
        ident = cst[:, 0:P]
        ones_d, ones_c, ones_h = (cst[:, i * P:(i + 1) * P] for i in (1, 2, 3))
        perm1, perm2, sel = cst[:, 4 * P:5 * P], cst[:, 5 * P:6 * P], cst[:, 6 * P:6 * P + 2]
        by_distance = nc.dram_tensor("bias_by_distance", (A_HEADS + B_HEADS, P, VLEN), F32).ap()
        by_offset = nc.dram_tensor("rpb_by_offset", (DEPTH, HEADS, 7, GRID_W, RPB_PAD), F32).ap()

        def par(layer, name, c=None, plus=0):
            a, b = PRM1[name]
            if c is None:
                return prm[:, layer, a:b]
            return prm[:, layer, a + c:a + c + 1] if type(plus) is int else prm[:, layer, bass.ds(a + c + plus, 1)]

        def par2(layer, name, c):
            return prm2[:, layer, PRM2[name][0] + c:PRM2[name][0] + c + 1]

        first = {}
        n = 0
        for kind, size in (("l1", L1_SLABS), ("l2", L2_SLABS)):
            for layer in range(DEPTH):
                first[kind, layer] = n
                n += size
        assert n == N_SLABS

        def streams(ap, layer, lo=0, hi=SEQ):
            n = 2 if layer == 0 else 1
            return ap[:, 0:n * SEQ].rearrange("p (s t) -> p s t", s=n)[:, :, lo:hi]

        def n_tok(layer):
            return T_BOTH if layer == 0 else SEQ

        def parts(layer):
            return [(s, slice(s * SEQ, (s + 1) * SEQ)) for s in range(2 if layer == 0 else 1)]

        L1_PLAN = []
        for h in range(HEADS):
            more = h + 1 < HEADS
            L1_PLAN += [("Sx", h + 1)] * more + [("gate", 2 * h), ("T", h)] + [("Sc", h + 1)] * more
            L1_PLAN += [("mean", 0)] * (not more) + [("gate", 2 * h + 1), ("V", h)]
        L1_PLAN.append(("var", 0))
        TAPS_QK, TAPS_V, TAPS_HEAD = 5, 7, 4

        def sx_bank(h, t):
            return (4, 2)[h % 2] + t

        def px(h):
            return (p_x, sq)[h % 2]

        UNITS = [("a", h, 0) for h in range(A_HEADS)] + [("c", h, 0) for h in range(C_HEADS)]
        UNITS += [("b", h, c) for h in range(B_HEADS) for c in range(2)]
        N_UNITS = len(UNITS)

        def unit_steps(t, slab=None):
            steps = []
            if t < N_UNITS:
                steps.append(("S", t))
            if 0 <= t - 2:
                steps.append(("V", t - 2))
            if slab:
                steps.append(slab)
            if 0 <= t - 1 < N_UNITS:
                steps.append(("T", t - 1))
            return steps
        L2_PLAN = [("slab", c) for c in range(KI, QCR)] + [("wi", 0)]
        for h, c in enumerate(range(QA, GC)):
            L2_PLAN += [("slab", c), ("index", h)]
        for q in range(4):
            L2_PLAN += [("vals", 0, q), ("top", 2 * q), ("top", 2 * q + 1)]
        L2_PLAN += [("slab", c) for c in range(QCR, QB)]
        beside = [("vals", 1, q) for q in range(4)] + [("slab", c) for c in range(QB, QA)]
        beside += [None, ("slab", GC), None, ("slab", GC + 1)]
        for t in range(N_UNITS + 2):
            L2_PLAN += unit_steps(t, beside[t] if t < len(beside) else None)
        L2_AT = {}
        for st in L2_PLAN:
            if st[0] in ("slab", "vals"):
                L2_AT[st] = len(L2_AT)
        assert len(L2_AT) == L2_FRONT + 8
        TILES = ((S1, N1), (S2, N2), (S0, N0))

        def has_values(t):
            return UNITS[t][0::2] != ("b", 0)

        def l2_bank(step):
            at_ = L2_AT[step[0], step[1], 0] if step[0] == "vals" else L2_AT[step]
            return at_ % 4

        block = ctx.enter_context(nc.Block())

        @block.sync
        def _(sp):
            def load(i, it=None):
                plus = 0 if it is None else it * 8
                if i >= RING:
                    sp.wait_ge(sem("w_lo_ready"), i - RING + 1 + plus)
                src = A["wstream"][i] if it is None else A["wstream"][bass.ds(i + plus, 1)].rearrange("a p n -> (a p) n")
                sp.dma_start(raw[:, i % RING, :], src).then_inc(sem(f"slab_landed{i % RING}"), 16)

            def load_ada(u):
                for a in range(4 * u, 4 * u + 4):
                    if a >= ADA_RING:
                        sp.wait_ge(sem("ada_slab_read"), a - ADA_RING + 1)
                    sp.dma_start(ada_raw[:, a % ADA_RING, :], A["wada"][a]).then_inc(sem(f"ada_landed{a % ADA_RING}"), 16)

            for u in range(ADA_FIRST):
                load_ada(u)
            for i in range(RING):
                load(i)
            for u in range(ADA_FIRST, ADA_BUBBLE):
                load_ada(u)
            for i in range(ADA_UNITS - ADA_BUBBLE):
                load_ada(ADA_BUBBLE + i)
                load(RING + i)
            start = RING + ADA_UNITS - ADA_BUBBLE
            reps = (N_SLABS - start) // 8
            with sp.Fori(0, reps) as it:
                for b in range(8):
                    load(start + b, it)
            for i in range(start + reps * 8, N_SLABS):
                load(i)
            for c in range(DC):
                sp.wait_ge(*after("out_ready", c))
                sp.dma_start(out[c * P:(c + 1) * P, :], nb[:, c % 4, 0:SEQ]).then_inc(*done(f"stored{c % 4}", c, 16))
            for c in range(DC - 4, DC):
                sp.wait_ge(*after(f"stored{c % 4}", c))

        def ada_landed(a):
            return sem(f"ada_landed{a % ADA_RING}"), 16 * (a // ADA_RING + 1)

        def landed(i):
            return sem(f"slab_landed{i % RING}"), 16 * (i // RING + 1)

        @block.gpsimd
        def _(pool):
            def rest(q, it=None):
                plus = 0 if it is None else it * 8
                pool.wait_ge(sem("w_hi_ready"), q + 1 + plus)
                s = q % RING
                pool.tensor_tensor(w_lo[:, s, :], raw[:, s, :], w_hi[:, s, :].bitcast(F32), ALU.subtract)\
                    .then_inc(sem("w_lo_ready"), 1)

            reps = N_SLABS // 8
            with pool.Fori(0, reps) as it:
                for b in range(8):
                    rest(b, it)
            for q in range(reps * 8, N_SLABS):
                rest(q)

        @block.scalar
        def _(act):
            nxt = [0]

            def round_weights(q, it=None):
                i, s = q, q % RING
                a, n = landed(i)
                act.wait_ge(a, n + (0 if it is None else it * (8 // RING) * 16))
                if q >= RING:
                    act.wait_ge(sem("slab_used"), q - RING + 1 + (0 if it is None else it * 8))
                act.activation(w_hi[:, s, :], raw[:, s, :], ACT.Copy).then_inc(sem("w_hi_ready"), 1)

            def ahead(i):
                while nxt[0] <= min(i + RING - 1, N_SLABS - 1):
                    round_weights(nxt[0])
                    nxt[0] += 1

            def copy(dst, src, **kw):
                return act.activation(dst, src, ACT.Copy, **kw)

            tb = A["tables"]
            act.dma_start(cst[:, :], tb[:, TAB["ident"][0]:TAB["sel"][1]]).then_inc(*done("const_in", 0, 16))
            act.dma_start(cvec[:, :, :], A["cvec"]).then_inc(*done("const_in", 1, 16))
            act.dma_start(X[:, :, :], A["x_in"]).then_inc(*done("x_in", 0, 16))
            act.dma_start(prm[:, :, :], A["prm1"]).then_inc(*done("prm_in", 0, 16))
            act.dma_start(tab1[:, :], tb[:, TAB["cos1"][0]:TAB["win"][1]]).then_inc(*done("tab1_in", 0, 16))
            act.dma_start(prm2[:, :, :], A["prm2"]).then_inc(*done("const2_in", 0, 16))
            act.dma_start(fin_g[:, :, :], A["fin_g"]).then_inc(*done("const2_in", 1, 16))
            act.dma_start(oneh[0:32, 0, :], tb[0:32, TAB["onehot"][0]:TAB["onehot"][1]]).then_inc(*done("vec_in", 0, 16))
            act.dma_start(oneh[0:12, 1, :], tb[0:12, TAB["vmask"][0]:TAB["vmask"][1]]).then_inc(*done("vec_in", 1, 16))
            act.dma_start(relb[0:32, :], A["rel_bias"]).then_inc(*done("vec_in", 2, 16))
            for layer in range(DEPTH):
                for h in range(HEADS):
                    off = ((layer * HEADS + h) * 15 + 4) * RPB_PAD
                    src = bass.AP(A["rpb"].tensor, off, [[RPB_PAD, 7], [0, GRID_W], [1, RPB_PAD]])
                    act.dma_start(by_offset[layer, h], src).then_inc(*done(f"rpb_rows{layer}", h, 16))
            act.wait_ge(*after("const_in", 1))
            act.activation(cth[:, :, :], cvec[:, :, :], ACT.Tanh, scale=0.5).then_inc(*done("c_tanh", 0))

            def ada_copy(u):
                act.wait_ge(sem("ada_slab_read"), 4 * (u + 1))
                if u >= 2:
                    act.wait_ge(*after("ada_turned", u - 2))
                copy(ada_part[:, u % 2, :], aux[2 + u % 2][:, :]).then_inc(*done("ada_part_out", u))

            def load_bias(layer, h):
                for t in range(2):
                    for r in range(2):
                        off = ((layer * HEADS + h) * 7 + 3 - (2 * t + r)) * GRID_W * RPB_PAD + GRID_W - 1
                        src = bass.AP(by_offset.tensor, off, [[RPB_PAD - 1, GRID_W], [GRID_W * RPB_PAD, 4], [1, GRID_W]])
                        act.dma_start(biash[r * GRID_W:(r + 1) * GRID_W, h % 2, t, :]
                                      .rearrange("p (a b) -> p a b", a=4), src)\
                            .then_inc(*done(f"bias_in{h % 2}", (layer, h, t, r), 16))

            def root(dst, mean, name, key):
                act.activation(dst, mean, ACT.Sqrt, bias=eps[:, 0:1]).then_inc(*done(name, key))

            def norm(tag, X_, T, k_ready, summed=True, slab=None):
                for c in range(DC):
                    if slab is not None:
                        ahead(slab + c)
                    if k_ready:
                        act.wait_ge(*after(*k_ready(c)))
                    if c >= (2 if summed else 3):
                        act.wait_ge(*after("norm_summed" if summed else "norm_added", (tag, c - 2)))
                    dst = rinv[:, 0:T] if not summed and c == 0 else sq[:, c % 2, 0:T]
                    act.activation(dst, X_[:, c, 0:T], ACT.Square).then_inc(*done("norm_sq", (tag, c)))
                act.wait_ge(*after("norm_summed", (tag, DC - 1)))
                root(rinv[:, 0:T], aux[0][:, 0:T], "norm_root", tag)

            def norm_round(tag, hi, shift, streams_):
                for c in range(DC):
                    act.wait_ge(*after("normed", (tag, c)))
                    for st, cols in streams_:
                        if shift is None:
                            i = copy(hi[:, c, cols], nb[:, c % 4, cols])
                        else:
                            i = act.activation(hi[:, c, cols], nb[:, c % 4, cols], ACT.Identity, bias=shift(c, st))
                        i.then_inc(*(done("norm_hi", (tag, c)) if st == streams_[-1][0] else done("norm_hi_part", (tag, c, st))))

            def network1(layer):
                T = n_tok(layer)
                first_slab = first["l1", layer]
                def shift(row):
                    return lambda c, st: mod[:, layer, row + c, st:st + 1]
                if layer == 0:
                    act.wait_ge(*after("x_in", 0))
                    act.wait_ge(*after("eps_set", 0))
                norm((layer, 1), X, T_BOTH, None if layer == 0 else lambda c: ("down_out", (layer - 1, c)), layer == 0)
                if layer == 0:
                    for u in range(ADA_FIRST):
                        ada_copy(u)
                ahead(first_slab)
                if layer == 0:
                    act.wait_ge(*after("ada_mod", ADA_FIRST - 1))
                norm_round((layer, 1), h_hi, shift(0), parts(0))
                if layer == 0:
                    for u in range(ADA_FIRST, ADA_BUBBLE):
                        ada_copy(u)
                    act.wait_ge(*after("vec_ready", 0))
                    act.dma_start(by_distance, vec[0:12, :].unsqueeze(1).to_broadcast((12, P, VLEN)))\
                        .then_inc(*done("vec_out", 0, 16))

                def attend(kind, n):
                    if kind == "gate":
                        ahead(s + n)
                        act.wait_ge(*after("chunk", (layer, "gate", n)))
                        act.activation(gates[:, n, 0:T], lin[n % 2][:, 0:T], ACT.Tanh, scale=0.5)\
                            .then_inc(*done("gate_out", (layer, n)))
                    elif kind == "Sx":
                        for t in range(2):
                            act.wait_ge(*after("attn_max", (layer, n, t)))
                            m = 4 * (n % 2) + t
                            act.activation(px(n)[:, t, :], bank[sx_bank(n, t)][:, :], ACT.Exp, bias=small[:, m:m + 1],
                                           accum_out=small[:, 8 + m:9 + m]).then_inc(*done("attn_exp", (layer, n, t)))
                        if n and n + 1 < HEADS:
                            load_bias(layer, n + 1)
                    elif kind == "Sc" and layer == 0:
                        act.wait_ge(*after("attn_max", (layer, n, 3)))
                        for t in range(2):
                            m = 4 * (n % 2) + 2 + t
                            act.activation(p_c[:, t, :], aux[2][:, t * 256:(t + 1) * 256], ACT.Exp, bias=small[:, m:m + 1],
                                           accum_out=small[:, 8 + m:9 + m]).then_inc(*done("attn_exp", (layer, n, 2 + t)))
                    elif kind == "T":
                        if n:
                            act.wait_ge(*after("attn_pv", (layer, n - 1)))
                        for t in range(2):
                            act.wait_ge(*after("attn_turned", (layer, n, t)))
                            copy(pt_x[:, :, t * P:(t + 1) * P], bank[sx_bank(n, t)][:, :].rearrange("p (k q) -> p k q", k=4))\
                                .then_inc(*done("attn_pt", (layer, n, t)))
                        if layer == 0:
                            act.wait_ge(*after("attn_turned", (layer, n, 2)))
                            copy(pt_c[:, :, :].rearrange("p k (t q) -> p t k q", t=2),
                                 aux[2][:, :].rearrange("p (t k q) -> p t k q", t=2, k=2))\
                                .then_inc(*done("attn_pt", (layer, n, 2)))
                    elif kind == "V":
                        act.wait_ge(*after("attn_pv", (layer, n)))
                        r = slice((n % 2) * HD, (n % 2) * HD + HD)
                        copy(at_hi[r, n // 2, 0:T], aux[3][r, 0:T]).then_inc(*done("attn_hi", (layer, n)))
                    elif kind == "var":
                        ahead(s + 2 * DC)
                        for c in range(CONV_C):
                            act.wait_ge(*after("conv_centred", (layer, c)))
                            if c >= 2:
                                act.wait_ge(*after("ln_var", (layer, c - 2)))
                            act.activation(sq[:, c % 2, 0:T], cv[:, c, 0:T], ACT.Square).then_inc(*done("ln_sq", (layer, c)))

                def ada_here(i):
                    if layer == 0 and i < ADA_UNITS - ADA_BUBBLE:
                        ada_copy(ADA_BUBBLE + i)
                s = first_slab
                for c in range(CONV_C):
                    ahead(s)
                    act.wait_ge(*after("chunk", (layer, "glu_g", c)))
                    if c >= 2:
                        act.wait_ge(*after("glu_out", (layer, c - 2)))
                    act.activation(glu_t[:, c % 2, 0:T], lin[(2 * c) % 4][:, 0:T], ACT.Tanh, scale=0.5)\
                        .then_inc(*done("glu_tanh", (layer, c)))
                    ada_here(2 * c)
                    ahead(s + 1)
                    ada_here(2 * c + 1)
                    s += 2
                for c in range(2 * QC):
                    ahead(s)
                    act.wait_ge(*after("chunk", (layer, "qk", c)))
                    Tq = T if c < QC else T_BOTH
                    dst = (qT[:, c, 0:Tq] if c < QC else kT[:, c - QC, 0:Tq])
                    copy(dst, lin[c % 4][:, 0:Tq], scale=HD ** -0.5 if c < QC else 1.0)\
                        .then_inc(*done("qk_out", (layer, c)))
                    ada_here(GLU_SLABS + c)
                    s += 1
                act.wait_ge(*after("glu_out", (layer, CONV_C - 1)))
                act.wait_ge(*after(f"rpb_rows{layer}", HEADS - 1))
                load_bias(layer, 0)
                for q in range(QKV_V_SLABS):
                    ahead(s + q)
                    ada_here(GLU_SLABS + 2 * QC + q)
                attend("Sx", 0)
                for tt in range(4):
                    act.wait_ge(*after("chunk", (layer, "v", tt)))
                    copy(V[:, tt, :], lin[tt][:, :]).then_inc(*done("v_out", (layer, tt)))
                s += QKV_V_SLABS
                if layer == 0:
                    act.wait_ge(*after("ada_turned", ADA_UNITS - 1))
                load_bias(layer, 1)
                attend("Sc", 0)
                for step in L1_PLAN:
                    attend(*step)
                s += 2 * DC
                act.wait_ge(*after("ln_var", (layer, CONV_C - 1)))
                root(rinv[:, 0:T], aux[1][:, 0:T], "ln_root", layer)
                for c in range(CONV_C + 1):
                    if c < CONV_C:
                        act.wait_ge(*after("conv_affine", (layer, c)))
                        act.activation(sq[:, c % 2, 0:T], nb[:, c, 0:T], ACT.Tanh).then_inc(*done("conv_tanh", (layer, c)))
                    if c:
                        act.wait_ge(*after("conv_silu", (layer, c - 1)))
                        copy(cv_hi[:, c - 1, 0:T], nb[:, c - 1, 0:T]).then_inc(*done("conv_hi", (layer, c - 1)))
                for m in range(DC):
                    ahead(s)
                    act.wait_ge(*after("merged", (layer, m)))
                    copy(y_hi[:, m, 0:T], nr[:, m % 2, 0:T]).then_inc(*done("merge_hi", (layer, m)))
                    s += 1
                s += DC
                norm((layer, 2), X, T, lambda c: ("mix_out", (layer, c)), False, s - DC)
                norm_round((layer, 2), h_hi, shift(3 * DC), parts(layer))

                def up(j, b, it=None):
                    plus = 0 if it is None else it * 4
                    for w, buf in enumerate((up_a, up_g)):
                        if it is None:
                            ahead(s + 2 * j + w)
                        else:
                            round_weights(nxt[0] + 2 * b + w, it)
                        act.wait_ge(sem("slab_used"), s + 2 * j + w + 1 + plus * 2)
                        if j >= 2 or it is not None:
                            act.wait_ge(sem("up_out"), base_up + j - 1 + plus)
                        cc = w * FF_C + j
                        wcol, bcol = par(layer, "fdw", 2 * FF_C + cc, plus), par(layer, "fdwb", cc, plus)
                        ps = lin[(2 * b + w) % 4]
                        act.activation(buf[:, b % 2, 0:T], ps[:, 0:T], ACT.Identity, bias=bcol, scale=wcol)\
                            .then_inc(*done("up_mid", (layer, j, w)))
                    act.wait_ge(sem("up_conv"), 2 * (base_up + j + 1) + plus * 2)
                    act.activation(up_t[:, b % 2, 0:T], up_g[:, b % 2, 0:T], ACT.Tanh)\
                        .then_inc(*done("up_tanh", (layer, j)))

                base_up = FF_C * layer
                s_down = s + 2 * FF_C

                def down(j, b, it=None):
                    plus = 0 if it is None else it * 8
                    if it is not None or j >= 2:
                        act.wait_ge(sem("slab_used"), s_down + j - 1 + plus)
                    src = ffa[:, j, 0:T] if it is None else ffa[:, bass.ds(j + plus, 1), 0:T].rearrange("p a t -> p (a t)")
                    if j < 2:
                        act.wait_ge(*after("up_out", (layer, j)))
                    if j == 2:
                        act.wait_ge(*after("up_all", layer))
                    if j == 2 and layer == DEPTH - 1:
                        act.wait_ge(*after("vec_out", 0))
                        act.dma_start(H[:, :, 0:META], A["meta"]).then_inc(*done("meta_in", 0, 16))
                        act.dma_start(wi_r[:, :, :], A["wi"][0]).then_inc(*done("wi_in", 0, 16))
                        act.dma_start(lamp[:, :], A["lam"][0:1, :].to_broadcast((P, P))).then_inc(*done("lam_in", 0, 16))
                        act.dma_start(decay0[0:16, :, :], tb[0:16, TAB["decay0"][0]:TAB["decay0"][1]]
                                      .rearrange("p (h n) -> p h n", h=4)).then_inc(*done("tab2_in", 0, 16))
                        nh = A_HEADS + B_HEADS
                        for r, (lo, n, off) in enumerate(((S1, N1, T2 - 1 - META), (S2, N2, T2 - 1 - META - P), (S0, N0, T2 - 1))):
                            act.dma_start(bias2[:, :, lo:lo + n],
                                          bass.AP(by_distance.tensor, off, [[VLEN - 1, P], [P * VLEN, nh], [1, n]]))\
                                .then_inc(*done("bias2_in", r, 16))
                    copy(dn_hi[:, j % 2, 0:T], src).then_inc(*done("down_hi", (layer, j)))
                    if it is None:
                        if j >= 2:
                            ahead(s_down + j)
                    else:
                        round_weights(nxt[0] + b, it)
                for j in range(2):
                    up(j, j)
                for j in range(2):
                    down(j, j)
                up_first = nxt[0]
                with act.Fori(0, 5) as it:
                    for b in range(4):
                        up(2 + b, b, it)
                nxt[0] = up_first + 40
                again("up_mid", 4 * 2 * 4)
                again("up_tanh", 4 * 4)
                s += 2 * FF_C

                ahead(s)
                ahead(s + 1)
                for j in range(2, 5):
                    down(j, j)
                dn_first = nxt[0]
                with act.Fori(0, 2) as it:
                    for b in range(8):
                        down(5 + b, b, it)
                nxt[0] = dn_first + 16
                again("down_hi", 8)
                down(FF_C - 1, 0)

            def network2(layer):
                s = first["l2", layer]
                tag = ("n2", layer)
                if layer == 0:
                    norm(("fin", 1), X, SEQ, lambda c: ("down_out", (1, c)), False)
                    act.wait_ge(*after("meta_in", 0))
                else:
                    act.dma_start(lamp[:, :], A["lam"][layer:layer + 1, :].to_broadcast((P, P)))\
                        .then_inc(*done("lam_in", layer, 16))
                    act.dma_start(wi_r[:, :, :], A["wi"][layer]).then_inc(*done("wi_in", layer, 16))
                norm((layer, 3), H, T2, lambda c: ("fin1", c) if layer == 0 else ("ff2_out", (0, c)), layer == 0)
                if layer == 0:
                    act.dma_start(tab2[:, :], tb[:, TAB["cos2"][0]:TAB["decay1"][1]]).then_inc(*done("tab2_in", 1, 16))
                ahead(s)
                both = [(0, slice(0, T2))]
                norm_round((layer, 3), u_hi, None, both)
                act.wait_ge(*after("wi_in", layer))
                copy(wi_w[:, 0, :, :], wi_r[:, :, :]).then_inc(*done("wi_hi", layer))
                act.wait_ge(*after("lam_sum", (layer, 1)))
                act.activation(lam[:, 2:4], lam[:, 0:2], ACT.Exp).then_inc(*done("lam_exp", layer))
                for step in L2_PLAN:
                    kind, k = step[0:2]
                    if kind == "slab":
                        c = k
                        ahead(s + L2_AT[step])
                        act.wait_ge(*after("chunk", (layer, "p2", c)))
                        ps = lin[l2_bank(step)][:, 0:T2]
                        if c >= GC:
                            act.activation(nt[:, c % 2, 0:T2], ps, ACT.Tanh, scale=0.5).then_inc(*done("p2_out", (layer, c)))
                        else:
                            scale = HD ** -0.5 if QA <= c < KA or KCR <= c < QB else 32 ** -0.5 if QB <= c < KB else 1.0
                            copy(pj[:, c, :], ps, scale=scale).then_inc(*done("p2_out", (layer, c)))
                    elif kind == "vals":
                        ahead(s + L2_AT[step])
                        if step[2] == 3:
                            for tt in range(3):
                                n = P if tt else META
                                act.wait_ge(*after("chunk", (layer, "v2", k, tt)))
                                copy(V2[0:n, tt, k * 512:(k + 1) * 512], lin[(l2_bank(step) + tt) % 4][0:n, :])\
                                    .then_inc(*done("v2_out", (layer, k, tt)))
                    elif kind == "index":
                        act.wait_ge(*after("index_dot", (layer, k)))
                        if k >= 2:
                            act.wait_ge(*after("index_sum", (layer, k - 2)))
                        act.activation(relu2[:, k % 2, :], aux[k % 2][:, 0:N1 + N2], ACT.Relu)\
                            .then_inc(*done("index_relu", (layer, k)))
                    elif kind == "S" and UNITS[k][0] != "c":
                        act.wait_ge(*after("max2", (layer, k, 2)))
                        if k >= 3:
                            act.wait_ge(*after("prob2", (layer, k - 2)))
                            if UNITS[k - 3][0] != "c" and UNITS[k - 3][0::2] != ("b", 0):
                                act.wait_ge(*after("turned2", (layer, k - 3)))
                        for t, (lo, n) in enumerate(TILES):
                            m = 3 * (k % 3) + t
                            act.activation(p2[:, k % 3, lo:lo + n], aux[k % 2][:, lo:lo + n], ACT.Exp,
                                           bias=small[:, m:m + 1], accum_out=small[:, 9 + m:10 + m])\
                                .then_inc(*done("exp2", (layer, k, t)))
                    elif kind == "T" and UNITS[k][0] != "c" and UNITS[k][0::2] != ("b", 0):
                        if k >= 2 and has_values(k - 2):
                            act.wait_ge(*after("pv2", (layer, k - 2)))
                        act.wait_ge(*after("turned2", (layer, k)))
                        copy(pt0[0:META, k % 2, :], aux[k % 2][0:META, 0:T2]).then_inc(*done("pt2", (layer, k, 0)))
                        copy(pt1[:, k % 2, :], aux[2][:, 0:384]).then_inc(*done("pt2", (layer, k, 1)))
                    elif kind == "V" and has_values(k):
                        name, h, _ = UNITS[k]
                        act.wait_ge(*after("pv2", (layer, k)))
                        r = slice((h % 2) * HD, (h % 2) * HD + HD)
                        if name == "a":
                            dst = o_hi[r, h // 2, :]
                        else:
                            dst = bc_raw[r, h // 2 + (2 if name == "c" else 0), :]
                        copy(dst, aux[3][r, 0:T2]).then_inc(*done("unit_out", (layer, k)))
                act.wait_ge(*after("unit_out", (layer, N_UNITS - 1)))
                for c in range(4):
                    if c >= 2:
                        act.wait_ge(*after("bc_summed", (layer, c - 2)))
                    act.activation(sq[:, c % 2, 0:T2], bc_raw[:, c, :], ACT.Square).then_inc(*done("bc_sq", (layer, c)))
                for c in range(4):
                    act.wait_ge(*after("bc_summed", (layer, c)))
                    root(bc_r[:, c, :], aux[c][:, 0:T2], "bc_root", (layer, c))
                for c in range(4):
                    act.wait_ge(*after("bc_normed", (layer, c)))
                    copy(o_hi[:, 4 + c, :], nr[:, c % 2, 0:T2]).then_inc(*done("bc_hi", (layer, c)))
                s += L2_FRONT + 8
                norm((layer, 4), H, T2, lambda c: ("mix2_out", (layer, c)), False, s)
                s += DC
                norm_round((layer, 4), u_hi, None, both)

                def ff1(j, b, it=None):
                    plus = 0 if it is None else it * 8
                    if it is None:
                        ahead(s + j)
                    else:
                        round_weights(nxt[0] + b, it)
                    act.wait_ge(sem("slab_used"), s + j + 1 + plus)
                    if it is not None or j >= 2:
                        act.wait_ge(sem("ff1_out"), base + j - 1 + plus)
                    act.activation(up_t[:, b % 2, 0:T2], lin[b % 4][:, 0:T2], ACT.Relu).then_inc(*done("ff1_relu", (layer, j)))
                base = FF2_C * layer
                s_ff2 = s + FF2_C

                def ff2(j, b, it=None):
                    plus = 0 if it is None else it * 8
                    if it is not None or j >= 2:
                        act.wait_ge(sem("slab_used"), s_ff2 + j - 1 + plus)
                    src = ff2a[:, j, :] if it is None else ff2a[:, bass.ds(j + plus, 1), :].rearrange("p a t -> p (a t)")
                    if j < 2:
                        act.wait_ge(*after("ff1_out", (layer, j)))
                    if j == 2:
                        act.wait_ge(*after("ff1_all", layer))
                    copy(dn_hi[:, j % 2, 0:T2], src).then_inc(*done("ff2_hi", (layer, j)))
                    if it is None:
                        if j >= 2:
                            ahead(s_ff2 + j)
                    else:
                        round_weights(nxt[0] + b, it)
                for j in range(8):
                    ff1(j, j)
                for j in range(2):
                    ff2(j, j)
                f1 = nxt[0]
                with act.Fori(0, 3) as it:
                    for b in range(8):
                        ff1(8 + b, b, it)
                nxt[0] = f1 + 24
                again("ff1_relu", 16)
                s += FF2_C

                ahead(s)
                ahead(s + 1)
                for j in range(2, 7):
                    ff2(j, j)
                reps = 3 if layer == 0 else 2
                f2 = nxt[0]
                with act.Fori(0, reps) as it:
                    for b in range(8):
                        ff2(7 + b, b, it)
                nxt[0] = f2 + reps * 8
                again("ff2_hi", 8 * (reps - 1))
                for j in range(7 + reps * 8, FF2_C):
                    ff2(j, j)

            for layer in range(DEPTH):
                network1(layer)
            for layer in range(DEPTH):
                network2(layer)
            norm(("fin", 2), H, T2, lambda c: ("ff2_out", (1, c)), False)

        @block.tensor
        def _(pe):
            readers = {}

            def claim(b):
                if b in readers:
                    pe.wait_ge(*after(*readers.pop(b)))

            def weights(i, it=None):
                pe.wait_ge(sem("w_lo_ready"), i + 1 + (0 if it is None else it * 8))

            def three(o, i, k, a_hi, a_lo, start, stop, col=None):
                s = i % RING
                hi, lo = w_hi[:, s, k * P:(k + 1) * P], w_lo[:, s, k * P:(k + 1) * P]
                pe.matmul(o, hi, a_hi, start=start, stop=False)
                pe.matmul(o, hi, a_lo, start=False, stop=False)
                return pe.matmul(o, lo, a_hi, start=False, stop=stop)

            def chunk(i, b, T, a_hi, a_lo, key, reader, h_key=None):
                weights(i)
                claim(b)
                for k in range(DC):
                    if h_key:
                        pe.wait_ge(*after("norm_lo", (h_key, k)))
                    mm = three(bank[b][:, 0:T], i, k, a_hi[:, k, 0:T], a_lo[:, k, 0:T], k == 0, k == DC - 1)
                mm.then_inc(*done("slab_used", i))
                seen["chunk", key] = seen["slab_used", i]
                readers[b] = reader

            def norm_sum(tag, T, summed=True):
                claim(4)
                if not summed:
                    pe.wait_ge(*after("norm_added", (tag, DC - 1)))
                    pe.matmul(aux[0][:, 0:T], ones_d, rinv[:, 0:T], start=True, stop=True)\
                        .then_inc(*done("norm_summed", (tag, DC - 1)))
                for c in range(DC if summed else 0):
                    pe.wait_ge(*after("norm_sq", (tag, c)))
                    pe.matmul(aux[0][:, 0:T], ones_d, sq[:, c % 2, 0:T], start=c == 0, stop=c == DC - 1)\
                        .then_inc(*done("norm_summed", (tag, c)))
                readers[4] = ("norm_root", tag)

            def ada_turn(u):
                pe.wait_ge(*after("ada_part_out", u))
                for j in range(4):
                    mm = pe.matmul(aux[2 + u % 2][:, 2 * j:2 * j + 2], ada_part[:, u % 2, j * P:(j + 1) * P], sel,
                                   start=True, stop=True)
                mm.then_inc(*done("ada_turned", u))
                readers[6 + u % 2] = ("ada_mod", u)

            def ada(u):
                claim(6 + u % 2)
                for q in range(4):
                    a = 4 * u + q
                    pe.wait_ge(*ada_landed(a))
                    for j in range(2):
                        k = 2 * q + j
                        g = 32 * (k % 4)
                        mm = pe.matmul(aux[2 + u % 2][g:g + 32, :], cs[:, k, :], ada_raw[:, a % ADA_RING, j * 512:(j + 1) * 512],
                                       start=k < 4, stop=k >= 4, tile_position=(0, g))
                    mm.then_inc(*done("ada_slab_read", a))
                if u and u != ADA_FIRST:
                    ada_turn(u - 1)
                if u == ADA_FIRST - 1:
                    ada_turn(u)

            def network1(layer):
                T = n_tok(layer)
                norm_sum((layer, 1), T_BOTH, summed=layer == 0)
                if layer == 0:
                    for u in range(ADA_BUBBLE):
                        ada(u)

                def ada_here(i):
                    if layer == 0 and i < ADA_UNITS - ADA_BUBBLE:
                        ada(ADA_BUBBLE + i)
                    elif layer == 0 and i == ADA_UNITS - ADA_BUBBLE:
                        ada_turn(ADA_UNITS - 1)
                s = first["l1", layer]
                for c in range(CONV_C):
                    chunk(s, (2 * c) % 4, T, h_hi, h_lo, (layer, "glu_g", c), ("glu_tanh", (layer, c)),
                          (layer, 1) if c == 0 else None)
                    ada_here(2 * c)
                    chunk(s + 1, (2 * c + 1) % 4, T, h_hi, h_lo, (layer, "glu_a", c), ("glu_out", (layer, c)))
                    ada_here(2 * c + 1)
                    s += 2
                for c in range(2 * QC):
                    Tq = T if c < QC else T_BOTH
                    chunk(s, c % 4, Tq, h_hi, h_lo, (layer, "qk", c), ("qk_out", (layer, c)))
                    if c:
                        rope(layer, c - 1)
                    ada_here(GLU_SLABS + c)
                    s += 1
                for q in range(QKV_V_SLABS):
                    weights(s)
                    for j in range(2):
                        k = 2 * q + j
                        wh, wl = (w[:, s % RING, j * 512:(j + 1) * 512] for w in (w_hi, w_lo))
                        for tt in range(4):
                            if k == 0:
                                claim(tt)
                            a, b = (x[:, k, tt * P:(tt + 1) * P] for x in (h_hi, h_lo))
                            pe.matmul(lin[tt][:, :], a, wh, start=k == 0, stop=False)
                            pe.matmul(lin[tt][:, :], b, wh, start=False, stop=False)
                            mm = pe.matmul(lin[tt][:, :], a, wl, start=False, stop=k == DC - 1)
                    mm.then_inc(*done("slab_used", s))
                    if q == 0:
                        rope(layer, 2 * QC - 1)
                    ada_here(GLU_SLABS + 2 * QC + q)
                    if q == 2:
                        scores_x(layer, 0)
                    s += 1
                for tt in range(4):
                    seen["chunk", (layer, "v", tt)] = seen["slab_used", s - 1]
                    readers[tt] = ("v_out", (layer, tt))
                scores_c(layer, 0)
                for kind, n in L1_PLAN:
                    if kind == "gate":
                        chunk(s + n, n % 2, T, h_hi, h_lo, (layer, "gate", n), ("gate_out", (layer, n)))
                    elif kind == "Sx":
                        scores_x(layer, n)
                    elif kind == "Sc":
                        scores_c(layer, n)
                    elif kind == "T":
                        turn(layer, n)
                    elif kind == "V":
                        values(layer, n)
                    elif kind == "mean":
                        claim(4)
                        for c in range(CONV_C):
                            pe.wait_ge(*after("conv_tap", (layer, c, TAPS - 1)))
                            mm = pe.matmul(aux[0][:, 0:T], ones_c, cv[:, c, 0:T], start=c == 0, stop=c == CONV_C - 1)
                        mm.then_inc(*done("ln_mean", layer))
                        readers[4] = ("conv_centred", (layer, CONV_C - 1))
                    elif kind == "var":
                        claim(5)
                        for c in range(CONV_C):
                            pe.wait_ge(*after("ln_sq", (layer, c)))
                            pe.matmul(aux[1][:, 0:T], ones_c, sq[:, c % 2, 0:T], start=c == 0, stop=c == CONV_C - 1)\
                                .then_inc(*done("ln_var", (layer, c)))
                        readers[5] = ("ln_root", layer)
                s += 2 * DC

                def attention_branch(m):
                    weights(s + m)
                    claim(m % 4)
                    if m == 0:
                        pe.wait_ge(*after("attn_lo", (layer, HEADS - 1)))
                    for k in range(4):
                        three(bank[m % 4][:, 0:T], s + m, 4 + k, at_hi[:, k, 0:T], at_lo[:, k, 0:T], k == 0, k == 3)

                def conv_branch(m):
                    b = 4 + m % 4
                    claim(b)
                    for k in range(4):
                        if m == 0:
                            pe.wait_ge(*after("conv_lo", (layer, k)))
                        mm = three(bank[b][:, 0:T], s + m, k, cv_hi[:, k, 0:T], cv_lo[:, k, 0:T], k == 0, k == 3)
                    mm.then_inc(*done("slab_used", s + m))
                    seen["chunk", (layer, "branch", m)] = seen["slab_used", s + m]
                    readers[b] = readers[m % 4] = ("merged", (layer, m))
                for m in range(RING):
                    attention_branch(m)
                for m in range(RING):
                    conv_branch(m)
                for m in range(RING, DC):
                    attention_branch(m)
                    conv_branch(m)
                s += DC
                for m in range(DC):
                    if m == 0:
                        pe.wait_ge(*after("merge_lo", (layer, DC - 1)))
                    chunk(s, m % 4, T, y_hi, y_lo, (layer, "mix", m), ("mix_out", (layer, m)))
                    s += 1
                norm_sum((layer, 2), T, summed=False)

                def up(j, b, it=None):
                    plus = 0 if it is None else it * 4
                    for w in range(2):
                        i = s + 2 * j + w
                        weights(i, it)
                        bk = (2 * b + w) % 4
                        if it is None:
                            claim(bk)
                        else:
                            pe.wait_ge(sem("up_conv"), 2 * (FF_C * layer + j - 2) + w + 1 + plus * 2)
                        for k in range(DC):
                            if j == 0 and w == 0:
                                pe.wait_ge(*after("norm_lo", ((layer, 2), k)))
                            mm = three(bank[bk][:, 0:T], i, k, h_hi[:, k, 0:T], h_lo[:, k, 0:T], k == 0, k == DC - 1)
                        mm.then_inc(*done("slab_used", i))
                for j in range(2):
                    up(j, j)
                with pe.Fori(0, 5) as it:
                    for b in range(4):
                        up(2 + b, b, it)
                again("slab_used", 4 * 8)
                s += 2 * FF_C

                def down(j, ms, it=None):
                    plus = 0 if it is None else it * 8
                    weights(s + j, it)
                    pe.wait_ge(sem("down_lo"), FF_C * layer + j + 1 + plus)
                    for m in ms:
                        if j == 0:
                            claim(m)
                        mm = three(bank[m][:, 0:T], s + j, m, dn_hi[:, j % 2, 0:T], dn_lo[:, j % 2, 0:T],
                                   j == 0, j == FF_C - 1)
                        if j == FF_C - 1 and m < DC - 1:
                            mm.then_inc(*done("down_sum", (layer, m)))
                    return mm

                down(0, range(4, DC))
                down(1, range(4, DC))
                pe.wait_ge(*after("up_all", layer))
                down(0, range(4)).then_inc(*done("slab_used", s))
                down(1, range(4)).then_inc(*done("slab_used", s + 1))
                for j in range(2, 5):
                    down(j, range(DC)).then_inc(*done("slab_used", s + j))
                with pe.Fori(0, 2) as it:
                    for b in range(8):
                        down(5 + b, range(DC), it).then_inc(*done("slab_used", s + 5 + b))
                again("slab_used", 8)
                down(FF_C - 1, range(DC)).then_inc(*done("slab_used", s + FF_C - 1))
                seen["chunk", (layer, "down")] = counts["slab_used"]
                for m in range(DC):
                    readers[m] = ("down_out", (layer, m))

            def rope(layer, c):
                claim(5)
                src = qT[:, c, 0:SEQ] if c < QC else kT[:, c - QC, 0:SEQ]
                pe.wait_ge(*after("qk_out", (layer, c)))
                pe.matmul(aux[1][:, 0:SEQ], perm1, src, start=True, stop=True).then_inc(*done("rope_turn", (layer, c)))
                readers[5] = ("rope_part", (layer, c))

            def scores_x(layer, h):
                r = slice((h % 2) * HD, (h % 2) * HD + HD)
                c = h // 2
                pe.wait_ge(*after("rope_out", (layer, 2 * QC - 1)))
                for t in range(2):
                    b = sx_bank(h, t)
                    claim(b)
                    pe.matmul(bank[b][:, :], qT[r, c, t * P:(t + 1) * P], kT[r, c, :], start=True, stop=True)\
                        .then_inc(*done("attn_score", (layer, h, t)))
                    readers[b] = ("attn_exp", (layer, h, t))

            def scores_c(layer, h):
                r = slice((h % 2) * HD, (h % 2) * HD + HD)
                c = h // 2
                if layer == 0:
                    claim(6)
                    for t in range(2):
                        pe.matmul(aux[2][:, t * 256:(t + 1) * 256], qT[r, c, SEQ + t * P:SEQ + (t + 1) * P],
                                  kT[r, c, SEQ:T_BOTH], start=True, stop=True)\
                            .then_inc(*done("attn_score", (layer, h, 2 + t)))

            def turn(layer, h):
                for t in range(2):
                    b = sx_bank(h, t)
                    pe.wait_ge(*after("attn_prob", (layer, h, t)))
                    for k in range(4):
                        mm = pe.transpose(bank[b][:, k * P:(k + 1) * P], px(h)[:, t, k * P:(k + 1) * P], ident)
                    mm.then_inc(*done("attn_turned", (layer, h, t)))
                    readers[b] = ("attn_pt", (layer, h, t))
                if layer == 0:
                    pe.wait_ge(*after("attn_prob", (layer, h, 3)))
                    for t in range(2):
                        for k in range(2):
                            mm = pe.transpose(aux[2][:, (2 * t + k) * P:(2 * t + k + 1) * P],
                                              p_c[:, t, k * P:(k + 1) * P], ident)
                    mm.then_inc(*done("attn_turned", (layer, h, 2)))
                    readers[6] = ("attn_pt", (layer, h, 2))

            def values(layer, h):
                r = slice((h % 2) * HD, (h % 2) * HD + HD)
                claim(7)
                pe.wait_ge(*after("v_out", (layer, 3)))
                pe.wait_ge(*after("attn_pt", (layer, h, 2 if layer == 0 else 1)))
                for k in range(4):
                    mm = pe.matmul(aux[3][r, 0:SEQ], V[:, k, h * HD:(h + 1) * HD], pt_x[:, k, :],
                                   start=k == 0, stop=k == 3)
                if layer == 0:
                    for k in range(2):
                        mm = pe.matmul(aux[3][r, SEQ:T_BOTH], V[:, 2 + k, h * HD:(h + 1) * HD], pt_c[:, k, :],
                                       start=k == 0, stop=k == 1)
                mm.then_inc(*done("attn_pv", (layer, h)))
                readers[7] = ("attn_lo", (layer, h))

            def network2(layer):
                s = first["l2", layer]
                if layer == 0:
                    norm_sum(("fin", 1), SEQ, summed=False)
                norm_sum((layer, 3), T2, summed=layer == 0)
                fresh = True
                for step in L2_PLAN:
                    kind, k = step[0:2]
                    if kind == "slab":
                        reader = ("p2_out", (layer, k)) if k < GC else ("gate2", (layer, k))
                        chunk(s + L2_AT[step], l2_bank(step), T2, u_hi, u_lo, (layer, "p2", k), reader,
                              (layer, 3) if fresh else None)
                        fresh = False
                        if QCR < k < QB:
                            rope2(layer, k - 1)
                    elif kind == "vals":
                        q = step[2]
                        i = s + L2_AT[step]
                        weights(i)
                        for j in range(2):
                            kk = 2 * q + j
                            wh, wl = (w[:, i % RING, j * 512:(j + 1) * 512] for w in (w_hi, w_lo))
                            for tt in range(3):
                                b = (l2_bank(step) + tt) % 4
                                if kk == 0:
                                    claim(b)
                                t0 = 0 if tt == 0 else META + (tt - 1) * P
                                a, al = (x[:, kk, t0:t0 + P] for x in (u_hi, u_lo))
                                pe.matmul(lin[b][:, :], a, wh, start=kk == 0, stop=False)
                                pe.matmul(lin[b][:, :], al, wh, start=False, stop=False)
                                mm = pe.matmul(lin[b][:, :], a, wl, start=False, stop=kk == DC - 1)
                        mm.then_inc(*done("slab_used", i))
                        if k == 1 and q == 0:
                            rope2(layer, QB - 1)
                        if q == 3:
                            for tt in range(3):
                                seen["chunk", (layer, "v2", k, tt)] = seen["slab_used", i]
                                readers[(l2_bank(step) + tt) % 4] = ("v2_out", (layer, k, tt))
                    elif kind == "wi":
                        pe.wait_ge(*after("wi_lo", layer))
                        claim(6)
                        for t in range(2):
                            for kk in range(DC):
                                t0 = META + t * P
                                a, al = (x[:, kk, t0:t0 + P] for x in (u_hi, u_lo))
                                o = aux[2][:, 8 * t:8 * t + 8]
                                pe.matmul(o, a, wi_w[:, 0, kk, :], start=kk == 0, stop=False)
                                pe.matmul(o, al, wi_w[:, 0, kk, :], start=False, stop=False)
                                mm = pe.matmul(o, a, wi_w[:, 1, kk, :], start=False, stop=kk == DC - 1)
                        mm.then_inc(*done("wi_made", layer))
                        readers[6] = ("wi_out", layer)
                    elif kind == "index":
                        r = slice((k % 2) * HD, (k % 2) * HD + HD)
                        claim(4 + k % 2)
                        pe.wait_ge(*after("p2_out", (layer, QI + 3)))
                        q = pj[r, QI + k // 2, :]
                        pe.matmul(aux[k % 2][:, S1:S1 + N1], q[:, META:META + P], pj[r, KI, 0:N1], start=True, stop=True)
                        pe.matmul(aux[k % 2][:, S2:S2 + N2], q[:, META + P:T2], pj[r, KI, 0:N2], start=True, stop=True)\
                            .then_inc(*done("index_dot", (layer, k)))
                        readers[4 + k % 2] = ("index_relu", (layer, k))
                    elif kind == "S" and UNITS[k][0] != "c" or kind == "T" and UNITS[k][0] == "c":
                        scores2(layer, k)
                    elif kind == "T" and has_values(k):
                        turn2(layer, k)
                    elif kind == "V" and has_values(k):
                        values2(layer, k)
                for c in range(4):
                    pe.wait_ge(*after("bc_sq", (layer, c)))
                    claim(4 + c)
                    pe.matmul(aux[c][:, 0:T2], ones_h, sq[:, c % 2, 0:T2], start=True, stop=True)\
                        .then_inc(*done("bc_summed", (layer, c)))
                    readers[4 + c] = ("bc_root", (layer, c))
                s += L2_FRONT + 8
                for m in range(DC):
                    if m == 0:
                        pe.wait_ge(*after("unit_lo", (layer, A_HEADS - 1)))
                        pe.wait_ge(*after("bc_lo", (layer, 3)))
                    chunk(s, m % 4, T2, o_hi, o_lo, (layer, "mix2", m), ("mix2_out", (layer, m)))
                    s += 1
                norm_sum((layer, 4), T2, summed=False)

                def ff1(j, b, it=None):
                    plus = 0 if it is None else it * 8
                    weights(s + j, it)
                    if it is None:
                        if j < 4:
                            claim(b % 4)
                        else:
                            pe.wait_ge(*after("ff1_out", (layer, j - 4)))
                    else:
                        pe.wait_ge(sem("ff1_out"), FF2_C * layer + j - 3 + plus)
                    for k in range(DC):
                        if j == 0:
                            pe.wait_ge(*after("norm_lo", ((layer, 4), k)))
                        mm = three(lin[b % 4][:, 0:T2], s + j, k, u_hi[:, k, :], u_lo[:, k, :], k == 0, k == DC - 1)
                    mm.then_inc(*done("slab_used", s + j))
                for j in range(8):
                    ff1(j, j)
                with pe.Fori(0, 3) as it:
                    for b in range(8):
                        ff1(8 + b, b, it)
                again("slab_used", 16)
                s += FF2_C

                def ff2(j, ms, it=None):
                    plus = 0 if it is None else it * 8
                    weights(s + j, it)
                    pe.wait_ge(sem("ff2_lo"), FF2_C * layer + j + 1 + plus)
                    for m in ms:
                        if j == 0:
                            claim(m)
                        mm = three(bank[m][:, 0:T2], s + j, m, dn_hi[:, j % 2, 0:T2], dn_lo[:, j % 2, 0:T2], j == 0, j == FF2_C - 1)
                        if j == FF2_C - 1 and m < DC - 1:
                            mm.then_inc(*done("ff2_sum", (layer, m)))
                    return mm

                ff2(0, range(4, DC))
                ff2(1, range(4, DC))
                pe.wait_ge(*after("ff1_all", layer))
                ff2(0, range(4)).then_inc(*done("slab_used", s))
                ff2(1, range(4)).then_inc(*done("slab_used", s + 1))
                for j in range(2, 7):
                    ff2(j, range(DC)).then_inc(*done("slab_used", s + j))
                with pe.Fori(0, 3) as it:
                    for b in range(8):
                        ff2(7 + b, range(DC), it).then_inc(*done("slab_used", s + 7 + b))
                again("slab_used", 16)
                ff2(FF2_C - 1, range(DC)).then_inc(*done("slab_used", s + FF2_C - 1))
                seen["chunk", (layer, "ff2")] = counts["slab_used"]
                for m in range(DC):
                    readers[m] = ("ff2_out", (layer, m))

            def rope2(layer, c):
                claim(5)
                pe.wait_ge(*after("p2_out", (layer, c)))
                pe.matmul(aux[1][:, 0:T2], perm2, pj[:, c, :], start=True, stop=True).then_inc(*done("rope2_turn", (layer, c)))
                readers[5] = ("rope2_part", (layer, c))

            def scores2(layer, t):
                name, h, c = UNITS[t]
                r = slice((h % 2) * HD + 32 * c, (h % 2) * HD + 32 * c + (32 if name == "b" else HD))
                Q, K = {"a": (QA, KA), "b": (QB, KB), "c": (QCR, KCR)}[name]
                q, kk = pj[r, Q + h // 2, :], pj[r, K + h // 2, :]
                if name == "c":
                    pe.wait_ge(*after("rope2_out", (layer, QB - 1)))
                    claim(4 + t % 2)
                    pe.matmul(aux[t % 2][0:META, 0:T2], kk[:, 0:META], q, start=True, stop=True)
                    claim(6)
                    pe.matmul(aux[2][:, 0:256], kk[:, META:META + P], q[:, META:T2], start=True, stop=True)
                    pe.matmul(aux[2][:, 256:384], kk[:, META + P:T2], q[:, META + P:T2], start=True, stop=True)\
                        .then_inc(*done("score2", (layer, t)))
                    readers[4 + t % 2] = ("pt2c", (layer, t, 0))
                    readers[6] = ("pt2c", (layer, t, 1))
                    return
                pe.wait_ge(*after("p2_out", (layer, K + (3 if name == "a" else 1))))
                claim(4 + t % 2)
                o = aux[t % 2]
                pe.matmul(o[:, S1:S1 + N1], q[:, META:META + P], kk[:, 0:N1], start=True, stop=True)
                pe.matmul(o[:, S2:S2 + N2], q[:, META + P:T2], kk[:, 0:N2], start=True, stop=True)
                pe.matmul(o[:, S0:S0 + N0], q[:, 0:P], kk[:, 0:N0], start=True, stop=True)\
                    .then_inc(*done("score2", (layer, t)))
                readers[4 + t % 2] = ("exp2", (layer, t, 2))

            def turn2(layer, t):
                pe.wait_ge(*after("prob2", (layer, t)))
                claim(4 + t % 2)
                pr = p2[:, t % 3, :]
                o0 = aux[t % 2][0:META, :]
                pe.matmul(o0[:, 0:META], pr[0:META, S0:S0 + META], ident[0:META, 0:META], start=True, stop=True)
                pe.matmul(o0[:, META:META + P], pr[:, S1:S1 + META], ident, start=True, stop=True)
                pe.matmul(o0[:, META + P:T2], pr[:, S2:S2 + META], ident, start=True, stop=True)
                claim(6)
                pe.transpose(aux[2][:, 0:P], pr[:, S1 + META:S1 + META + P], ident)
                pe.transpose(aux[2][:, P:2 * P], pr[:, S2 + META:S2 + META + P], ident)
                pe.transpose(aux[2][:, 2 * P:3 * P], pr[:, S2 + META + P:S2 + T2], ident)\
                    .then_inc(*done("turned2", (layer, t)))
                readers[4 + t % 2] = ("pt2", (layer, t, 0))
                readers[6] = ("pt2", (layer, t, 1))

            def values2(layer, t):
                name, h, _ = UNITS[t]
                r = slice((h % 2) * HD, (h % 2) * HD + HD)
                col = {"a": 0, "b": 512, "c": 768}[name] + h * HD
                claim(7)
                pe.wait_ge(*after("pt2c" if name == "c" else "pt2", (layer, t, 1)))
                pe.wait_ge(*after("v2_out", (layer, 0 if name == "a" else 1, 2)))
                pe.matmul(aux[3][r, 0:T2], V2[0:META, 0, col:col + HD], pt0[0:META, t % 2, :], start=True, stop=False)
                pe.matmul(aux[3][r, META:T2], V2[:, 1, col:col + HD], pt1[:, t % 2, 0:256], start=False, stop=False)
                pe.matmul(aux[3][r, META + P:T2], V2[:, 2, col:col + HD], pt1[:, t % 2, 256:384], start=False, stop=True)\
                    .then_inc(*done("pv2", (layer, t)))
                readers[7] = ("unit_lo", (layer, h)) if name == "a" else ("unit_out", (layer, t))

            pe.wait_ge(*after("vec_in", 2))
            for b, (lo, hi) in enumerate(((0, 512), (512, VLEN))):
                mm = pe.matmul(lin[b][0:12, 0:hi - lo], relb[0:32, :], oneh[0:32, 0, lo:hi], start=True, stop=True)
            mm.then_inc(*done("vec_made", 0))
            readers[0] = readers[1] = ("vec_ready", 0)
            pe.wait_ge(*after("const_in", 1))
            pe.wait_ge(*after("c_silu", 0))
            for layer in range(DEPTH):
                network1(layer)
            for layer in range(DEPTH):
                network2(layer)
            norm_sum(("fin", 2), T2, summed=False)

        @block.vector
        def _(dve):
            def tt(o, a, b, op):
                return dve.tensor_tensor(o, a, b, op)

            def ts(o, a, s1, op0, s2=None, op1=None):
                if op1 is None:
                    return dve.tensor_scalar(o, a, s1, None, op0)
                return dve.tensor_scalar(o, a, s1, s2, op0, op1)

            def stt(o, a, s, b, op0, op1):
                return dve.scalar_tensor_tensor(out=o, in0=a, scalar=s, in1=b, op0=op0, op1=op1)

            def inverse(ap, root, name, key):
                dve.wait_ge(*after(root, key))
                dve.reciprocal(ap, ap).then_inc(*done(name, key))
                dve.wait_ge(*after(name, key))

            def norm_add(tag, c, T):
                dve.wait_ge(*after("norm_sq", (tag, c)))
                if c > 1:
                    dve.wait_ge(*after("norm_added", (tag, c - 1)))
                tt(rinv[:, 0:T], rinv[:, 0:T], sq[:, c % 2, 0:T], ALU.add).then_inc(*done("norm_added", (tag, c)))

            def norm(tag, X_, T, hi, lo, scale, shift, streams_):
                inverse(rinv[:, 0:T], "norm_root", "norm_rinv", tag)

                def rest(c):
                    dve.wait_ge(*after("norm_hi", (tag, c)))
                    for st, cols in streams_:
                        h = hi[:, c, cols].bitcast(F32)
                        if shift is None:
                            i = tt(lo[:, c, cols], nb[:, c % 4, cols], h, ALU.subtract)
                        else:
                            i = stt(lo[:, c, cols], nb[:, c % 4, cols], shift(c, st), h, ALU.add, ALU.subtract)
                        i.then_inc(*(done("norm_lo", (tag, c)) if st == streams_[-1][0] else done("norm_lo_part", (tag, c))))
                for c in range(DC):
                    if c >= 4:
                        dve.wait_ge(*after("norm_lo", (tag, c - 4)))
                    for st, cols in streams_:
                        i = stt(nb[:, c % 4, cols], X_[:, c, cols], scale(c, st), rinv[:, cols], ALU.mult, ALU.mult)
                        i.then_inc(*(done("normed", (tag, c)) if st == streams_[-1][0] else done("normed_part", (tag, c))))
                    if c >= 2:
                        rest(c - 2)
                rest(DC - 2)
                rest(DC - 1)

            dve.memset(eps[:, :], EPS).then_inc(*done("eps_set", 0))
            dve.memset(cs[:, :, :], 0.0).then_inc(*done("c_silu_part", 0))
            dve.wait_ge(*after("c_tanh", 0))
            dve.wait_ge(*after("c_silu_part", 0))
            ts(cth[:, :, :], cth[:, :, :], 1.0, ALU.add, 0.5, ALU.mult).then_inc(*done("c_silu_part", 1))
            dve.wait_ge(*after("c_silu_part", 1))
            tt(cs[:, :, 0:2], cth[:, :, :], cvec[:, :, :], ALU.mult).then_inc(*done("c_silu", 0))

            def ada_mod(u):
                layer, n = divmod(u, 12)
                dve.wait_ge(*after("ada_turned", u))
                rows = slice(4 * n, 4 * n + 4)
                b = par(layer, "bada")[:, rows].unsqueeze(2).to_broadcast((P, 4, 2))
                tt(mod[:, layer, rows, :], aux[2 + u % 2][:, 0:8].rearrange("p (c s) -> p c s", s=2), b, ALU.add)\
                    .then_inc(*done("ada_mod", u))
                if n == 3:
                    dve.wait_ge(*after("ada_mod", u))
                    for st in range(2):
                        stt(a1[:, layer, :, st], mod[:, layer, DC:2 * DC, st], 1.0, par(layer, "n1g"), ALU.add, ALU.mult)\
                            .then_inc(*done("scale1_ready", (layer, st)))
                if n == 11:
                    dve.wait_ge(*after("ada_mod", u))
                    for st in range(2):
                        stt(a2[:, layer, :, st], mod[:, layer, 4 * DC:5 * DC, st], 1.0, par(layer, "n2g"), ALU.add, ALU.mult)\
                            .then_inc(*done("mod_part", (layer, st)))
                    ts(gh[:, layer, 0, :, :], mod[:, layer, 2 * DC:3 * DC, :], 0.5, ALU.mult).then_inc(*done("mod_part", (layer, 4)))
                    dve.tensor_copy(gh[:, layer, 1, :, :], mod[:, layer, 5 * DC:6 * DC, :]).then_inc(*done("mod_ready", layer))

            def half_parameters(layer):
                for n, (name, lo, hi) in enumerate((("dw", 0, CONV_C * TAPS), ("lng", 0, CONV_C), ("lnb", 0, CONV_C),
                                                    ("fdwb", FF_C, 2 * FF_C))):
                    v = par(layer, name)[:, lo:hi]
                    ts(v, v, 0.5, ALU.mult).then_inc(*done("prm_half", (layer, n)))
                fdw = par(layer, "fdw").rearrange("p (t c) -> p t c", t=3)[:, :, FF_C:2 * FF_C]
                ts(fdw, fdw, 0.5, ALU.mult).then_inc(*done("prm_half", (layer, 4)))

            def network1(layer):
                T = n_tok(layer)
                if layer:
                    dve.wait_ge(*after("down_done", layer - 1))
                dve.memset(upad[:, :, :, 0:HALO], 0.0).then_inc(*done("halo", (layer, 0)))
                dve.memset(upad[:, :, :, HALO + SEQ:], 0.0).then_inc(*done("halo", (layer, 1)))

                def scale(of):
                    return lambda c, st: of[:, layer, c, st:st + 1]

                def shift(row):
                    return lambda c, st: mod[:, layer, row + c, st:st + 1]

                def ada_here(i):
                    if layer == 0 and i <= ADA_UNITS - ADA_BUBBLE:
                        ada_mod(ADA_BUBBLE + i - 1)
                if layer == 0:
                    for u in range(ADA_FIRST):
                        ada_mod(u)
                    dve.wait_ge(*after("x_in", 0))
                dve.wait_ge(*after("scale1_ready", (layer, 1)))
                norm((layer, 1), X, T_BOTH, h_hi, h_lo, scale(a1), shift(0), parts(0))
                if layer == 0:
                    for u in range(ADA_FIRST, ADA_BUBBLE - 1):
                        ada_mod(u)
                for c in range(CONV_C):
                    ada_here(2 * c)
                    dve.wait_ge(*after("glu_tanh", (layer, c)))
                    dve.wait_ge(*after("chunk", (layer, "glu_a", c), ))
                    n = 2 if layer == 0 else 1
                    stt(upad[:, c, 0:n, HALO:HALO + SEQ], streams(glu_t[:, c % 2, :], layer), 1.0,
                        streams(lin[(2 * c + 1) % 4], layer), ALU.add, ALU.mult).then_inc(*done("glu_out", (layer, c)))
                    ada_here(2 * c + 1)
                taps = [(c, t) for c in range(CONV_C) for t in range(TAPS)]

                def tap(count):
                    for c, t in taps[:count]:
                        n = 2 if layer == 0 else 1
                        src = upad[:, c, 0:n, t:t + SEQ]
                        w = par(layer, "dw", c * TAPS + t)
                        dst = streams(cv[:, c, :], layer)
                        if t == 0:
                            if c == 0:
                                dve.wait_ge(*after("glu_out", (layer, CONV_C - 1)))
                                dve.wait_ge(*after("vec_out", 0))
                            ts(dst, src, w, ALU.mult, par(layer, "dwb", c), ALU.add).then_inc(*done("conv_tap", (layer, c, t)))
                        else:
                            dve.wait_ge(*after("conv_tap", (layer, c, t - 1)))
                            stt(dst, src, w, dst, ALU.mult, ALU.add).then_inc(*done("conv_tap", (layer, c, t)))
                    del taps[:count]

                def biased_max(h, units):
                    bh = biash[:, h % 2, :, :]
                    if 0 in units:
                        dve.wait_ge(*after(f"bias_in{h % 2}", (layer, h, 1, 1)))
                        m = win.unsqueeze(1).to_broadcast((P, 8, GRID_W))
                        tt(bh.rearrange("p t (a b) -> p (t a) b", a=4), bh.rearrange("p t (a b) -> p (t a) b", a=4), m, ALU.add)\
                            .then_inc(*done("bias_masked", (layer, h)))
                        dve.wait_ge(*after("bias_masked", (layer, h)))
                    for u in units:
                        dve.wait_ge(*after("attn_score", (layer, h, u if u < 2 else 3)))
                        if u < 2:
                            ps = bank[sx_bank(h, u)]
                            tt(ps[:, 0:SEQ], ps[:, 0:SEQ], bh[:, u, :], ALU.add).then_inc(*done("attn_added", (layer, h, u)))
                            dve.wait_ge(*after("attn_added", (layer, h, u)))
                            x = ps[:, :]
                        else:
                            x = aux[2][:, (u - 2) * 256:(u - 1) * 256]
                        m = 4 * (h % 2) + u
                        dve.tensor_reduce(small[:, m:m + 1], x, AXX, ALU.max, negate=True).then_inc(*done("attn_max", (layer, h, u)))

                def probabilities(h):
                    for u in [0, 1] + [2, 3] * (layer == 0):
                        m = 16 + 4 * (h % 2) + u
                        dve.wait_ge(*after("attn_exp", (layer, h, u)))
                        dve.reciprocal(small[:, m:m + 1], small[:, m - 8:m - 7]).then_inc(*done("attn_recip", (layer, h, u)))
                        dve.wait_ge(*after("attn_recip", (layer, h, u)))
                        pr = px(h)[:, u, :] if u < 2 else p_c[:, u - 2, :]
                        ts(pr, pr, small[:, m:m + 1], ALU.mult).then_inc(*done("attn_prob", (layer, h, u)))

                def rest(h):
                    r = slice((h % 2) * HD, (h % 2) * HD + HD)
                    dve.wait_ge(*after("attn_hi", (layer, h)))
                    tt(at_lo[r, h // 2, 0:T], aux[3][r, 0:T], at_hi[r, h // 2, 0:T].bitcast(F32), ALU.subtract)\
                        .then_inc(*done("attn_lo", (layer, h)))

                if layer == 0:
                    dve.wait_ge(*after("tab1_in", 0))
                for c in range(2 * QC):
                    ada_here(GLU_SLABS + c)
                    src = qT[:, c, 0:SEQ] if c < QC else kT[:, c - QC, 0:SEQ]
                    dve.wait_ge(*after("rope_turn", (layer, c)))
                    tt(nt[:, c % 2, 0:SEQ], aux[1][:, 0:SEQ], sin1, ALU.mult).then_inc(*done("rope_part", (layer, c)))
                    tt(src, src, cos1, ALU.mult).then_inc(*done("rope_cos", (layer, c)))
                    dve.wait_ge(*after("rope_cos", (layer, c)))
                    dve.wait_ge(*after("rope_part", (layer, c)))
                    tt(src, src, nt[:, c % 2, 0:SEQ], ALU.add).then_inc(*done("rope_out", (layer, c)))
                    if c < 2 * QC - 1:
                        tap(TAPS_QK)
                for q in range(QKV_V_SLABS):
                    ada_here(GLU_SLABS + 2 * QC + q)
                    if q < QKV_V_SLABS - 1:
                        tap(TAPS_V)
                biased_max(0, [0, 1])
                tap(TAPS_V)
                if layer == 0:
                    biased_max(0, [2, 3])
                for kind, h in L1_PLAN:
                    if kind == "Sx":
                        biased_max(h, [0, 1])
                    elif kind == "Sc":
                        if layer == 0:
                            biased_max(h, [2, 3])
                        tap(TAPS_HEAD)
                    elif kind == "T":
                        probabilities(h)
                        if h:
                            rest(h - 1)
                        tap(TAPS_HEAD if h < HEADS - 1 else len(taps))
                    elif kind == "mean":
                        dve.wait_ge(*after("ln_mean", layer))
                        for c in range(CONV_C):
                            tt(cv[:, c, 0:T], cv[:, c, 0:T], aux[0][:, 0:T], ALU.subtract).then_inc(*done("conv_centred", (layer, c)))
                    elif kind == "V" and h == HEADS - 1:
                        rest(h)
                inverse(rinv[:, 0:T], "ln_root", "ln_rstd", layer)
                for c in range(CONV_C + 2):
                    if c < CONV_C:
                        v = nb[:, c, 0:T]
                        stt(v, cv[:, c, 0:T], par(layer, "lng", c), rinv[:, 0:T], ALU.mult, ALU.mult)\
                            .then_inc(*done("conv_scaled", (layer, c)))
                        dve.wait_ge(*after("conv_scaled", (layer, c)))
                        ts(v, v, par(layer, "lnb", c), ALU.add).then_inc(*done("conv_affine", (layer, c)))
                    if 1 <= c <= CONV_C:
                        v = nb[:, c - 1, 0:T]
                        dve.wait_ge(*after("conv_tanh", (layer, c - 1)))
                        stt(v, sq[:, (c - 1) % 2, 0:T], 1.0, v, ALU.add, ALU.mult).then_inc(*done("conv_silu", (layer, c - 1)))
                    if c >= 2:
                        dve.wait_ge(*after("conv_hi", (layer, c - 2)))
                        tt(cv_lo[:, c - 2, 0:T], nb[:, c - 2, 0:T], cv_hi[:, c - 2, 0:T].bitcast(F32), ALU.subtract)\
                            .then_inc(*done("conv_lo", (layer, c - 2)))
                def merge_rest(m):
                    dve.wait_ge(*after("merge_hi", (layer, m)))
                    tt(y_lo[:, m, 0:T], nr[:, m % 2, 0:T], y_hi[:, m, 0:T].bitcast(F32), ALU.subtract)\
                        .then_inc(*done("merge_lo", (layer, m)))
                for m in range(DC):
                    dve.wait_ge(*after("chunk", (layer, "branch", m)))
                    if m == 0:
                        dve.wait_ge(*after("gate_out", (layer, 2 * DC - 1)))
                    if m:
                        dve.wait_ge(*after("merged", (layer, m - 1)))
                    stt(nt[:, 0, 0:T], gates[:, 2 * m, 0:T], 1.0, bank[4 + m % 4][:, 0:T], ALU.add, ALU.mult)\
                        .then_inc(*done("merge_part", (layer, m, 0)))
                    stt(nt[:, 1, 0:T], gates[:, 2 * m + 1, 0:T], 1.0, bank[m % 4][:, 0:T], ALU.add, ALU.mult)\
                        .then_inc(*done("merge_part", (layer, m, 1)))
                    dve.wait_ge(*after("merge_part", (layer, m, 1)))
                    tt(nr[:, m % 2, 0:T], nt[:, 0, 0:T], nt[:, 1, 0:T], ALU.add).then_inc(*done("merged", (layer, m)))
                    if m:
                        merge_rest(m - 1)
                merge_rest(DC - 1)
                dve.wait_ge(*after("mod_ready", layer))
                for m in range(DC):
                    dve.wait_ge(*after("chunk", (layer, "mix", m)))
                    ps = parts(layer)
                    for st, cols in ps:
                        i = stt(X[:, m, cols], lin[m % 4][:, cols], gh[:, layer, 0, m, st:st + 1], X[:, m, cols], ALU.mult, ALU.add)
                        i.then_inc(*(done("mix_out", (layer, m)) if st == ps[-1][0] else done("mix_part", (layer, m))))
                    if m >= 2:
                        norm_add((layer, 2), m - 1, T)
                norm_add((layer, 2), DC - 1, T)
                norm((layer, 2), X, T, h_hi, h_lo, scale(a2), shift(3 * DC), parts(layer))

                base = FF_C * layer

                def up(j, b, it=None):
                    plus = 0 if it is None else it * 4
                    for w, buf in enumerate((up_a, up_g)):
                        cc = w * FF_C + j
                        ps = streams(lin[(2 * b + w) % 4], layer)
                        acc = streams(buf[:, b % 2, :], layer)
                        dve.wait_ge(sem("up_mid"), 2 * (base + j) + w + 1 + plus * 2)
                        for t, (o, i) in ((0, (slice(1, SEQ), slice(0, SEQ - 1))), (2, (slice(0, SEQ - 1), slice(1, SEQ)))):
                            wcol = par(layer, "fdw", t * 2 * FF_C + cc, plus)
                            ins = stt(acc[:, :, o], ps[:, :, i], wcol, acc[:, :, o], ALU.mult, ALU.add)
                            if t == 0:
                                ins.then_inc(*done("up_left", (layer, j, w)))
                                dve.wait_ge(sem("up_left"), 2 * (base + j) + w + 1 + plus * 2)
                            else:
                                ins.then_inc(*done("up_conv", (layer, j, w)))
                    dve.wait_ge(sem("up_tanh"), base + j + 1 + plus)
                    t_ = up_t[:, b % 2, 0:T]
                    stt(t_, t_, 1.0, up_g[:, b % 2, 0:T], ALU.add, ALU.mult).then_inc(*done("up_silu", (layer, j)))
                    dve.wait_ge(sem("up_silu"), base + j + 1 + plus)
                    dst = ffa[:, j, 0:T] if it is None else ffa[:, bass.ds(j + plus, 1), 0:T].rearrange("p a t -> p (a t)")
                    tt(dst, t_, up_a[:, b % 2, 0:T], ALU.mult).then_inc(*done("up_out", (layer, j)))
                def down(j, b, it=None):
                    plus = 0 if it is None else it * 8
                    dve.wait_ge(sem("down_hi"), base + j + 1 + plus)
                    src = ffa[:, j, 0:T] if it is None else ffa[:, bass.ds(j + plus, 1), 0:T].rearrange("p a t -> p (a t)")
                    tt(dn_lo[:, j % 2, 0:T], src, dn_hi[:, j % 2, 0:T].bitcast(F32), ALU.subtract)\
                        .then_inc(*done("down_lo", (layer, j)))
                for j in range(2):
                    up(j, j)
                for j in range(2):
                    down(j, j)
                with dve.Fori(0, 5) as it:
                    for b in range(4):
                        up(2 + b, b, it)
                for n, k in (("up_left", 32), ("up_conv", 32), ("up_silu", 16), ("up_out", 16)):
                    again(n, k)
                seen["up_all", layer] = counts["up_out"]

                for j in range(2, 5):
                    down(j, j)
                with dve.Fori(0, 2) as it:
                    for b in range(8):
                        down(5 + b, b, it)
                again("down_lo", 8)
                down(FF_C - 1, 0)
                ps = parts(layer)
                tag = (layer + 1, 1) if layer + 1 < DEPTH else ("fin", 1)
                n_norm = T_BOTH if layer + 1 < DEPTH else SEQ
                for m in range(DC):
                    dve.wait_ge(*(after("down_sum", (layer, m)) if m < DC - 1 else after("chunk", (layer, "down"))))
                    for st, cols in ps:
                        i = stt(X[:, m, cols], bank[m][:, cols], gh[:, layer, 1, m, st:st + 1], X[:, m, cols], ALU.mult, ALU.add)
                        i.then_inc(*(done("down_out", (layer, m)) if st == ps[-1][0] else done("down_part", (layer, m))))
                    if m >= 2:
                        norm_add(tag, m - 1, n_norm)
                norm_add(tag, DC - 1, n_norm)
                seen["down_done", layer] = seen["down_out", (layer, DC - 1)]

            def rope2(layer, c):
                src = pj[:, c, :]
                dve.wait_ge(*after("rope2_turn", (layer, c)))
                tt(nt[:, c % 2, 0:T2], aux[1][:, 0:T2], sin2, ALU.mult).then_inc(*done("rope2_part", (layer, c)))
                tt(src, src, cos2, ALU.mult).then_inc(*done("rope2_cos", (layer, c)))
                dve.wait_ge(*after("rope2_part", (layer, c)))
                dve.wait_ge(*after("rope2_cos", (layer, c)))
                tt(src, src, nt[:, c % 2, 0:T2], ALU.add).then_inc(*done("rope2_out", (layer, c)))

            def biased_max(layer, t):
                name, h, _ = UNITS[t]
                if name == "c":
                    return
                if layer == 0 and t == 0:
                    dve.wait_ge(*after("bias2_in", 2))
                dve.wait_ge(*after("score2", (layer, t)))
                s = aux[t % 2][:, 0:S_ALL]
                tt(s, s, bias2[:, h if name == "a" else A_HEADS + h, :], ALU.add).then_inc(*done("biased2", (layer, t)))
                dve.wait_ge(*after("biased2", (layer, t)))
                if name == "a":
                    tt(s[:, 0:N1 + N2], s[:, 0:N1 + N2], nsel[:, :], ALU.add).then_inc(*done("chosen2", (layer, t)))
                    dve.wait_ge(*after("chosen2", (layer, t)))
                for n_, (lo, n) in enumerate(TILES):
                    m = 3 * (t % 3) + n_
                    dve.tensor_reduce(small[:, m:m + 1], aux[t % 2][:, lo:lo + n], AXX, ALU.max, negate=True)\
                        .then_inc(*done("max2", (layer, t, n_)))

            def probabilities(layer, t):
                name, h, comp = UNITS[t]
                if name == "c":
                    if layer == 0:
                        dve.wait_ge(*after("tab2_in", 1))
                    dve.wait_ge(*after("score2", (layer, t)))
                    if has_values(t - 2):
                        dve.wait_ge(*after("pv2", (layer, t - 2)))
                    tt(pt0[0:META, t % 2, :], aux[t % 2][0:META, 0:T2], decay0[0:META, h, :], ALU.mult)\
                        .then_inc(*done("pt2c", (layer, t, 0)))
                    tt(pt1[:, t % 2, :], aux[2][:, 0:384], decay1[:, h, :], ALU.mult).then_inc(*done("pt2c", (layer, t, 1)))
                    return
                m = 3 * (t % 3)
                dve.wait_ge(*after("exp2", (layer, t, 2)))
                dve.reciprocal(small[:, 18 + m:21 + m], small[:, 9 + m:12 + m]).then_inc(*done("recip2", (layer, t)))
                dve.wait_ge(*after("recip2", (layer, t)))
                if name == "b" and comp:
                    ts(small[:, 18 + m:21 + m], small[:, 18 + m:21 + m], lam[:, 5:6], ALU.mult).then_inc(*done("recip2b", (layer, t)))
                    dve.wait_ge(*after("recip2b", (layer, t)))
                for n_, (lo, n) in enumerate(TILES):
                    pr = p2[:, t % 3, lo:lo + n]
                    w = small[:, 18 + m + n_:19 + m + n_]
                    if name == "b" and comp:
                        dve.wait_ge(*after("prob2", (layer, t - 1)))
                        i = stt(pr, pr, w, p2[:, (t - 1) % 3, lo:lo + n], ALU.mult, ALU.add)
                    else:
                        i = ts(pr, pr, w, ALU.mult)
                    i.then_inc(*(done("prob2", (layer, t)) if n_ == 2 else done("prob2a", (layer, t, n_))))

            def network2(layer):
                if layer == 0:
                    inverse(rinv[:, 0:SEQ], "norm_root", "norm_rinv", ("fin", 1))
                    dve.wait_ge(*after("const2_in", 1))
                    for c in range(DC):
                        stt(H[:, c, META:T2], X[:, c, 0:SEQ], fin_g[:, 0, c:c + 1], rinv[:, 0:SEQ], ALU.mult, ALU.mult)\
                            .then_inc(*done("fin1", c))
                    dve.wait_ge(*after("meta_in", 0))
                def gain(name):
                    return lambda c, st: par2(layer, name, c)
                both = [(0, slice(0, T2))]
                norm((layer, 3), H, T2, u_hi, u_lo, gain("nmix"), None, both)
                dve.wait_ge(*after("lam_in", layer))
                for j in range(2):
                    if j:
                        dve.wait_ge(*after("lam_sum", (layer, 0)))
                    dve.tensor_tensor_reduce(small[:, 64:96], lamp[:, 64 * j:64 * j + 32], lamp[:, 64 * j + 32:64 * j + 64],
                                             1.0, 0.0, ALU.mult, ALU.add, lam[:, j:j + 1])\
                        .then_inc(*done("lam_sum", (layer, j)))
                lam_i = lambda_init(layer)
                dve.wait_ge(*after("lam_exp", layer))
                tt(lam[:, 4:5], lam[:, 3:4], lam[:, 2:3], ALU.subtract).then_inc(*done("lam_part", (layer, 2)))
                dve.wait_ge(*after("lam_part", (layer, 2)))
                ts(lam[:, 5:6], lam[:, 4:5], lam_i, ALU.subtract).then_inc(*done("lam_part", (layer, 3)))
                a = PRM2["dnorm"][0]
                ts(prm2[:, layer, a:a + 1], prm2[:, layer, a:a + 1], 1.0 - lam_i, ALU.mult).then_inc(*done("lam_part", (layer, 4)))
                a = PRM2["rnorm"][0]
                ts(prm2[:, layer, a:a + 2], prm2[:, layer, a:a + 2], 0.5, ALU.mult).then_inc(*done("lam_part", (layer, 5)))
                dve.wait_ge(*after("wi_hi", layer))
                tt(wi_w[:, 1, :, :], wi_r[:, :, :], wi_w[:, 0, :, :].bitcast(F32), ALU.subtract).then_inc(*done("wi_lo", layer))

                for step in L2_PLAN:
                    kind, k = step[0:2]
                    if kind == "wi":
                        dve.wait_ge(*after("wi_made", layer))
                        ts(wis, aux[2][:, 0:16], IDX_HEADS ** -0.5 * 64 ** -0.5, ALU.mult).then_inc(*done("wi_out", layer))
                        if layer == 0:
                            dve.wait_ge(*after("tab2_in", 1))
                        dve.wait_ge(*after("wi_out", layer))
                    elif kind == "index":
                        h = k
                        dve.wait_ge(*after("index_relu", (layer, h)))
                        for t, (lo, n) in enumerate(((S1, N1), (S2, N2))):
                            w = wis[:, 8 * t + h:8 * t + h + 1]
                            src = relu2[:, h % 2, lo:lo + n]
                            if h == 0:
                                i = ts(score[:, lo:lo + n], src, w, ALU.mult)
                            else:
                                if t == 0:
                                    dve.wait_ge(*after("index_sum", (layer, h - 1)))
                                i = stt(score[:, lo:lo + n], src, w, score[:, lo:lo + n], ALU.mult, ALU.add)
                            i.then_inc(*(done("index_sum", (layer, h)) if t else done("index_part", (layer, h))))
                        if h == IDX_HEADS - 1:
                            dve.wait_ge(*after("index_sum", (layer, h)))
                            tt(score[:, :], score[:, :], causal, ALU.add).then_inc(*done("top", (layer, 0)))
                            dve.wait_ge(*after("top", (layer, 0)))
                    elif kind == "top":
                        r = k
                        for t, (lo, n) in enumerate(((S1, N1), (S2, N2))):
                            dve.max(small[:, 48 + 8 * t:56 + 8 * t], score[:, lo:lo + n]).then_inc(*done("top", (layer, 1, r, t)))
                        for t, (lo, n) in enumerate(((S1, N1), (S2, N2))):
                            dve.wait_ge(*after("top", (layer, 1, r, t)))
                            dve.match_replace(score[:, lo:lo + n], small[:, 48 + 8 * t:56 + 8 * t], score[:, lo:lo + n], TAKEN)\
                                .then_inc(*done("top", (layer, 2, r, t)))
                        dve.wait_ge(*after("top", (layer, 2, r, 1)))
                        if r == TOPK // 8 - 1:
                            ts(nsel[:, :], score[:, :], TAKEN / 2, ALU.is_gt, NEG, ALU.mult).then_inc(*done("selected", layer))
                            dve.wait_ge(*after("selected", layer))
                    elif kind == "slab":
                        if QCR < k < QB:
                            rope2(layer, k - 1)
                        if k >= GC:
                            dve.wait_ge(*after("p2_out", (layer, k)))
                            stt(pj[:, k, :], nt[:, k % 2, 0:T2], 1.0, lin[l2_bank(step)][:, 0:T2], ALU.add, ALU.mult)\
                                .then_inc(*done("gate2", (layer, k)))
                    elif kind == "vals" and step[1:] == (1, 0):
                        rope2(layer, QB - 1)
                    elif kind == "S":
                        biased_max(layer, k)
                    elif kind == "T":
                        probabilities(layer, k)
                    if (kind == "T" and k and UNITS[k - 1][0] == "a"):
                        k = k - 1
                        h = UNITS[k][1]
                        r = slice((h % 2) * HD, (h % 2) * HD + HD)
                        dve.wait_ge(*after("unit_out", (layer, k)))
                        tt(o_lo[r, h // 2, :], aux[3][r, 0:T2], o_hi[r, h // 2, :].bitcast(F32), ALU.subtract)\
                            .then_inc(*done("unit_lo", (layer, h)))

                def bc_rest(c):
                    dve.wait_ge(*after("bc_hi", (layer, c)))
                    tt(o_lo[:, 4 + c, :], nr[:, c % 2, 0:T2], o_hi[:, 4 + c, :].bitcast(F32), ALU.subtract)\
                        .then_inc(*done("bc_lo", (layer, c)))
                for c in range(4):
                    inverse(bc_r[:, c, :], "bc_root", "bc_rinv", (layer, c))
                    tt(nt[:, c % 2, 0:T2], bc_raw[:, c, :], bc_r[:, c, :], ALU.mult).then_inc(*done("bc_x", (layer, c)))
                    dve.wait_ge(*after("bc_x", (layer, c)))
                    if c < 2:
                        i = ts(nr[:, c % 2, 0:T2], nt[:, c % 2, 0:T2], par2(layer, "dnorm", 0), ALU.mult)
                    else:
                        i = stt(nr[:, c % 2, 0:T2], nt[:, c % 2, 0:T2], par2(layer, "rnorm", c - 2), pj[:, GC + c - 2, :],
                                ALU.mult, ALU.mult)
                    i.then_inc(*done("bc_normed", (layer, c)))
                    if c:
                        bc_rest(c - 1)
                bc_rest(3)
                for m in range(DC):
                    dve.wait_ge(*after("chunk", (layer, "mix2", m)))
                    tt(H[:, m, :], lin[m % 4][:, 0:T2], H[:, m, :], ALU.add).then_inc(*done("mix2_out", (layer, m)))
                    if m >= 2:
                        norm_add((layer, 4), m - 1, T2)
                norm_add((layer, 4), DC - 1, T2)
                norm((layer, 4), H, T2, u_hi, u_lo, gain("nff"), None, both)
                base = FF2_C * layer

                def ff1(j, b, it=None):
                    plus = 0 if it is None else it * 8
                    dve.wait_ge(sem("ff1_relu"), base + j + 1 + plus)
                    dst = ff2a[:, j, :] if it is None else ff2a[:, bass.ds(j + plus, 1), :].rearrange("p a t -> p (a t)")
                    t_ = up_t[:, b % 2, 0:T2]
                    tt(dst, t_, t_, ALU.mult).then_inc(*done("ff1_out", (layer, j)))
                def ff2(j, b, it=None):
                    plus = 0 if it is None else it * 8
                    dve.wait_ge(sem("ff2_hi"), base + j + 1 + plus)
                    src = ff2a[:, j, :] if it is None else ff2a[:, bass.ds(j + plus, 1), :].rearrange("p a t -> p (a t)")
                    tt(dn_lo[:, j % 2, 0:T2], src, dn_hi[:, j % 2, 0:T2].bitcast(F32), ALU.subtract)\
                        .then_inc(*done("ff2_lo", (layer, j)))
                for j in range(8):
                    ff1(j, j)
                for j in range(2):
                    ff2(j, j)
                with dve.Fori(0, 3) as it:
                    for b in range(8):
                        ff1(8 + b, b, it)
                again("ff1_out", 16)
                seen["ff1_all", layer] = counts["ff1_out"]

                for j in range(2, 7):
                    ff2(j, j)
                with dve.Fori(0, 3) as it:
                    for b in range(8):
                        ff2(7 + b, b, it)
                again("ff2_lo", 16)
                ff2(FF2_C - 1, 0)
                tag = (layer + 1, 3) if layer + 1 < DEPTH else ("fin", 2)
                for m in range(DC):
                    dve.wait_ge(*(after("ff2_sum", (layer, m)) if m < DC - 1 else after("chunk", (layer, "ff2"))))
                    tt(H[:, m, :], bank[m][:, 0:T2], H[:, m, :], ALU.add).then_inc(*done("ff2_out", (layer, m)))
                    if m >= 2:
                        norm_add(tag, m - 1, T2)
                norm_add(tag, DC - 1, T2)

            dve.wait_ge(*after("vec_made", 0))
            for b, (lo, hi) in enumerate(((0, 512), (512, VLEN))):
                i = tt(vec[0:12, lo:hi], lin[b][0:12, 0:hi - lo], oneh[0:12, 1, lo:hi], ALU.add)
                i.then_inc(*(done("vec_ready", 0) if b else done("vec_part", 0)))
            dve.wait_ge(*after("prm_in", 0))
            for layer in range(DEPTH):
                half_parameters(layer)
            for layer in range(DEPTH):
                network1(layer)
            for layer in range(DEPTH):
                network2(layer)
            tag = ("fin", 2)
            inverse(rinv[:, 0:T2], "norm_root", "norm_rinv", tag)
            for c in range(DC):
                if c >= 4:
                    dve.wait_ge(*after(f"stored{c % 4}", c - 4))
                stt(nb[:, c % 4, 0:SEQ], H[:, c, META:T2], fin_g[:, 1, c:c + 1], rinv[:, META:T2], ALU.mult, ALU.mult)\
                    .then_inc(*done("out_ready", c))
    return seen


def shape_tables():
    t = np.zeros((P, TAB_N), np.float32)

    def put(name, v):
        a, b = TAB[name]
        t[:v.shape[0], a:b] = v
    i = np.arange(P)
    put("ident", np.eye(P))
    put("ones_d", np.full((P, P), 1 / D))
    put("ones_c", np.full((P, P), 1 / (CONV_C * P)))
    put("ones_h", (i[:, None] // HD == i[None, :] // HD) / HD)
    for name, half in (("perm1", 16), ("perm2", 32)):
        m = np.zeros((P, P))
        for j in range(P):
            low = j % (2 * half) < half
            m[j + half if low else j - half, j] = -1 if low else 1
        put(name, m)
    sel = np.zeros((P, 2))
    for g in range(4):
        for s in range(2):
            sel[32 * g + s, s] = 1
    put("sel", sel)
    f = np.float32
    pos = np.arange(SEQ)
    inv = (f(10000.0) ** (-np.arange(0, 32, 2, dtype=f) / f(32))).astype(f)
    ang = np.zeros((P, SEQ), f)
    for j in range(P):
        d = j % HD
        where = pos // GRID_W if d < 32 else pos % GRID_W
        ang[j] = where.astype(f) * inv[d % 16]
    put("cos1", np.cos(ang))
    put("sin1", np.sin(ang))
    q, k = np.arange(GRID_W)[:, None], np.arange(GRID_W)[None, :]
    start = np.clip(q - 8, 0, GRID_W - 16)
    w = np.where((k >= start) & (k < start + 16), 0.0, NEG)
    put("win", np.concatenate([w, w]))
    inv = (f(10000.0) ** (-np.arange(0, 64, 2, dtype=f) / f(64))).astype(f)
    ang = inv[(i % HD) % 32][:, None] * np.arange(T2, dtype=f)[None, :]
    put("cos2", np.cos(ang))
    put("sin2", np.sin(ang))
    c = np.zeros((P, N1 + N2))
    c[:, :N1] = np.where(np.arange(N1)[None] <= META + i[:, None], 0, NEG)
    c[:, N1:] = np.where(np.arange(N2)[None] <= META + P + i[:, None], 0, NEG)
    put("causal", c)
    lg = np.log1p(-np.exp2(-5.0 - np.arange(C_HEADS)))

    def decay(keys, queries):
        d = queries[None, None, :] - keys[:, None, None]
        return np.where(d >= 0, np.exp(lg[None, :, None] * np.maximum(d, 0)), 0.0)
    d1 = np.concatenate([decay(META + i, np.arange(META, T2)), decay(META + P + i, np.arange(META + P, T2))], axis=2)
    put("decay1", d1.reshape(P, -1))
    put("decay0", decay(np.arange(META), np.arange(T2)).reshape(META, -1))
    dist = T2 - 1 - np.arange(VLEN)
    n = np.maximum(dist, 0)
    large = 16 + (np.log(np.maximum(n, 1).astype(f) / f(16)) / f(math.log(8)) * f(16)).astype(np.int32)
    bucket = np.where(n < 16, n, np.minimum(large, 31))
    put("onehot", (bucket[None, :] == np.arange(32)[:, None]) & (dist >= 0)[None, :])
    put("vmask", np.broadcast_to(np.where(dist >= 0, 0.0, NEG), (12, VLEN)))
    return t


def by_feature(v):
    v = v.reshape(*v.shape[:-1], -1, P)
    return np.moveaxis(v, -1, 0)


def weight_stream(w):
    slabs = []

    def tiles(m, c0):
        return m[:, c0:c0 + P].reshape(-1, P, P).transpose(1, 0, 2).reshape(P, -1)

    def wide(m):
        for q in range(m.shape[0] // (2 * P)):
            slabs.append(m[2 * P * q:2 * P * (q + 1)].reshape(2, P, 512).transpose(1, 0, 2).reshape(P, -1))
    for l in range(DEPTH):
        m = w["w_in"][l]
        for c in range(CONV_C):
            slabs += [tiles(m, 512 + c * P), tiles(m, c * P)]
        for c in range(2 * QC):
            slabs.append(tiles(m, 1024 + c * P))
        wide(m[:, 2048:2560])
        for c in range(DC):
            slabs += [tiles(m, 2560 + c * P), tiles(m, 2560 + D + c * P)]
        for c in range(DC):
            slabs.append(np.concatenate([tiles(w["w_conv_out"][l], c * P), tiles(w["w_na_out"][l], c * P)], axis=1))
        for c in range(DC):
            slabs.append(tiles(w["w_out"][l], c * P))
        for j in range(FF_C):
            slabs += [tiles(w["w_up"][l], j * P), tiles(w["w_up"][l], (FF_C + j) * P)]
        slabs += list(w["w_down"][l].reshape(FF_C, P, D))
    for l in range(DEPTH):
        m = w["w_in_2"][l]
        at = {"qa": 0, "ka": 512, "va": 1024, "qi": 1536, "ki": 2048, "qb": 2120, "kb": 2376, "vb": 2632,
              "qc": 2888, "kc": 3144, "vc": 3400, "gc": 3656}

        def feature(names):
            for name, n in names:
                for c in range(n):
                    slabs.append(tiles(m, at[name] + c * P))
        slabs.append(tiles(np.concatenate([m[:, 2048:2112]] * 2, axis=1), 0))
        feature([("qi", 4), ("qa", 4), ("ka", 4)])
        wide(m[:, at["va"]:at["va"] + 512])
        feature([("qc", 2), ("kc", 2)])
        wide(np.concatenate([m[:, at["vb"]:at["vb"] + 256], m[:, at["vc"]:at["vc"] + 256]], axis=1))
        feature([("qb", 2), ("kb", 2), ("gc", 2)])
        for c in range(DC):
            slabs.append(tiles(w["w_out_2"][l], c * P))
        for c in range(FF2_C):
            slabs.append(tiles(w["w_ff1_2"][l], c * P))
        slabs += list(w["w_ff2_2"][l].reshape(FF2_C, P, D))
    return np.stack(slabs)


def ada_stream(w_ada):
    w = w_ada.reshape(DEPTH, DC // 2, 2, P, 12, 512).transpose(0, 4, 1, 3, 2, 5)
    return w.reshape(DEPTH * 12 * (DC // 2), P, SLAB)


def kernel(**inputs):
    import concourse.bacc as bacc
    from concourse.bass_utils import run_bass_kernel_spmd as run

    w = {k: np.asarray(v) for k, v in inputs.items()}
    prm1, prm2 = [], []
    for l in range(DEPTH):
        dw = by_feature(w["conv_dw"][l]).transpose(0, 2, 1).reshape(P, -1)
        prm1.append(np.concatenate([
            by_feature(w["norm1_g"][l]), dw, by_feature(w["conv_dw_b"][l]), by_feature(w["conv_ln_g"][l]),
            by_feature(w["conv_ln_b"][l]), by_feature(w["norm2_g"][l]), by_feature(w["ffn_dw"][l]).reshape(P, -1),
            by_feature(w["ffn_dw_b"][l]), by_feature(w["b_ada"][l])], axis=1))
        dn = w["diff_norm_2"][l]
        prm2.append(np.concatenate([
            by_feature(w["norm_mix_2"][l]), np.concatenate([dn, dn])[:, None], by_feature(w["ret_norm_2"][l]),
            by_feature(w["norm_ff_2"][l])], axis=1))
    rpb = np.zeros((DEPTH, HEADS, 15, RPB_PAD), w["na_rpb"].dtype)
    rpb[..., 48:79] = w["na_rpb"]
    arrays = {
        "wstream": weight_stream(w),
        "wada": ada_stream(w["w_ada"]),
        "tables": shape_tables(),
        "x_in": np.concatenate([by_feature(w["x"][0]).transpose(0, 2, 1), by_feature(w["ctx"][0]).transpose(0, 2, 1)], axis=2),
        "cvec": np.stack([by_feature(w["c"][0]), by_feature(w["c_ctx"])], axis=2),
        "prm1": np.stack(prm1, axis=1),
        "prm2": np.stack(prm2, axis=1),
        "fin_g": np.stack([by_feature(w["final_norm_g"]), by_feature(w["final_norm_2"])], axis=1),
        "rpb": rpb,
        "meta": by_feature(w["meta_2"]).transpose(0, 2, 1),
        "rel_bias": w["rel_bias_2"],
        "lam": w["diff_lambda_2"].reshape(DEPTH, P),
        "wi": w["w_in_2"][:, :, 2112:2120].reshape(DEPTH, DC, P, 8).transpose(0, 2, 1, 3),
    }
    arrays = {k: np.ascontiguousarray(v) for k, v in arrays.items()}

    def emit(marks):
        nc = bacc.Bacc("TRN2", target_bir_lowering=False, num_devices=1)
        args = {k: nc.dram_tensor(f"in_{k}", v.shape, mybir.dt.from_np(v.dtype), kind="ExternalInput").ap()
                for k, v in arrays.items()}
        out = nc.dram_tensor("out_x", (D, SEQ), F32, kind="ExternalOutput").ap()
        return nc, build(nc, args, out, marks)

    _, marks = emit({})
    nc, again = emit(marks)
    assert marks == again
    r = run(nc, [{f"in_{k}": v for k, v in arrays.items()}], core_ids=[0])
    return np.ascontiguousarray(r.results[0]["out_x"].T)[None]
```
